# Optimizing a Trainium2 kernel written in Bass

```python
import jax, jax.numpy as jnp
from jax import lax
import numpy as np

D_MODEL = 1024
BATCH = 1
SEQ = 256
DEPTH = 2

GRID_W = 64
CTX_LEN = 256

ATTN_HEAD_DIM = 64
ATTN_HEADS = 8
ATTN_KV_HEADS = 2
ATTN_Q_PER_KV = ATTN_HEADS // ATTN_KV_HEADS
ATTN_WIDTH = ATTN_HEADS * ATTN_HEAD_DIM
ATTN_KV_WIDTH = ATTN_KV_HEADS * ATTN_HEAD_DIM
Q_BLOCK = 128
ROPE_THETA = 10000.0
ROPE_AXIS_DIM = ATTN_HEAD_DIM // 2

GLA_HEADS = 4
GLA_DK = 64
GLA_DV = 128
GLA_K_WIDTH = GLA_HEADS * GLA_DK
GLA_V_WIDTH = GLA_HEADS * GLA_DV
GLA_GATE_RANK = 16
GLA_GATE_TEMP = 16.0
GLA_CHUNK = 64

SGU_GROUPS = 4
SGU_CHUNK = 128
SGU_WIDTH = 512
SGU_GROUP_DIM = SGU_WIDTH // SGU_GROUPS

DEEPNORM_ALPHA = (2 * DEPTH) ** 0.25
DEEPNORM_BETA = (8 * DEPTH) ** -0.25
EPS = 1e-6

SPLIT_SIZES = (
    ATTN_WIDTH, ATTN_KV_WIDTH, ATTN_KV_WIDTH, ATTN_WIDTH,
    GLA_K_WIDTH, GLA_K_WIDTH, GLA_V_WIDTH, GLA_GATE_RANK, GLA_GATE_RANK,
    GLA_V_WIDTH,
    SGU_WIDTH, SGU_WIDTH, SGU_WIDTH,
    D_MODEL, D_MODEL, D_MODEL,
)
PROJ_WIDTH = sum(SPLIT_SIZES)


def _split_points():
    pts, acc = [], 0
    for s in SPLIT_SIZES[:-1]:
        acc += s
        pts.append(acc)
    return pts

def layer_norm(x, g, b):
    xf = x.astype(jnp.float32)
    mu = jnp.mean(xf, axis=-1, keepdims=True)
    var = jnp.mean(jnp.square(xf - mu), axis=-1, keepdims=True)
    return ((xf - mu) * lax.rsqrt(var + EPS) * g + b).astype(x.dtype)

def rms_norm(x, g):
    xf = x.astype(jnp.float32)
    y = xf * lax.rsqrt(jnp.mean(jnp.square(xf), axis=-1, keepdims=True) + EPS)
    return (y * g).astype(x.dtype)

def axial_rope_angles(rows):
    row = jnp.repeat(jnp.arange(rows, dtype=jnp.float32), GRID_W)
    col = jnp.tile(jnp.arange(GRID_W, dtype=jnp.float32), rows)
    freqs = ROPE_THETA ** (-jnp.arange(0, ROPE_AXIS_DIM, 2, dtype=jnp.float32) / ROPE_AXIS_DIM)
    return row[:, None] * freqs, col[:, None] * freqs

def rope_1d(x, ang):
    m = ang.shape[-1]
    cos = jnp.cos(ang)[None, :, None, :]
    sin = jnp.sin(ang)[None, :, None, :]
    x1, x2 = x[..., :m], x[..., m:]
    return jnp.concatenate([x1 * cos - x2 * sin, x1 * sin + x2 * cos], axis=-1)

def apply_axial_rope(x, ang_r, ang_c):
    xf = x.astype(jnp.float32)
    out = jnp.concatenate([rope_1d(xf[..., :ROPE_AXIS_DIM], ang_r),
                           rope_1d(xf[..., ROPE_AXIS_DIM:], ang_c)], axis=-1)
    return out.astype(x.dtype)

def gqa_project(pq, pk, pv, q_norm, k_norm):
    B, N, _ = pq.shape
    q = rms_norm(pq.reshape(B, N, ATTN_HEADS, ATTN_HEAD_DIM), q_norm)
    k = rms_norm(pk.reshape(B, N, ATTN_KV_HEADS, ATTN_HEAD_DIM), k_norm)
    v = pv.reshape(B, N, ATTN_KV_HEADS, ATTN_HEAD_DIM)
    return q, k, v

def attend(q, k, v):
    s = jnp.einsum('btgrd,blgd->bgrtl', q, k, preferred_element_type=jnp.float32) * (ATTN_HEAD_DIM ** -0.5)
    p = jax.nn.softmax(s, axis=-1)
    return jnp.einsum('bgrtl,blgd->btgrd', p.astype(v.dtype), v)

def blocked_attention(q, k, v):
    B, N = q.shape[:2]
    nb = N // Q_BLOCK
    qb = q.reshape(B, nb, Q_BLOCK, ATTN_KV_HEADS, ATTN_Q_PER_KV, ATTN_HEAD_DIM)
    qb = jnp.moveaxis(qb, 1, 0)
    ob = lax.map(lambda qi: attend(qi, k, v), qb)
    return jnp.moveaxis(ob, 0, 1).reshape(B, N, ATTN_WIDTH)

def gla_scan(q, k, v, g, s0):
    B, H, N, dk = q.shape
    dv = v.shape[-1]
    nc = N // GLA_CHUNK
    mask = jnp.tril(jnp.ones((GLA_CHUNK, GLA_CHUNK), dtype=bool))

    def chunks(t):
        return jnp.moveaxis(t.reshape(B, H, nc, GLA_CHUNK, t.shape[-1]), 2, 0)

    def step(s, inp):
        qc, kc, vc, gc = inp
        b = jnp.cumsum(gc, axis=2)
        b_last = b[:, :, -1:, :]
        inter = jnp.einsum('bhtd,bhde->bhte', qc * jnp.exp(b), s)
        rel = jnp.where(mask[:, :, None], b[:, :, :, None, :] - b[:, :, None, :, :], -jnp.inf)
        att = jnp.einsum('bhtd,bhsd,bhtsd->bhts', qc, kc, jnp.exp(rel))
        o = inter + jnp.einsum('bhts,bhse->bhte', att, vc)
        s_new = jnp.exp(b_last[:, :, 0, :])[..., None] * s + \
            jnp.einsum('bhsd,bhse->bhde', kc * jnp.exp(b_last - b), vc)
        return s_new, o

    s_fin, o = lax.scan(step, s0, (chunks(q), chunks(k), chunks(v), chunks(g)))
    return jnp.moveaxis(o, 0, 2).reshape(B, H, N, dv), s_fin

def gla_heads(pq, pk, pv, paf, pab, a2_f, ab_f, a2_b, ab_b):
    B, N, _ = pq.shape

    def heads(t, d):
        return t.reshape(B, N, GLA_HEADS, d).transpose(0, 2, 1, 3).astype(jnp.float32)

    def log_decay(pa, a2, ab):
        z = (pa @ a2 + ab).astype(jnp.float32)
        return heads(jax.nn.log_sigmoid(z) / GLA_GATE_TEMP, GLA_DK)

    q = heads(pq, GLA_DK) * (GLA_DK ** -0.5)
    k = heads(pk, GLA_DK)
    v = heads(pv, GLA_DV)
    return q, k, v, log_decay(paf, a2_f, ab_f), log_decay(pab, a2_b, ab_b)

def gla_finish(o, o_norm, dtype):
    B, H, N, dv = o.shape
    o = rms_norm(o.transpose(0, 2, 1, 3), o_norm)
    return o.reshape(B, N, H * dv).astype(dtype)

def sgu(pu, pv, ln_g, ln_b, w_s, b_s):
    B, N, _ = pu.shape
    nch = N // SGU_CHUNK
    vn = layer_norm(pv, ln_g, ln_b).reshape(B, nch, SGU_CHUNK, SGU_GROUPS, SGU_GROUP_DIM)
    mixed = jnp.einsum('gts,bnsgc->bntgc', w_s, vn) + b_s.T[None, None, :, :, None]
    return pu * mixed.reshape(B, N, SGU_WIDTH)

def trunk_layer(x, ctx, c, c_ctx, p, ang_r, ang_c, need_ctx):
    B = x.shape[0]
    shift, scale, gate = jnp.split(jax.nn.silu(c) @ p['w_ada'] + p['b_ada'], 3, axis=-1)
    shift_c, scale_c, gate_c = jnp.split(jax.nn.silu(c_ctx) @ p['w_ada'] + p['b_ada'], 3, axis=-1)
    h = x * (1.0 + scale[:, None, :]) + shift[:, None, :]
    hc = ctx * (1.0 + scale_c) + shift_c

    pts = _split_points()
    (a_q, a_k, a_v, a_g, g_q, g_k, g_v, g_af, g_ab, g_g,
     s_u, s_v, s_g, m_a, m_g, m_s) = jnp.split(h @ p['w_in'], pts, axis=-1)
    (ca_q, ca_k, ca_v, ca_g, cg_q, cg_k, cg_v, cg_af, cg_ab, cg_g,
     cs_u, cs_v, cs_g, cm_a, cm_g, cm_s) = jnp.split(hc @ p['w_in'], pts, axis=-1)

    ql, kl, vl = gqa_project(a_q, a_k, a_v, p['q_norm'], p['k_norm'])
    ql = apply_axial_rope(ql, ang_r, ang_c)
    kl = apply_axial_rope(kl, ang_r, ang_c)
    qc, kc, vc = gqa_project(ca_q, ca_k, ca_v, p['q_norm'], p['k_norm'])
    k_all = jnp.concatenate([kc, kl], axis=1)
    v_all = jnp.concatenate([vc, vl], axis=1)
    y_attn = blocked_attention(ql, k_all, v_all) * jax.nn.silu(a_g)

    qlg, klg, vlg, gfl, gbl = gla_heads(g_q, g_k, g_v, g_af, g_ab, p['a2_f'], p['ab_f'], p['a2_b'], p['ab_b'])
    qcg, kcg, vcg, gfc, gbc = gla_heads(cg_q, cg_k, cg_v, cg_af, cg_ab, p['a2_f'], p['ab_f'], p['a2_b'], p['ab_b'])
    zeros = jnp.zeros((B, GLA_HEADS, GLA_DK, GLA_DV), jnp.float32)
    flip = lambda t: jnp.flip(t, axis=2)
    oc_f, s_f = gla_scan(qcg, kcg, vcg, gfc, zeros)
    oc_b, s_b = gla_scan(flip(qcg), flip(kcg), flip(vcg), flip(gbc), zeros)
    ol_f, _ = gla_scan(qlg, klg, vlg, gfl, s_f)
    ol_b, _ = gla_scan(flip(qlg), flip(klg), flip(vlg), flip(gbl), s_b)
    y_gla = gla_finish(ol_f + flip(ol_b), p['gla_o_norm'], x.dtype) * jax.nn.silu(g_g)

    y_sgu = sgu(s_u, s_v, p['sgu_ln_g'], p['sgu_ln_b'], p['sgu_w'], p['sgu_b']) * jax.nn.silu(s_g)

    def merge(ya, yg, ys, ga, gg, gs):
        m = (jax.nn.sigmoid(ga) * (ya @ p['w_br_attn'])
             + jax.nn.sigmoid(gg) * (yg @ p['w_br_gla'])
             + jax.nn.sigmoid(gs) * (ys @ p['w_br_sgu']))
        return m @ p['w_out']

    out = merge(y_attn, y_gla, y_sgu, m_a, m_g, m_s)
    x_new = layer_norm(DEEPNORM_ALPHA * x + gate[:, None, :] * out, p['post_g'], p['post_b'])

    if not need_ctx:
        return x_new, ctx

    L = ctx.shape[1]
    yc_attn = attend(qc.reshape(B, L, ATTN_KV_HEADS, ATTN_Q_PER_KV, ATTN_HEAD_DIM), kc, vc)
    yc_attn = yc_attn.reshape(B, L, ATTN_WIDTH) * jax.nn.silu(ca_g)
    yc_gla = gla_finish(oc_f + flip(oc_b), p['gla_o_norm'], ctx.dtype) * jax.nn.silu(cg_g)
    yc_sgu = sgu(cs_u, cs_v, p['sgu_ln_g'], p['sgu_ln_b'], p['sgu_w'], p['sgu_b']) * jax.nn.silu(cs_g)
    out_c = merge(yc_attn, yc_gla, yc_sgu, cm_a, cm_g, cm_s)
    ctx_new = layer_norm(DEEPNORM_ALPHA * ctx + gate_c * out_c, p['post_g'], p['post_b'])
    return x_new, ctx_new

def first_inputs(seed: int = 0) -> dict:
    key = jax.random.key(seed)
    ks = iter(jax.random.split(key, 32))

    def nrm(shape, s):
        return jax.random.normal(next(ks), shape, jnp.float32) * s

    L, D = DEPTH, D_MODEL
    return {
        "x": nrm((BATCH, SEQ, D), 1.0),
        "c": nrm((BATCH, D), 1.0),
        "ctx": nrm((BATCH, CTX_LEN, D), 1.0),
        "c_ctx": nrm((D,), 1.0),
        "w_ada": nrm((L, D, 3 * D), 0.5 * D ** -0.5),
        "b_ada": nrm((L, 3 * D), 0.02),
        "w_in": nrm((L, D, PROJ_WIDTH), D ** -0.5),
        "attn_q_norm": 1.0 + nrm((L, ATTN_HEAD_DIM), 0.02),
        "attn_k_norm": 1.0 + nrm((L, ATTN_HEAD_DIM), 0.02),
        "gla_a2_f": nrm((L, GLA_GATE_RANK, GLA_K_WIDTH), GLA_GATE_RANK ** -0.5),
        "gla_ab_f": nrm((L, GLA_K_WIDTH), 0.1),
        "gla_a2_b": nrm((L, GLA_GATE_RANK, GLA_K_WIDTH), GLA_GATE_RANK ** -0.5),
        "gla_ab_b": nrm((L, GLA_K_WIDTH), 0.1),
        "gla_o_norm": 1.0 + nrm((L, GLA_DV), 0.02),
        "sgu_ln_g": 1.0 + nrm((L, SGU_WIDTH), 0.02),
        "sgu_ln_b": nrm((L, SGU_WIDTH), 0.02),
        "sgu_w": nrm((L, SGU_GROUPS, SGU_CHUNK, SGU_CHUNK), SGU_CHUNK ** -0.5),
        "sgu_b": 1.0 + nrm((L, SGU_GROUPS, SGU_CHUNK), 0.02),
        "w_br_attn": nrm((L, ATTN_WIDTH, D), ATTN_WIDTH ** -0.5 * DEEPNORM_BETA),
        "w_br_gla": nrm((L, GLA_V_WIDTH, D), GLA_V_WIDTH ** -0.5 * DEEPNORM_BETA),
        "w_br_sgu": nrm((L, SGU_WIDTH, D), SGU_WIDTH ** -0.5 * DEEPNORM_BETA),
        "w_out": nrm((L, D, D), D ** -0.5 * DEEPNORM_BETA),
        "post_ln_g": 1.0 + nrm((L, D), 0.02),
        "post_ln_b": nrm((L, D), 0.02),
    }

def first_block(x, c, ctx, c_ctx, w_ada, b_ada, w_in, attn_q_norm, attn_k_norm,
              gla_a2_f, gla_ab_f, gla_a2_b, gla_ab_b, gla_o_norm,
              sgu_ln_g, sgu_ln_b, sgu_w, sgu_b,
              w_br_attn, w_br_gla, w_br_sgu, w_out, post_ln_g, post_ln_b):
    n_lat = x.shape[1]
    rows = n_lat // GRID_W
    ang_r, ang_c = axial_rope_angles(rows)
    for i in range(DEPTH):
        p = {
            'w_ada': w_ada[i], 'b_ada': b_ada[i], 'w_in': w_in[i],
            'q_norm': attn_q_norm[i], 'k_norm': attn_k_norm[i],
            'a2_f': gla_a2_f[i], 'ab_f': gla_ab_f[i], 'a2_b': gla_a2_b[i], 'ab_b': gla_ab_b[i],
            'gla_o_norm': gla_o_norm[i],
            'sgu_ln_g': sgu_ln_g[i], 'sgu_ln_b': sgu_ln_b[i], 'sgu_w': sgu_w[i], 'sgu_b': sgu_b[i],
            'w_br_attn': w_br_attn[i], 'w_br_gla': w_br_gla[i], 'w_br_sgu': w_br_sgu[i],
            'w_out': w_out[i], 'post_g': post_ln_g[i], 'post_b': post_ln_b[i],
        }
        x, ctx = trunk_layer(x, ctx, c, c_ctx, p, ang_r, ang_c, need_ctx=(i < DEPTH - 1))
    return x


DEPTH_2 = 1

CHUNK = 64
ATT_HEADS = 8
HEAD_DIM = 64
ATT_WIDTH = ATT_HEADS * HEAD_DIM
LRU_WIDTH = D_MODEL - ATT_WIDTH
LRU_BLOCKS = 8
LRU_BLOCK_DIM = LRU_WIDTH // LRU_BLOCKS
CONV_WIDTH = 4
LRU_C = 8.0
N_GROUPS = 4
EXPERTS_PER_GROUP = 8
TOP_K_INNER = 2
D_EXPERT = 256
RMS_EPS = 1e-6
IN_SIZES = (ATT_WIDTH, ATT_WIDTH, ATT_WIDTH, ATT_HEADS, LRU_WIDTH, LRU_WIDTH)
IN_COLS = sum(IN_SIZES)


def rmsnorm(x, g):
    xf = x.astype(jnp.float32)
    inv = lax.rsqrt(jnp.mean(xf * xf, axis=-1, keepdims=True) + RMS_EPS)
    return (xf * inv * g.astype(jnp.float32)).astype(x.dtype)

def forgetting_attention(q, k, v, log_f):
    b, s, h, dh = q.shape
    c = jnp.cumsum(log_f, axis=1).transpose(0, 2, 1)
    n_blk = s // Q_BLOCK
    q_blk = q.reshape(b, n_blk, Q_BLOCK, h, dh).transpose(1, 0, 2, 3, 4)
    c_blk = c.reshape(b, h, n_blk, Q_BLOCK).transpose(2, 0, 1, 3)
    starts = jnp.arange(n_blk, dtype=jnp.int32) * Q_BLOCK
    k_pos = jnp.arange(s, dtype=jnp.int32)
    scale = HEAD_DIM ** -0.5

    def one_block(args):
        qb, cb, start = args
        logits = jnp.einsum('bqhd,bkhd->bhqk', qb, k, preferred_element_type=jnp.float32) * scale
        decay = cb[..., :, None] - c[..., None, :]
        q_pos = start + jnp.arange(Q_BLOCK, dtype=jnp.int32)
        causal = k_pos[None, :] <= q_pos[:, None]
        logits = jnp.where(causal, logits + decay, -1e30)
        p = jax.nn.softmax(logits, axis=-1)
        return jnp.einsum('bhqk,bkhd->bqhd', p.astype(v.dtype), v)

    out = lax.map(one_block, (q_blk, c_blk, starts))
    return out.transpose(1, 0, 2, 3, 4).reshape(b, s, h * dh)

def causal_depthwise_conv(x, w, bias):
    s = x.shape[1]
    xp = jnp.pad(x, ((0, 0), (CONV_WIDTH - 1, 0), (0, 0)))
    out = bias + w[0] * xp[:, 0:s]
    for tap in range(1, CONV_WIDTH):
        out = out + w[tap] * xp[:, tap:tap + s]
    return out

def block_diag_linear(x, w, b):
    xb = x.reshape(x.shape[:-1] + (LRU_BLOCKS, LRU_BLOCK_DIM))
    y = jnp.einsum('bsni,nij->bsnj', xb, w) + b
    return y.reshape(x.shape)

def rg_lru(x, w_a, b_a, w_x, b_x, lam):
    r = jax.nn.sigmoid(block_diag_linear(x, w_a, b_a)).astype(jnp.float32)
    i = jax.nn.sigmoid(block_diag_linear(x, w_x, b_x))
    log_a = -LRU_C * r * jax.nn.softplus(-lam.astype(jnp.float32))
    a = jnp.exp(log_a)
    mult = jnp.sqrt(-jnp.expm1(2.0 * log_a))
    u = mult * (i * x).astype(jnp.float32)

    def combine(left, right):
        a_l, u_l = left
        a_r, u_r = right
        return a_r * a_l, a_r * u_l + u_r

    _, hseq = lax.associative_scan(combine, (a, u), axis=1)
    return hseq.astype(x.dtype)

def hierarchical_moe(t, w_group, b_group, w_inner, b_inner, w_gate, w_up, w_down):
    group_p = jax.nn.softmax((t @ w_group + b_group).astype(jnp.float32), axis=-1)
    g_w, g_idx = lax.top_k(group_p, 1)
    inner_all = jnp.einsum('nd,gde->nge', t, w_inner) + b_inner
    inner_logits = jnp.take_along_axis(inner_all, g_idx[:, :, None], axis=1)[:, 0]
    inner_p = jax.nn.softmax(inner_logits.astype(jnp.float32), axis=-1)
    e_w, e_idx = lax.top_k(inner_p, TOP_K_INNER)
    e_w = e_w / jnp.sum(e_w, axis=-1, keepdims=True)
    expert_w = jnp.sum(jax.nn.one_hot(e_idx, EXPERTS_PER_GROUP, dtype=jnp.float32) * e_w[..., None], axis=1)
    combine = (g_w[:, :, None]
               * jax.nn.one_hot(g_idx[:, 0], N_GROUPS, dtype=jnp.float32)[:, :, None]
               * expert_w[:, None, :]).astype(t.dtype)
    y = jnp.zeros_like(t)
    for g in range(N_GROUPS):
        hg = jax.nn.silu(jnp.einsum('nd,edf->nef', t, w_gate[g])) * jnp.einsum('nd,edf->nef', t, w_up[g])
        y = y + jnp.einsum('nef,efd->nd', hg * combine[:, g, :, None], w_down[g])
    return y

def second_inputs(seed: int = 0) -> dict:
    key = jax.random.key(seed)
    ks = jax.random.split(key, 24)
    nrm = jax.random.normal
    L, D, G, E, F = DEPTH_2, D_MODEL, N_GROUPS, EXPERTS_PER_GROUP, D_EXPERT
    a0 = jax.random.uniform(ks[10], (L, LRU_WIDTH), minval=0.9, maxval=0.999)
    sig = a0 ** (1.0 / LRU_C)
    lam = jnp.log(sig) - jnp.log1p(-sig)
    return {
        'x': nrm(ks[0], (BATCH, SEQ, D), jnp.float32),
        'mix_norm': 1.0 + 0.05 * nrm(ks[1], (L, D), jnp.float32),
        'w_in': nrm(ks[2], (L, D, IN_COLS), jnp.float32) * D ** -0.5,
        'b_forget': jnp.linspace(1.0, 6.0, ATT_HEADS, dtype=jnp.float32) + 0.1 * nrm(ks[3], (L, ATT_HEADS), jnp.float32),
        'conv_w': nrm(ks[4], (L, CONV_WIDTH, LRU_WIDTH), jnp.float32) * CONV_WIDTH ** -0.5,
        'conv_b': 0.02 * nrm(ks[5], (L, LRU_WIDTH), jnp.float32),
        'w_a': nrm(ks[6], (L, LRU_BLOCKS, LRU_BLOCK_DIM, LRU_BLOCK_DIM), jnp.float32) * LRU_BLOCK_DIM ** -0.5,
        'b_a': 0.02 * nrm(ks[7], (L, LRU_BLOCKS, LRU_BLOCK_DIM), jnp.float32),
        'w_x': nrm(ks[8], (L, LRU_BLOCKS, LRU_BLOCK_DIM, LRU_BLOCK_DIM), jnp.float32) * LRU_BLOCK_DIM ** -0.5,
        'b_x': 0.02 * nrm(ks[9], (L, LRU_BLOCKS, LRU_BLOCK_DIM), jnp.float32),
        'lru_lambda': lam,
        'w_out': nrm(ks[11], (L, D, D), jnp.float32) * D ** -0.5,
        'ffn_norm': 1.0 + 0.05 * nrm(ks[12], (L, D), jnp.float32),
        'w_group': nrm(ks[13], (L, D, G), jnp.float32) * D ** -0.5,
        'b_group': 0.01 * nrm(ks[14], (L, G), jnp.float32),
        'w_inner': nrm(ks[15], (L, G, D, E), jnp.float32) * D ** -0.5,
        'b_inner': 0.01 * nrm(ks[16], (L, G, E), jnp.float32),
        'w_gate': nrm(ks[17], (L, G, E, D, F), jnp.float32) * D ** -0.5,
        'w_up': nrm(ks[18], (L, G, E, D, F), jnp.float32) * D ** -0.5,
        'w_down': nrm(ks[19], (L, G, E, F, D), jnp.float32) * F ** -0.5,
        'final_norm': 1.0 + 0.05 * nrm(ks[20], (D,), jnp.float32),
    }

def second_block(x, mix_norm, w_in, b_forget, conv_w, conv_b, w_a, b_a, w_x, b_x, lru_lambda,
              w_out, ffn_norm, w_group, b_group, w_inner, b_inner, w_gate, w_up, w_down, final_norm):
    b, s, d = x.shape
    split_points = [int(v) for v in np.cumsum(IN_SIZES)[:-1]]
    for l in range(DEPTH_2):
        h = rmsnorm(x, mix_norm[l])
        z = h @ w_in[l]
        q, k, v, f_logit, gate_in, rec_in = jnp.split(z, split_points, axis=-1)
        log_f = jax.nn.log_sigmoid(f_logit.astype(jnp.float32) + b_forget[l].astype(jnp.float32))
        att = forgetting_attention(q.reshape(b, s, ATT_HEADS, HEAD_DIM),
                                   k.reshape(b, s, ATT_HEADS, HEAD_DIM),
                                   v.reshape(b, s, ATT_HEADS, HEAD_DIM), log_f)
        rec = causal_depthwise_conv(rec_in, conv_w[l], conv_b[l])
        rec = rg_lru(rec, w_a[l], b_a[l], w_x[l], b_x[l], lru_lambda[l])
        lru_out = rec * jax.nn.gelu(gate_in, approximate=True)
        x = x + jnp.concatenate([att, lru_out], axis=-1) @ w_out[l]
        h2 = rmsnorm(x, ffn_norm[l]).reshape(b * s, d)
        y = hierarchical_moe(h2, w_group[l], b_group[l], w_inner[l], b_inner[l],
                             w_gate[l], w_up[l], w_down[l])
        x = x + y.reshape(b, s, d)
    return rmsnorm(x, final_norm)


def setup_inputs(seed=0):
    out = dict(first_inputs(seed))
    for name, value in second_inputs(seed + 1).items():
        if name != "x":
            out[name + "_2"] = value
    return out


def reference(
    x, c, ctx, c_ctx, w_ada, b_ada, w_in, attn_q_norm, attn_k_norm, gla_a2_f, gla_ab_f,
    gla_a2_b, gla_ab_b, gla_o_norm, sgu_ln_g, sgu_ln_b, sgu_w, sgu_b, w_br_attn, w_br_gla,
    w_br_sgu, w_out, post_ln_g, post_ln_b, mix_norm_2, w_in_2, b_forget_2, conv_w_2, conv_b_2,
    w_a_2, b_a_2, w_x_2, b_x_2, lru_lambda_2, w_out_2, ffn_norm_2, w_group_2, b_group_2,
    w_inner_2, b_inner_2, w_gate_2, w_up_2, w_down_2, final_norm_2,
):
    x = first_block(
        x, c, ctx, c_ctx, w_ada, b_ada, w_in, attn_q_norm, attn_k_norm, gla_a2_f, gla_ab_f,
        gla_a2_b, gla_ab_b, gla_o_norm, sgu_ln_g, sgu_ln_b, sgu_w, sgu_b, w_br_attn, w_br_gla,
        w_br_sgu, w_out, post_ln_g, post_ln_b,
    )
    return second_block(
        x, mix_norm_2, w_in_2, b_forget_2, conv_w_2, conv_b_2, w_a_2, b_a_2, w_x_2, b_x_2,
        lru_lambda_2, w_out_2, ffn_norm_2, w_group_2, b_group_2, w_inner_2, b_inner_2, w_gate_2,
        w_up_2, w_down_2, final_norm_2,
    )


_drawn_inputs = setup_inputs


def setup_inputs(seed=0):
    import zlib

    import numpy as np

    out = dict(_drawn_inputs(seed))
    spreads = {}
    factors = {'ctx': 6.598,
     'c_ctx': 4.955,
     'b_ada': 4.038,
     'attn_q_norm': 8.0,
     'attn_k_norm': 8.0,
     'gla_a2_f': 8.0,
     'gla_ab_f': 8.0,
     'gla_a2_b': 8.0,
     'gla_ab_b': 8.0,
     'gla_o_norm': 30.626,
     'sgu_ln_g': 45.625,
     'sgu_ln_b': 42.727,
     'sgu_b': 42.539,
     'w_br_attn': 3.894,
     'b_a_2': 36.885,
     'b_x_2': 8.0,
     'b_group_2': 21.563,
     'b_inner_2': 12.906}
    for name, (base, spread) in spreads.items():
        noise = np.random.default_rng([zlib.crc32(name.encode()), seed]).standard_normal(out[name].shape)
        drawn = base * np.exp(spread * noise) if base else spread * noise
        out[name] = __import__('jax').numpy.asarray(drawn.astype(out[name].dtype))
    for name, factor in factors.items():
        out[name] = (out[name] * factor).astype(out[name].dtype)
    return out
```

```python
from contextlib import ExitStack

import concourse.bass as bass
import numpy as np
from concourse import mybir

F32 = mybir.dt.float32
I32 = mybir.dt.int32
ALU = mybir.AluOpType
ACT = mybir.ActivationFunctionType
AX = mybir.AxisListType

P = 128
D = 1024
KT = D // P
TOK = 512
DEPTH = 2
ALPHA = (2 * DEPTH) ** 0.25
EPS = 1e-6
LEVELS = [64, 32, 16, 8, 4, 2, 1]
NCH = TOK // P
SLOT = 4096
NSLOT = 4

C_ID, C_ONES, C_BONES, C_ROT, C_COS, C_SIN = 0, 128, 256, 384, 512, 768
C_MASK = 1024
C_EPS = C_MASK + 128 * len(LEVELS)
C_ONE = C_EPS + 1
C_W = C_EPS + 4
A_BADA, A_QN, A_KN, A_ABF, A_ABB, A_ON = 0, 24, 25, 26, 28, 30
A_A2 = 32
A_WS = A_A2 + 512
A_W = A_WS + 512
R_G, R_B, R_SB = 0, 512, 1024
R_W = 1536


M_ID, M_TRI, M_ONES, M_IOTA, M_CAUSAL, M_SEL = 0, 128, 256, 384, 512, 640
M_EPS = M_SEL + 1024
M_ONE = M_EPS + 1
M_GI = M_EPS + 2
M_NORM1, M_NORM2 = M_GI + 8, M_GI + 16
M_CONVW, M_CONVB = M_GI + 24, M_GI + 40
M_BA, M_BX, M_LAM, M_BF = M_GI + 44, M_GI + 48, M_GI + 52, M_GI + 56
M_BR = M_BF + 1
M_WF = M_BR + 36
M_WR = M_WF + 64
M_WA = M_WR + 288
M_WX = M_WA + 512
M_W = M_WX + 512
M_TOK = 256
G, E, FF = 4, 8, 256
ESLOT = KT * 2 * FF + 2 * D
NESLOT = 4


def trunk_slots(l):
    w = [(f"ada{i}", SLOT) for i in range(4)]
    w += [(n, SLOT) for n in ("sg", "su", "ag", "gg")]
    w += [("ak_gq_gate", 8 * 416), ("aq", SLOT), ("gk_av", 8 * 384), ("gv", SLOT), ("sv", SLOT)]
    for b in "sag":
        w += [(f"m{b}0", SLOT), (f"wbr{b}", SLOT), (f"m{b}1", SLOT)]
    w += [(f"ada{i}", SLOT) for i in (4, 5)] + [("wo0", SLOT), ("wo1", SLOT)]
    return [(f"{l}.{n}", k) for n, k in w]


def mixer_slots():
    return [(f"x.{n}", SLOT) for n in ("rec", "q", "k", "v", "gat", "wo0", "wo1")]


STREAM = trunk_slots(0) + trunk_slots(1) + mixer_slots()
SLOT_OF = {n: i for i, (n, _) in enumerate(STREAM)}
SLOT_WIDTH = [k for _, k in STREAM]



class Signal:

    def __init__(self, ctx, nc, name):
        self.sem = ctx.enter_context(nc.semaphore(name))
        self.count = self.base = 0

    def one(self):
        self.count += 1
        return self.sem, 1

    def dma(self):
        self.count += 16
        return self.sem, 16

    def at(self, k):
        return self.sem, self.base + k

    def now(self):
        return self.sem, self.count

    def seal(self):
        self.base = self.count


class Banks:

    def __init__(self, ctx, nc, name, n):
        self.tiles = [ctx.enter_context(nc.psum_tensor(f"{name}{i}", [P, 512], F32)) for i in range(n)]
        self.ready_sem = ctx.enter_context(nc.semaphore(f"{name}_ready"))
        self.evac_sem = [ctx.enter_context(nc.semaphore(f"{name}{i}_evacuated")) for i in range(n)]
        self.job = {}

    def open(self, pe, name):
        n, size = len(self.job), len(self.tiles)
        assert name not in self.job, name
        self.job[name] = n
        if n >= size:
            pe.wait_ge(self.evac_sem[n % size], n // size)
        return self.tiles[n % size]

    def done(self):
        return self.ready_sem, 1

    def tile(self, name):
        return self.tiles[self.job[name] % len(self.tiles)]

    def ready(self, name):
        return self.ready_sem, self.job[name] + 1

    def evac(self, name):
        return self.evac_sem[self.job[name] % len(self.tiles)], 1

    def evacuated(self, name):
        n, size = self.job[name], len(self.tiles)
        return self.evac_sem[n % size], n // size + 1


class Weights:

    def __init__(self, ctx, nc, dram):
        self.dram = dram
        self.ring = ctx.enter_context(nc.sbuf_tensor("weight_ring", [P, NSLOT, SLOT], F32))
        self.landed = [ctx.enter_context(nc.semaphore(f"slot{i}_landed")) for i in range(NSLOT)]
        self.last_reader = {}
        self.issued = 0

    def slot(self, pe, name, last_reader):
        i = SLOT_OF[name]
        pe.wait_ge(self.landed[i % NSLOT], 16 * (i // NSLOT + 1))
        self.last_reader[i] = last_reader
        return self.ring[:, i % NSLOT, 0:SLOT_WIDTH[i]]

    def issue(self, sp, upto):
        for i in range(self.issued, min(upto, len(STREAM))):
            if i >= NSLOT:
                banks, job = self.last_reader[i - NSLOT]
                sp.wait_ge(*banks.ready(job))
            k = SLOT_WIDTH[i]
            sp.dma_start(self.ring[:, i % NSLOT, 0:k], self.dram[i, :, 0:k]).then_inc(self.landed[i % NSLOT], 16)
        self.issued = max(self.issued, min(upto, len(STREAM)))


def linker(eng, own):
    def link(ins):
        ins.then_inc(*own.one())
        eng.wait_ge(*own.now())
    return link


class Signals:

    def __init__(self, ctx, nc):
        self.all = []

        def signal(name):
            self.all.append(Signal(ctx, nc, name))
            return self.all[-1]

        self.cond_in = signal("cond_in")
        self.small_in = signal("small_in")
        self.x_in = signal("x_in")
        self.post_in = signal("post_in")
        self.silu_c = signal("silu_c")
        self.h_ready = signal("h_ready")
        self.normed = signal("normed")
        self.roped = signal("roped")
        self.soft = signal("soft")
        self.head_rstd = signal("head_rstd")
        self.neg_max = signal("neg_max")
        self.probs = signal("probs")
        self.keys = signal("keys")
        self.key_diff = signal("key_diff")
        self.key_exp = signal("key_exp")
        self.lev_diff = signal("lev_diff")
        self.lev_exp = signal("lev_exp")
        self.lev_q = signal("lev_q")
        self.lev_k = signal("lev_k")
        self.query_exp = signal("query_exp")
        self.queries = signal("queries")
        self.sv_stat = signal("sv_stat")
        self.sv_rstd = signal("sv_rstd")
        self.vn = signal("vn")
        self.osq = signal("osq")
        self.orstd = signal("orstd")
        self.x_stat = signal("x_stat")
        self.x_rstd = signal("x_rstd")
        self.act_own = signal("act_own")
        self.dve_own = signal("dve_own")
        self.norm_rstd = signal("norm_rstd")
        self.scaled = signal("scaled")
        self.fsoft = signal("fsoft")
        self.cum = signal("cum")
        self.conv = signal("conv")
        self.gates_ri = signal("gates_ri")
        self.lam = signal("lam")
        self.lru_mult = signal("lru_mult")
        self.lru_seq = signal("lru_seq")
        self.route_max = signal("route_max")
        self.route_exp = signal("route_exp")
        self.inner_max = signal("inner_max")
        self.inner_exp = signal("inner_exp")
        self.one_hot = signal("one_hot")
        self.selected = signal("selected")
        self.silu_g = signal("silu_g")
        self.slots_w = signal("slots_w")
        self.x_done = signal("x_done")
        self.norm_out = signal("norm_out")
        self.over_flag = signal("over_flag")

    def seal(self):
        for s in self.all:
            s.seal()



def units_of(l):
    return [(s, j, t) for s in ((0, 1) if l == 0 else (1,)) for j in range(4) for t in range(2)]


def trunk_schedule(l):
    n_units = len(units_of(l))
    t0 = 0 if l == 0 else 2
    first = [("ada", 0)] + [("h", k) for k in range(KT)]
    first += [(n, i) for n in ("sg", "su", "ag", "gg") for i in range(4)]
    first += [("ak", 0), ("gq", 0), ("gq", 1), ("gate", 0)]
    first += [("z", i) for i in range(4)] + [("aq", i) for i in range(4)]
    first += [("gk", 0), ("gk", 1), ("decay", 0)] + [("stat", i) for i in range(5)] + [("av", 0)]
    first += [("rot", i) for i in range(5)]
    att = []
    for i in range(n_units + 2):
        att.append([s for s in (("score", i), ("turn", i - 1), ("pv", i - 2)) if 0 <= s[1] < n_units])
    rest = [("key", 0), ("gv", 0), ("gv", 1), ("keyt", 0), ("key", 1), ("gv", 2), ("gv", 3), ("keyt", 1)]
    rest += [("kv", i) for i in range(3)] + [("diag", 0)]
    fill = [("sv", t) for t in range(t0, 4)] + [("mix", g) for g in range(4)]
    for i in range(len(LEVELS)):
        rest += [("level", i)]
        if fill:
            rest += [fill.pop(0)]
        rest += [("pairs", i)]
    rest += [("query", 0)] + fill
    steps, per = list(first), -(-len(rest) // len(att))
    for a in att:
        steps += a + rest[:per]
        rest = rest[per:]
    steps += rest
    steps += [("out", 0), ("out", 1), ("ostat", 0), ("out", 2), ("ostat", 1), ("out", 3), ("ostat", 2), ("ostat", 3)]
    steps += [("merge", (b, c)) for b in "sag" for c in range(8)]
    steps += [("gada", 0), ("growb", 0)]
    steps += [("final", t) for t in range(t0, 4)]
    return steps


def trunk_layer(nc, l, io, W, jobs, sig, consts, silu_c, xlat, GVX, hT):
    T0 = 0 if l == 0 else 256
    NT = TOK - T0
    C0 = T0 // P
    NC = NCH - C0
    steps = trunk_schedule(l)
    small_in = 16 * (3 if l == 0 else 2)
    units = units_of(l)
    PJ, PS, PT = jobs
    ident = consts[:, C_ID:C_ID + P]
    eps = consts[:, C_EPS:C_EPS + 1]
    one = consts[:, C_ONE:C_ONE + 1]
    J = lambda name, *i: f"{l}.{name}" + "".join(f".{x}" for x in i)

    with ExitStack() as ctx:
        def sb(name, shape, dt=F32):
            return ctx.enter_context(nc.sbuf_tensor(f"l{l}_{name}", shape, dt))

        par = sb("params", [P, A_W])
        rows = sb("rows", [P, R_W])
        qg = sb("q_and_gla", [P, 16, 512])
        Q, GQ, GK = qg[:, 0:4], qg[:, 4:6], qg[:, 6:8]
        mT = qg[:, 0:8]
        DQ, DK = qg[:, 8:10], qg[:, 10:12]
        SCR = qg[:, 12:16]
        PR = SCR[:, 0:4].rearrange("p (b u) l -> p b u l", b=2)
        K = sb("k", [P, 512])
        V = sb("v", [P, 4, P])
        BF, BB = sb("b_fwd", [P, 2, 512]), sb("b_bwd", [P, 2, 512])
        GV = GVX
        ATT = sb("gla_att", [P, 4, 512])
        ATH = ATT[:].rearrange("p (u x) (c y) -> p u (x c) y", u=2, c=2)
        KET = ATT[:, :, 0:384]
        S = sb("gla_state", [P, 4, 3, P])
        ED = sb("gla_chunk_decay", [P, 4, 4])
        YA, YG, YS = sb("y_attn", [P, 4, 512]), sb("y_gla", [P, 4, 512]), sb("y_sgu", [P, 4, 512])
        PTB = sb("probs_t", [P, 2, 2, 512])
        TMP = PTB[:].rearrange("p b u l -> p (b u) l")
        small = sb("small", [P, 2, 8])
        ada = sb("ada", [P, 24, 2])
        stats = sb("stats", [P, 4, 16])
        rstd4 = sb("rstd", [P, 4, 2])
        agT = sb("gate_in", [32, 512])
        xctx = GVX[:].rearrange("p (t a) c -> p t (a c)", t=2)
        VN = (xlat[:].rearrange("p t (a c) -> p (t a) c", a=2) if l == 0 else None)
        gateb = ATT[:].rearrange("p (s h) c -> p s h c", s=2)
        post = [BF[:].rearrange("p a c -> p (a c)"), BB[:].rearrange("p a c -> p (a c)")]

        def vn(t):
            if l == 0:
                return VN[:, t, :]
            return Q[:, 2 * (t - 2):2 * (t - 2) + 2, 0:256]

        def vn_group(t, g):
            if l == 0:
                return VN[:, t, g * P:(g + 1) * P]
            return Q[:, 2 * (t - 2) + g // 2, (g % 2) * P:(g % 2) * P + P]

        def xres(t):
            return xctx[:, t, :] if t < 2 else xlat[:, t - 2, :]

        def sq(i):
            return (SCR[:, i] if i < 4 else PTB[:, 0, 0])

        def DQK(i):
            return (DQ[:, 0], DQ[:, 1], DK[:, 0], DK[:, 1])[i]

        block = ctx.enter_context(nc.Block())

        @block.tensor
        def _(pe):
            def feature_major(banks, name, w, col, m, t0=T0, src=hT, kts=KT):
                acc = banks.open(pe, name)
                for k in range(kts):
                    last = pe.matmul(acc[0:m, 0:TOK - t0], w[:, k, col:col + m], src[:, k, t0:TOK],
                                     start=(k == 0), stop=(k == kts - 1))
                last.then_inc(*banks.done())

            def token_major(banks, name, w, col, n, t, src=hT):
                acc = banks.open(pe, name)
                for k in range(KT):
                    last = pe.matmul(acc[:, 0:n], src[:, k, t * P:(t + 1) * P], w[:, k, col:col + n],
                                     start=(k == 0), stop=(k == KT - 1))
                last.then_inc(*banks.done())

            held = {}

            def slot(name, last_reader, cols=512):
                if name not in held:
                    held[name] = W.slot(pe, f"{l}.{name}", last_reader).rearrange("p (k c) -> p k c", c=cols)
                return held[name]

            def ada_tiles(acc, m0, m1, job):
                for m in range(m0, m1):
                    w = slot(f"ada{m // 4}", (PT, job))
                    for k in range(KT):
                        last = pe.matmul(acc[:, 2 * (m - m0):2 * (m - m0) + 2], w[:, k, (m % 4) * P:(m % 4) * P + P],
                                         silu_c[:, k, :], start=(k == 0), stop=(k == KT - 1))
                last.then_inc(*PT.done())

            if l == 0:
                pe.wait_ge(*sig.silu_c.at(1))
            pe.wait_ge(*sig.small_in.at(small_in))
            for kind, i in steps:
                if kind == "ada":
                    ada_tiles(PT.open(pe, J("ada")), 0, 16, J("ada"))
                elif kind == "h":
                    if l:
                        acc = PT.open(pe, J("h", i))
                        for t in range(4):
                            last = pe.transpose(acc[:, t * P:(t + 1) * P], xres(t)[:, i * P:(i + 1) * P], ident)
                        last.then_inc(*PT.done())
                elif kind in ("sg", "su", "ag", "gg", "aq"):
                    if kind == "sg" and i == 0:
                        pe.wait_ge(*(PT.evacuated(J("h", KT - 1)) if l else sig.h_ready.at(1)))
                    feature_major(PJ, J(kind, i), slot(kind, (PJ, J(kind, 3))), i * P, P)
                elif kind == "ak":
                    feature_major(PJ, J("ak"), slot("ak_gq_gate", (PJ, J("gate")), 416), 0, P, 0)
                elif kind == "gq":
                    feature_major(PJ, J("gq", i), held["ak_gq_gate"], P + i * P, P)
                elif kind == "gate":
                    feature_major(PJ, J("gate"), held["ak_gq_gate"], 384, 32, 0)
                elif kind == "gk":
                    feature_major(PJ, J("gk", i), slot("gk_av", (PJ, J("av")), 384), i * P, P, 0)
                elif kind == "av":
                    acc = PJ.open(pe, J("av"))
                    for t in range(4):
                        for k in range(KT):
                            last = pe.matmul(acc[:, t * P:(t + 1) * P], hT[:, k, t * P:(t + 1) * P],
                                             held["gk_av"][:, k, 256:384], start=(k == 0), stop=(k == KT - 1))
                    last.then_inc(*PJ.done())
                elif kind in ("gv", "sv"):
                    token_major(PJ, J(kind, i), slot(kind, (PJ, J(kind, 3))), 0, 512, i)
                elif kind == "z":
                    if i == 0:
                        pe.wait_ge(*PJ.evacuated(J("gate")))
                    acc = PT.open(pe, J("z", i))
                    pe.matmul(acc[:, :], par[0:32, A_A2 + i * P:A_A2 + (i + 1) * P], agT[:, :],
                              start=True, stop=True).then_inc(*PT.done())
                elif kind == "stat":
                    n = TOK if i == 0 else NT
                    pe.wait_ge(*PJ.evacuated(J("ak") if i == 0 else J("aq", i - 1)))
                    acc = PT.open(pe, J("stat", i))
                    pe.matmul(acc[:, 0:n], consts[:, C_BONES:C_BONES + P], sq(i)[:, 0:n],
                              start=True, stop=True).then_inc(*PT.done())
                elif kind == "rot":
                    pe.wait_ge(*sig.normed.at(i + 1))
                    acc = PT.open(pe, J("rot", i))
                    src = K[:, 256:512] if i == 0 else Q[:, i - 1, 256:512]
                    pe.matmul(acc[:, 0:256], consts[:, C_ROT:C_ROT + P], src,
                              start=True, stop=True).then_inc(*PT.done())
                elif kind == "score":
                    s, j, t = units[i]
                    n = 256 * (s + 1)
                    if i == 0:
                        pe.wait_ge(*sig.roped.at(5))
                    for u in range(2):
                        acc = PS.open(pe, J("score", i, u))
                        tok = s * 256 + t * P
                        pe.matmul(acc[:, 0:n], Q[64 * u:64 * u + 64, j, tok:tok + P], K[64 * u:64 * u + 64, 0:n],
                                  start=True, stop=True).then_inc(*PS.done())
                elif kind == "turn":
                    s = units[i][0]
                    for u in range(2):
                        pe.wait_ge(*sig.probs.at(2 * i + u + 1))
                        acc = PT.open(pe, J("turn", i, u))
                        for b in range(2 * (s + 1)):
                            last = pe.transpose(acc[:, b * P:(b + 1) * P], PR[:, i % 2, u, b * P:(b + 1) * P], ident)
                        last.then_inc(*PT.done())
                elif kind == "pv":
                    s = units[i][0]
                    if i == 0:
                        pe.wait_ge(*PJ.evacuated(J("av")))
                    acc = PJ.open(pe, J("pv", i))
                    nb = 2 * (s + 1)
                    for u in range(2):
                        pe.wait_ge(*PT.evacuated(J("turn", i, u)))
                        for b in range(nb):
                            last = pe.matmul(acc[64 * u:64 * u + 64, 0:P], V[:, b, 64 * u:64 * u + 64],
                                             PTB[:, i % 2, u, b * P:(b + 1) * P], start=(b == 0), stop=(b == nb - 1))
                    last.then_inc(*PJ.done())
                elif kind == "keyt":
                    pe.wait_ge(*sig.keys.at(i + 1))
                    for p in range(2):
                        acc = PT.open(pe, J("keyt", i, p))
                        for n, c in enumerate((0, 1, 2) if i == 0 else (1, 0, 3)):
                            last = pe.transpose(acc[:, n * P:(n + 1) * P], DK[:, p, c * P:(c + 1) * P], ident)
                        last.then_inc(*PT.done())
                elif kind == "kv":
                    if i == 0:
                        pe.wait_ge(*PJ.evacuated(J("gv", 3)))
                        for d in range(2):
                            for p in range(2):
                                pe.wait_ge(*PT.evacuated(J("keyt", d, p)))
                    acc = PT.open(pe, J("kv", i))
                    for d in range(2):
                        c = (0, 1, 2)[i] if d == 0 else (1, 0, 3)[i]
                        for p in range(2):
                            for u in range(2):
                                last = pe.matmul(acc[64 * u:64 * u + 64, (2 * d + p) * P:(2 * d + p + 1) * P],
                                                 KET[:, 2 * d + p, i * P + 64 * u:i * P + 64 * u + 64],
                                                 GV[:, c, (2 * p + u) * P:(2 * p + u + 1) * P], start=True, stop=True)
                    last.then_inc(*PT.done())
                elif kind in ("diag", "pairs"):
                    if kind == "diag":
                        pe.wait_ge(*PJ.evacuated(J("gq", 1)))
                        pe.wait_ge(*PJ.evacuated(J("gk", 1)))
                        q, k = GQ, GK
                    else:
                        pe.wait_ge(*sig.lev_q.at(i + 1))
                        pe.wait_ge(*sig.lev_k.at(i + 1))
                        q, k = DQ, DK
                    for s2 in range(C0 // 2, 2):
                        for u in range(2):
                            acc = PT.open(pe, J(kind, i, s2, u))
                            for n in range(4):
                                c, p = 2 * s2 + n // 2, n % 2
                                last = pe.matmul(acc[:, n * P:(n + 1) * P], k[64 * u:64 * u + 64, p, c * P:(c + 1) * P],
                                                 q[64 * u:64 * u + 64, p, c * P:(c + 1) * P], start=True, stop=True)
                            last.then_inc(*PT.done())
                elif kind == "mix":
                    for c in range(C0, NCH):
                        pe.wait_ge(*sig.vn.at(c - C0 + 1))
                    acc = PJ.open(pe, J("mix", i))
                    for c in range(C0, NCH):
                        last = pe.matmul(acc[:, (c - C0) * P:(c - C0 + 1) * P], vn_group(c, i),
                                         par[:, A_WS + i * P:A_WS + (i + 1) * P], start=True, stop=True)
                    last.then_inc(*PJ.done())
                elif kind == "out":
                    if i == 0:
                        pe.wait_ge(*sig.queries.at(2))
                        pe.wait_ge(*PT.evacuated(J("kv", 2)))
                        pe.wait_ge(*PT.evacuated(J("pairs", len(LEVELS) - 1, 1, 0)))
                        pe.wait_ge(*PT.evacuated(J("pairs", len(LEVELS) - 1, 1, 1)))
                    p, u = i // 2, i % 2
                    acc = PJ.open(pe, J("out", i))
                    for c in range(C0, NCH):
                        o = acc[:, (c - C0) * P:(c - C0 + 1) * P]
                        from_state = [(d, n) for d, n in ((0, c), (1, c ^ 1)) if n > 0]
                        pe.matmul(o, GV[:, c, i * P:(i + 1) * P], ATH[:, u, c, p * P:(p + 1) * P], start=True, stop=False)
                        for x, (d, n) in enumerate(from_state):
                            b = (BF, BB)[d]
                            last = pe.matmul(o, S[64 * u:64 * u + 64, 2 * d + p, n - 1, :],
                                             b[64 * u:64 * u + 64, p, c * P:(c + 1) * P],
                                             start=False, stop=(x == len(from_state) - 1))
                    last.then_inc(*PJ.done())
                elif kind == "ostat":
                    pe.wait_ge(*sig.osq.at(i + 1))
                    acc = PT.open(pe, J("ostat", i))
                    pe.matmul(acc[:, 0:NT], consts[:, C_ONES:C_ONES + P], DQK(i)[:, 0:NT],
                              start=True, stop=True).then_inc(*PT.done())
                elif kind == "merge":
                    b, c = i
                    w = slot(f"m{b}{c // 4}", (PJ, J("gate_m", b, c // 4 * 4 + 3)))
                    feature_major(PJ, J("gate_m", b, c), w, (c % 4) * P, P)
                    y = {"s": YS, "a": YA, "g": YG}[b]
                    if c == 0:
                        pe.wait_ge(*PJ.evacuated({"s": J("mix", 3), "a": J("pv", len(units) - 1), "g": J("out", 3)}[b]))
                    w = slot(f"wbr{b}", (PS, J("br", b, 7)), 1024)
                    acc = PS.open(pe, J("br", b, c))
                    for k in range(4):
                        last = pe.matmul(acc[:, 0:NT], w[:, k, c * P:(c + 1) * P], y[:, k, T0:TOK],
                                         start=(k == 0), stop=(k == 3))
                    last.then_inc(*PS.done())
                elif kind == "gada":
                    ada_tiles(PT.open(pe, J("gada")), 16, 24, J("gada"))
                elif kind == "growb":
                    pe.wait_ge(*PT.evacuated(J("gada")))
                    for s in range(C0 // 2, 2):
                        for h in range(2):
                            acc = PT.open(pe, J("growb", s, h))
                            for m in range(4):
                                col = ada[:, 16 + 4 * h + m, s:s + 1]
                                last = pe.matmul(acc[:, m * P:(m + 1) * P], col.to_broadcast([P, P]), ident,
                                                 start=True, stop=True)
                            last.then_inc(*PT.done())
                elif kind == "final":
                    if i == C0:
                        pe.wait_ge(*PS.evacuated(J("br", "g", 7)))
                    for h in range(2):
                        w = slot(f"wo{h}", (PJ, J("final", 3, h)))
                        token_major(PJ, J("final", i, h), w, 0, 512, i, src=mT)

        @block.scalar
        def _(act):
            link = linker(act, sig.act_own)
            if l == 0:
                act.wait_ge(*sig.cond_in.at(16))
                act.activation(silu_c[:], silu_c[:], ACT.Silu).then_inc(*sig.silu_c.one())
            act.wait_ge(*sig.small_in.at(small_in))
            for kind, i in steps:
                if kind in ("sg", "ag", "gg"):
                    act.wait_ge(*PJ.ready(J(kind, i)))
                    y = {"sg": YS, "ag": YA, "gg": YG}[kind]
                    act.activation(y[:, i, T0:], PJ.tile(J(kind, i))[:, 0:NT], ACT.Silu).then_inc(*PJ.evac(J(kind, i)))
                elif kind in ("ak", "aq"):
                    name, n, t0 = (J("ak"), 0, 0) if kind == "ak" else (J("aq", i), i + 1, T0)
                    dst = K[:, :] if kind == "ak" else Q[:, i, T0:]
                    act.wait_ge(*PJ.ready(name))
                    acc = PJ.tile(name)[:, 0:TOK - t0]
                    act.activation(dst, acc, ACT.Copy)
                    act.activation(sq(n)[:, 0:TOK - t0], acc, ACT.Square).then_inc(*PJ.evac(name))
                elif kind == "gq":
                    act.wait_ge(*PJ.ready(J("gq", i)))
                    act.activation(GQ[:, i, T0:], PJ.tile(J("gq", i))[:, 0:NT], ACT.Copy, scale=0.125)\
                        .then_inc(*PJ.evac(J("gq", i)))
                elif kind == "gk":
                    act.wait_ge(*PJ.ready(J("gk", i)))
                    act.activation(GK[:, i, :], PJ.tile(J("gk", i))[:, :], ACT.Copy).then_inc(*PJ.evac(J("gk", i)))
                elif kind == "gate":
                    act.wait_ge(*PJ.ready(J("gate")))
                    act.activation(agT[:, :], PJ.tile(J("gate"))[0:32, :], ACT.Copy).then_inc(*PJ.evac(J("gate")))
                elif kind == "av":
                    act.wait_ge(*PJ.ready(J("av")))
                    act.activation(V[:], PJ.tile(J("av"))[:].rearrange("p (t c) -> p t c", t=4), ACT.Copy)\
                        .then_inc(*PJ.evac(J("av")))
                elif kind == "gv":
                    act.wait_ge(*PJ.ready(J("gv", i)))
                    act.activation(GV[:, i, :], PJ.tile(J("gv", i))[:, :], ACT.Copy).then_inc(*PJ.evac(J("gv", i)))
                elif kind == "z":
                    t = (DQ[:, 0], DQ[:, 1], DK[:, 0], DK[:, 1])[i]
                    act.wait_ge(*PT.ready(J("z", i)))
                    link(act.activation(t, PT.tile(J("z", i))[:, :], ACT.Abs, bias=par[:, A_ABF + i:A_ABF + i + 1]))
                    link(act.activation(t, t, ACT.Exp, scale=-1.0))
                    act.activation(t, t, ACT.Ln, bias=one).then_inc(*sig.soft.one())
                elif kind == "stat":
                    n = TOK if i == 0 else NT
                    act.wait_ge(*PT.ready(J("stat", i)))
                    act.activation(sq(i)[:, 0:n], PT.tile(J("stat", i))[:, 0:n], ACT.Ln, bias=eps)\
                        .then_inc(*PT.evac(J("stat", i)))
                    act.wait_ge(*PT.evacuated(J("stat", i)))
                    act.activation(sq(i)[:, 0:n], sq(i)[:, 0:n], ACT.Exp, scale=-0.5).then_inc(*sig.head_rstd.one())
                elif kind == "score":
                    s, j, t = units[i]
                    n = 256 * (s + 1)
                    for u in range(2):
                        act.wait_ge(*sig.neg_max.at(2 * i + u + 1))
                        if i == 0 and u == 0:
                            act.wait_ge(*sig.roped.at(5))
                        act.activation(PR[:, i % 2, u, 0:n], PS.tile(J("score", i, u))[:, 0:n], ACT.Exp,
                                       bias=small[:, i % 2, 2 + u:3 + u], scale=0.125,
                                       accum_out=small[:, i % 2, 4 + u:5 + u]).then_inc(*PS.evac(J("score", i, u)))
                elif kind == "turn":
                    n = 256 * (units[i][0] + 1)
                    for u in range(2):
                        act.wait_ge(*PT.ready(J("turn", i, u)))
                        if i >= 2:
                            act.wait_ge(*PJ.ready(J("pv", i - 2)))
                        act.activation(PTB[:, i % 2, u, 0:n], PT.tile(J("turn", i, u))[:, 0:n], ACT.Copy)\
                            .then_inc(*PT.evac(J("turn", i, u)))
                elif kind == "key":
                    act.wait_ge(*sig.key_diff.at(i + 1))
                    e = act.activation(DK, DK, ACT.Exp, scale=1 / 16)
                    b, edge = ((BF, 127), (BB, 0))[i]
                    bv = b[:].rearrange("p a (c t) -> p a c t", t=P)
                    act.activation(ED[:, 2 * i:2 * i + 2, :], bv[:, :, :, edge], ACT.Exp, scale=1 / 16)\
                        .then_inc(*sig.key_exp.one())
                elif kind == "keyt":
                    for p in range(2):
                        act.wait_ge(*PT.ready(J("keyt", i, p)))
                        act.activation(KET[:, 2 * i + p, :], PT.tile(J("keyt", i, p))[:, 0:384], ACT.Copy)\
                            .then_inc(*PT.evac(J("keyt", i, p)))
                elif kind == "level":
                    act.wait_ge(*sig.lev_diff.at(i + 1))
                    act.activation(DQ[:, :, T0:], DQ[:, :, T0:], ACT.Exp, scale=1 / 16)
                    act.activation(DK[:, :, T0:], DK[:, :, T0:], ACT.Exp, scale=1 / 16).then_inc(*sig.lev_exp.one())
                elif kind == "query":
                    if i == 0:
                        act.wait_ge(*sig.lev_diff.at(len(LEVELS)))
                    act.activation(BF[:, :, T0:], BF[:, :, T0:], ACT.Exp, scale=1 / 16).then_inc(*sig.query_exp.one())
                    act.activation(BB[:, :, T0:], BB[:, :, T0:], ACT.Exp, scale=1 / 16).then_inc(*sig.query_exp.one())
                elif kind == "sv":
                    act.wait_ge(*sig.sv_stat.at(i - C0 + 1))
                    link(act.activation(rstd4[:, i, 0:1], stats[:, i, 13:14], ACT.Ln, bias=eps))
                    act.activation(rstd4[:, i, 0:1], rstd4[:, i, 0:1], ACT.Exp, scale=-0.5).then_inc(*sig.sv_rstd.one())
                elif kind == "out":
                    act.wait_ge(*PJ.ready(J("out", i)))
                    act.activation(DQK(i)[:, 0:NT], PJ.tile(J("out", i))[:, 0:NT], ACT.Square).then_inc(*sig.osq.one())
                elif kind == "ostat":
                    act.wait_ge(*PT.ready(J("ostat", i)))
                    d = DQK(i)[:, 0:NT]
                    act.activation(d, PT.tile(J("ostat", i))[:, 0:NT], ACT.Ln, bias=eps).then_inc(*PT.evac(J("ostat", i)))
                    act.wait_ge(*PT.evacuated(J("ostat", i)))
                    act.activation(d, d, ACT.Exp, scale=-0.5).then_inc(*sig.orstd.one())
                elif kind == "merge":
                    b, c = i
                    n = "sag".index(b) * 8 + c
                    act.wait_ge(*PJ.ready(J("gate_m", b, c)))
                    if n >= 4:
                        act.wait_ge(*PS.evacuated(J("br", "sag"[(n - 4) // 8], (n - 4) % 8)))
                    act.activation(SCR[:, n % 4, 0:NT], PJ.tile(J("gate_m", b, c))[:, 0:NT], ACT.Sigmoid)\
                        .then_inc(*PJ.evac(J("gate_m", b, c)))
                elif kind == "growb":
                    for s in range(C0 // 2, 2):
                        for h in range(2):
                            act.wait_ge(*PT.ready(J("growb", s, h)))
                            act.activation(gateb[:, s, h, :], PT.tile(J("growb", s, h))[:, :], ACT.Copy)\
                                .then_inc(*PT.evac(J("growb", s, h)))
                elif kind == "final":
                    act.wait_ge(*sig.x_stat.at(i - C0 + 1))
                    link(act.activation(rstd4[:, i, 1:2], stats[:, i, 13:14], ACT.Ln, bias=eps))
                    act.activation(rstd4[:, i, 1:2], rstd4[:, i, 1:2], ACT.Exp, scale=-0.5).then_inc(*sig.x_rstd.one())

        @block.vector
        def _(dve):
            link = linker(dve, sig.dve_own)
            dve.wait_ge(*sig.small_in.at(small_in))

            att_banks = [(s2, u) for s2 in range(C0 // 2, 2) for u in range(2)]

            def att_of(s2, u):
                return ATT[:, 2 * u + s2, :].rearrange("p (h t) -> p h t", h=4)

            def half_views(x, h):
                return x[:, :, T0:].rearrange("p a (n two h) -> p a n two h", two=2, h=h)

            for kind, i in steps:
                if kind == "ada":
                    dve.wait_ge(*PT.ready(J("ada")))
                    acc = PT.tile(J("ada"))[:, 0:32].rearrange("p (m s) -> p m s", s=2)
                    bias = par[:, A_BADA:A_BADA + 16].unsqueeze(2).to_broadcast([P, 16, 2])
                    dve.tensor_tensor(ada[:, 0:16, :], acc, bias, ALU.add).then_inc(*PT.evac(J("ada")))
                    dve.wait_ge(*PT.evacuated(J("ada")))
                    link(dve.tensor_scalar(ada[:, 8:16, :], ada[:, 8:16, :], 1.0, None, ALU.add))
                    if l == 0:
                        dve.wait_ge(*sig.x_in.at(32))
                elif kind == "h":
                    if l:
                        dve.wait_ge(*PT.ready(J("h", i)))
                    for s in range(2):
                        src = PT.tile(J("h", i))[:, s * 256:(s + 1) * 256] if l else hT[:, i, s * 256:(s + 1) * 256]
                        last = dve.tensor_scalar(hT[:, i, s * 256:(s + 1) * 256], src, ada[:, 8 + i, s:s + 1],
                                                 ada[:, i, s:s + 1], ALU.mult, ALU.add)
                    if l:
                        last.then_inc(*PT.evac(J("h", i)))
                    elif i == KT - 1:
                        last.then_inc(*sig.h_ready.one())
                elif kind == "su":
                    dve.wait_ge(*PJ.ready(J("su", i)))
                    dve.wait_ge(*PJ.evacuated(J("sg", i)))
                    dve.tensor_tensor(YS[:, i, T0:], PJ.tile(J("su", i))[:, 0:NT], YS[:, i, T0:], ALU.mult)\
                        .then_inc(*PJ.evac(J("su", i)))
                elif kind == "z":
                    b = (BF, BB)[i // 2][:, i % 2, :]
                    dve.wait_ge(*sig.soft.at(i + 1))
                    dve.tensor_scalar(b, PT.tile(J("z", i))[:, :], par[:, A_ABF + i:A_ABF + i + 1], 0.0,
                                      ALU.add, ALU.min).then_inc(*PT.evac(J("z", i)))
                    dve.wait_ge(*PT.evacuated(J("z", i)))
                    t = (DQ[:, 0], DQ[:, 1], DK[:, 0], DK[:, 1])[i]
                    link(dve.tensor_tensor(b, b, t, ALU.subtract))
                elif kind == "decay":
                    for d in range(2):
                        for p in range(2):
                            for c in range(NCH):
                                b = (BF, BB)[d][:, p, c * P:(c + 1) * P]
                                if d:
                                    b = b[:, ::-1]
                                last = dve.tensor_tensor_scan(b, one.to_broadcast([P, P]), b, 0.0, ALU.mult, ALU.add)
                    link(last)
                elif kind == "stat":
                    n = slice(0, TOK) if i == 0 else slice(T0, TOK)
                    x = K[:, n] if i == 0 else Q[:, i - 1, n]
                    w = A_KN if i == 0 else A_QN
                    dve.wait_ge(*sig.head_rstd.at(i + 1))
                    dve.scalar_tensor_tensor(x, x, par[:, w:w + 1], sq(i)[:, 0:(TOK if i == 0 else NT)],
                                             ALU.mult, ALU.mult).then_inc(*sig.normed.one())
                elif kind == "rot":
                    x = K[:, 256:512] if i == 0 else Q[:, i - 1, 256:512]
                    t = sq(i)[:, 0:256]
                    dve.wait_ge(*PT.ready(J("rot", i)))
                    dve.tensor_tensor(t, PT.tile(J("rot", i))[:, 0:256], consts[:, C_SIN:C_SIN + 256], ALU.mult)\
                        .then_inc(*PT.evac(J("rot", i)))
                    link(dve.tensor_tensor(x, x, consts[:, C_COS:C_COS + 256], ALU.mult))
                    dve.tensor_tensor(x, x, t, ALU.add).then_inc(*sig.roped.one())
                elif kind == "score":
                    n = 256 * (units[i][0] + 1)
                    for u in range(2):
                        dve.wait_ge(*PS.ready(J("score", i, u)))
                        link(dve.reduce_max(small[:, i % 2, u:u + 1], PS.tile(J("score", i, u))[:, 0:n], AX.X))
                        dve.tensor_scalar(small[:, i % 2, 2 + u:3 + u], small[:, i % 2, u:u + 1], -0.125, None,
                                          ALU.mult).then_inc(*sig.neg_max.one())
                elif kind == "turn":
                    n = 256 * (units[i][0] + 1)
                    for u in range(2):
                        dve.wait_ge(*PS.evacuated(J("score", i, u)))
                        link(dve.reciprocal(small[:, i % 2, 6 + u:7 + u], small[:, i % 2, 4 + u:5 + u]))
                        dve.tensor_scalar(PR[:, i % 2, u, 0:n], PR[:, i % 2, u, 0:n], small[:, i % 2, 6 + u:7 + u],
                                          None, ALU.mult).then_inc(*sig.probs.one())
                elif kind == "pv":
                    s, j, t = units[i]
                    tok = s * 256 + t * P
                    dve.wait_ge(*PJ.ready(J("pv", i)))
                    if i == 0:
                        dve.wait_ge(*PJ.evacuated(J("ag", 3)))
                    dve.tensor_tensor(YA[:, j, tok:tok + P], PJ.tile(J("pv", i))[:, 0:P], YA[:, j, tok:tok + P],
                                      ALU.mult).then_inc(*PJ.evac(J("pv", i)))
                elif kind == "key":
                    b, edge = ((BF, 127), (BB, 0))[i]
                    bv = b[:].rearrange("p a (c t) -> p a c t", t=P)
                    dk = DK.rearrange("p a (c t) -> p a c t", t=P)
                    if i:
                        dve.wait_ge(*PT.ready(J("keyt", 0, 1)))
                    for p in range(2):
                        last = dve.tensor_tensor(dk[:, p], bv[:, p, :, edge:edge + 1].to_broadcast([P, NCH, P]),
                                                 bv[:, p], ALU.subtract)
                    last.then_inc(*sig.key_diff.one())
                    dve.wait_ge(*sig.key_exp.at(i + 1))
                    dve.wait_ge(*PJ.evacuated(J("gk", 1)))
                    dve.tensor_tensor(DK, DK, GK, ALU.mult).then_inc(*sig.keys.one())
                elif kind == "kv":
                    dve.wait_ge(*PT.ready(J("kv", i)))
                    for d in range(2):
                        c = (0, 1, 2)[i] if d == 0 else (1, 0, 3)[i]
                        for p in range(2):
                            n = 2 * d + p
                            kv = PT.tile(J("kv", i))[:, n * P:(n + 1) * P]
                            if i == 0:
                                last = dve.tensor_copy(S[:, n, 0, :], kv)
                            else:
                                last = dve.scalar_tensor_tensor(S[:, n, i, :], S[:, n, i - 1, :], ED[:, n, c:c + 1], kv,
                                                                ALU.mult, ALU.add)
                    last.then_inc(*PT.evac(J("kv", i)))
                    dve.wait_ge(*PT.evacuated(J("kv", i)))
                elif kind == "diag":
                    eye = ident.unsqueeze(1).to_broadcast([P, 4, P])
                    for s2, u in att_banks:
                        job = J("diag", 0, s2, u)
                        dve.wait_ge(*PT.ready(job))
                        acc = PT.tile(job)[:, :].rearrange("p (h t) -> p h t", h=4)
                        dve.scalar_tensor_tensor(att_of(s2, u), acc, 2.0, eye, ALU.mult, ALU.mult).then_inc(*PT.evac(job))
                elif kind == "level":
                    h = LEVELS[i]
                    if i == 0:
                        dve.wait_ge(*PT.ready(J("keyt", 1, 1)))
                        dve.wait_ge(*PJ.evacuated(J("gq", 1)))
                    else:
                        dve.wait_ge(*PT.ready(J("pairs", i - 1, 1, 1)))
                    f, b, q, k = (half_views(x, h) for x in (BF, BB, DQ, DK))
                    for p in range(2):
                        n = [P, NT // (2 * h), h]
                        fe = f[:, p, :, 0, h - 1:h].to_broadcast(n)
                        be = b[:, p, :, 1, 0:1].to_broadcast(n)
                        dve.tensor_tensor(q[:, p, :, 1, :], f[:, p, :, 1, :], fe, ALU.subtract)
                        dve.tensor_tensor(q[:, p, :, 0, :], b[:, p, :, 0, :], be, ALU.subtract)
                        dve.tensor_tensor(k[:, p, :, 0, :], fe, f[:, p, :, 0, :], ALU.subtract)
                        last = dve.tensor_tensor(k[:, p, :, 1, :], be, b[:, p, :, 1, :], ALU.subtract)
                    last.then_inc(*sig.lev_diff.one())
                    dve.wait_ge(*sig.lev_exp.at(i + 1))
                    dve.tensor_tensor(DQ[:, :, T0:], DQ[:, :, T0:], GQ[:, :, T0:], ALU.mult).then_inc(*sig.lev_q.one())
                elif kind == "pairs":
                    m = consts[:, C_MASK + i * P:C_MASK + (i + 1) * P].bitcast(I32).unsqueeze(1).to_broadcast([P, 4, P])
                    for s2, u in att_banks:
                        job = J("pairs", i, s2, u)
                        dve.wait_ge(*PT.ready(job))
                        acc = PT.tile(job)[:, :].rearrange("p (h t) -> p h t", h=4)
                        if i == 0:
                            dve.wait_ge(*PT.evacuated(J("diag", 0, s2, u)))
                        dve.copy_predicated(att_of(s2, u), m, acc).then_inc(*PT.evac(job))
                elif kind == "query":
                    for d, b in enumerate((BF, BB)):
                        dve.wait_ge(*sig.query_exp.at(d + 1))
                        dve.tensor_tensor(b[:, :, T0:], b[:, :, T0:], GQ[:, :, T0:], ALU.mult).then_inc(*sig.queries.one())
                elif kind == "sv":
                    dve.wait_ge(*PJ.ready(J("sv", i)))
                    acc = PJ.tile(J("sv", i))[:, :]
                    link(dve.bn_stats(stats[:, i, 0:6], acc))
                    dve.bn_aggr(stats[:, i, 12:14], stats[:, i, 0:6]).then_inc(*sig.sv_stat.one())
                    dve.wait_ge(*sig.sv_rstd.at(i - C0 + 1))
                    g = rows[:, R_G:R_G + 512]
                    b = rows[:, R_B:R_B + 512]
                    if l:
                        acc, g, b = (x.rearrange("p (a c) -> p a c", a=2) for x in (acc, g, b))
                        if i == C0:
                            dve.wait_ge(*sig.roped.at(5))
                    dve.tensor_scalar(vn(i), acc, stats[:, i, 12:13], rstd4[:, i, 0:1], ALU.subtract, ALU.mult)\
                        .then_inc(*PJ.evac(J("sv", i)))
                    dve.wait_ge(*PJ.evacuated(J("sv", i)))
                    link(dve.tensor_tensor(vn(i), vn(i), g, ALU.mult))
                    dve.tensor_tensor(vn(i), vn(i), b, ALU.add).then_inc(*sig.vn.one())
                elif kind == "mix":
                    dve.wait_ge(*PJ.ready(J("mix", i)))
                    acc = PJ.tile(J("mix", i))[:, 0:NT].rearrange("p (c t) -> p c t", t=P)
                    bias = rows[:, R_SB + i * P:R_SB + (i + 1) * P].unsqueeze(1).to_broadcast([P, NC, P])
                    link(dve.tensor_tensor(acc, acc, bias, ALU.add))
                    dve.tensor_tensor(YS[:, i, T0:], YS[:, i, T0:], PJ.tile(J("mix", i))[:, 0:NT], ALU.mult)\
                        .then_inc(*PJ.evac(J("mix", i)))
                elif kind == "ostat":
                    dve.wait_ge(*sig.orstd.at(i + 1))
                    d = DQK(i)[:, 0:NT]
                    link(dve.scalar_tensor_tensor(d, PJ.tile(J("out", i))[:, 0:NT], par[:, A_ON:A_ON + 1], d,
                                                  ALU.mult, ALU.mult))
                    dve.tensor_tensor(YG[:, i, T0:], YG[:, i, T0:], d, ALU.mult).then_inc(*PJ.evac(J("out", i)))
                elif kind == "merge":
                    b, c = i
                    n = "sag".index(b) * 8 + c
                    g = SCR[:, n % 4, 0:NT]
                    dve.wait_ge(*PJ.evacuated(J("gate_m", b, c)))
                    dve.wait_ge(*PS.ready(J("br", b, c)))
                    acc = PS.tile(J("br", b, c))[:, 0:NT]
                    if b == "s":
                        dve.tensor_tensor(mT[:, c, T0:], acc, g, ALU.mult).then_inc(*PS.evac(J("br", b, c)))
                    else:
                        link(dve.tensor_tensor(TMP[:, c % 4, 0:NT], acc, g, ALU.mult))
                        last = dve.tensor_tensor(mT[:, c, T0:], mT[:, c, T0:], TMP[:, c % 4, 0:NT], ALU.add)
                        last.then_inc(*PS.evac(J("br", b, c)))
                elif kind == "gada":
                    dve.wait_ge(*PT.ready(J("gada")))
                    acc = PT.tile(J("gada"))[:, 0:16].rearrange("p (m s) -> p m s", s=2)
                    bias = par[:, A_BADA + 16:A_BADA + 24].unsqueeze(2).to_broadcast([P, 8, 2])
                    dve.tensor_tensor(ada[:, 16:24, :], acc, bias, ALU.add).then_inc(*PT.evac(J("gada")))
                elif kind == "final":
                    x = xres(i)
                    if i == C0:
                        dve.wait_ge(*sig.post_in.at(16 * (4 if l == 0 else 2)))
                    for h in range(2):
                        if i % 2 == 0 and h == 0:
                            dve.wait_ge(*PT.evacuated(J("growb", i // 2, 1)))
                        dve.wait_ge(*PJ.ready(J("final", i, h)))
                        t = TMP[:, h, :]
                        dve.tensor_tensor(t, PJ.tile(J("final", i, h))[:, :], gateb[:, i // 2, h, :], ALU.mult)\
                            .then_inc(*PJ.evac(J("final", i, h)))
                        dve.wait_ge(*PJ.evacuated(J("final", i, h)))
                        xh = x[:, h * 512:(h + 1) * 512]
                        link(dve.scalar_tensor_tensor(xh, xh, ALPHA, t, ALU.mult, ALU.add))
                        link(dve.bn_stats(stats[:, i, 6 * h:6 * h + 6], xh))
                    dve.bn_aggr(stats[:, i, 12:14], stats[:, i, 0:12].rearrange("p (a b) -> p a b", a=2))\
                        .then_inc(*sig.x_stat.one())
                    dve.wait_ge(*sig.x_rstd.at(i - C0 + 1))
                    link(dve.tensor_scalar(x, x, stats[:, i, 12:13], rstd4[:, i, 1:2], ALU.subtract, ALU.mult))
                    link(dve.tensor_tensor(x, x, post[0], ALU.mult))
                    link(dve.tensor_tensor(x, x, post[1], ALU.add))

        @block.gpsimd
        def _(pool):
            pool.wait_ge(*PJ.evacuated(J("gk", 1)))
            for kind, i in steps:
                if kind == "level":
                    pool.wait_ge(*sig.lev_exp.at(i + 1))
                    pool.tensor_tensor(DK[:, :, T0:], DK[:, :, T0:], GK[:, :, T0:], ALU.mult).then_inc(*sig.lev_k.one())

        @block.sync
        def _(sp):
            if l == 0:
                sp.dma_start(silu_c[:], io["cond"]).then_inc(*sig.cond_in.dma())
                sp.dma_start(consts[:], io["consts"]).then_inc(*sig.small_in.dma())
            sp.dma_start(par[:], io["params"][l]).then_inc(*sig.small_in.dma())
            sp.dma_start(rows[:], io["rows"][l]).then_inc(*sig.small_in.dma())
            if l == 0:
                W.issue(sp, NSLOT)
                sp.dma_start(hT[:, 0:4, :], io["xT"][:, 0:4, :]).then_inc(*sig.x_in.dma())
                sp.dma_start(hT[:, 4:8, :], io["xT"][:, 4:8, :]).then_inc(*sig.x_in.dma())
            end = sum(len(trunk_slots(x)) for x in range(l + 1))
            W.issue(sp, SLOT_OF[f"{l}.wo0"] - 1)
            sp.wait_ge(*PJ.evacuated(J("out", 3)))
            if l == 0:
                sp.wait_ge(*PJ.ready(J("mix", 3)))
                sp.dma_start(xctx, io["ctx_rows"]).then_inc(*sig.post_in.dma())
                sp.dma_start(xlat[:], io["x_rows"]).then_inc(*sig.post_in.dma())
            for n in range(2):
                sp.dma_start(post[n], io["post"][l, n].partition_broadcast(P)).then_inc(*sig.post_in.dma())
            W.issue(sp, end + NSLOT)



def mixer_schedule():
    steps = [("norm", t) for t in range(2)] + [("turnx", i) for i in range(4)]
    steps += [("f", 0)] + [("rec", i) for i in range(4)] + [("q", i) for i in range(4)] + [("cum", 0)]
    steps += [("k", i) for i in range(4)] + [("ri", i) for i in range(4)] + [("v", t) for t in range(2)]
    steps += [("lru", 0)] + [("gat", i) for i in range(4)]
    for i in range(8 + 2):
        steps += [s for s in (("score", i), ("turn", i - 1), ("pv", i - 2)) if 0 <= s[1] < 8]
    return steps + [("out", t) for t in range(2)]


def mixer(nc, io, W, EW, jobs, sig, xlat):
    T = M_TOK
    PJ, PS, PT = jobs
    J = lambda name, *i: f"x.{name}" + "".join(f".{x}" for x in i)
    steps = mixer_schedule()
    units = [(j, t) for j in range(4) for t in range(2)]

    with ExitStack() as ctx:
        def sb(name, shape, dt=F32):
            return ctx.enter_context(nc.sbuf_tensor(f"x_{name}", shape, dt))

        par = sb("params", [P, M_W])
        ident = par[:, M_ID:M_ID + P]
        eps, one = par[:, M_EPS:M_EPS + 1], par[:, M_ONE:M_ONE + 1]
        XS = sb("scaled", [P, 2, D])
        hT = sb("hT", [P, KT, T])
        Q, K = sb("q", [P, 4, T]), sb("k", [P, 4, T])
        V = sb("v", [P, 2, 512])
        RP = sb("rec_padded", [P, 4, T + 3])
        Y = sb("conv", [P, 4, T])
        RG, IG = sb("r_gate", [P, 4, T]), sb("i_gate", [P, 4, T])
        MUL = XS[:].rearrange("p t (i c) -> p (t i) c", c=T)[:, 0:4]
        CAT = sb("mixed", [P, 8, T])
        CUM = sb("cum_decay", [8, T])
        FT = sb("f_tmp", [8, T])
        CT = sb("cum_decay_t", [P, 2, 8])
        CB = sb("cum_decay_rows", [P, 8, T])
        LG = sb("logits", [P, 2, T])
        PR, PTB = sb("probs", [P, 2, 2, T]), sb("probs_t", [P, 2, 2, T])
        small = sb("small", [P, 2, 8])
        st = sb("stats", [P, 8])
        lam = sb("lambda", [P, 16])
        block = ctx.enter_context(nc.Block())

        @block.tensor
        def _(pe):
            held = {}

            def slot(name, reader):
                if name not in held:
                    held[name] = W.slot(pe, f"x.{name}", reader).rearrange("p (k c) -> p k c", c=512)
                return held[name]

            pe.wait_ge(*sig.small_in.at(16))
            for kind, i in steps:
                if kind == "turnx":
                    if i == 0:
                        pe.wait_ge(*sig.scaled.at(2))
                    acc = PT.open(pe, J("turnx", i))
                    for n in range(4):
                        k, t = 2 * i + n // 2, n % 2
                        last = pe.transpose(acc[:, n * P:(n + 1) * P], XS[:, t, k * P:(k + 1) * P], ident)
                    last.then_inc(*PT.done())
                elif kind == "f":
                    pe.wait_ge(*PT.evacuated(J("turnx", 2)))
                    pe.wait_ge(*PT.evacuated(J("turnx", 3)))
                    acc = PT.open(pe, J("f"))
                    for k in range(KT):
                        last = pe.matmul(acc[0:8, 0:T], par[:, M_WF + 8 * k:M_WF + 8 * k + 8], hT[:, k, :],
                                         start=(k == 0), stop=(k == KT - 1))
                    last.then_inc(*PT.done())
                elif kind in ("rec", "q", "k", "gat"):
                    w = slot(kind, (PJ, J(kind, 3)))
                    acc = PJ.open(pe, J(kind, i))
                    for k in range(KT):
                        last = pe.matmul(acc[:, 0:T], w[:, k, i * P:(i + 1) * P], hT[:, k, :],
                                         start=(k == 0), stop=(k == KT - 1))
                    last.then_inc(*PJ.done())
                elif kind in ("v", "out"):
                    src = hT if kind == "v" else CAT
                    if kind == "out" and i == 0:
                        pe.wait_ge(*sig.lru_seq.at(1))
                        pe.wait_ge(*PJ.evacuated(J("pv", 6)))
                        pe.wait_ge(*PJ.evacuated(J("pv", 7)))
                    for h in range(1 if kind == "v" else 2):
                        name = "v" if kind == "v" else f"wo{h}"
                        last_job = J("v", 1) if kind == "v" else J("out", 1, h)
                        job = J("v", i) if kind == "v" else J("out", i, h)
                        w = slot(name, (PJ, last_job))
                        acc = PJ.open(pe, job)
                        for k in range(KT):
                            last = pe.matmul(acc[:, :], src[:, k, i * P:(i + 1) * P], w[:, k, :],
                                             start=(k == 0), stop=(k == KT - 1))
                        last.then_inc(*PJ.done())
                elif kind == "ri":
                    pe.wait_ge(*sig.conv.at(i + 1))
                    acc = PT.open(pe, J("ri", i))
                    for n, w in enumerate((M_WA, M_WX)):
                        last = pe.matmul(acc[:, n * T:(n + 1) * T], par[:, w + i * P:w + (i + 1) * P], Y[:, i, :],
                                         start=True, stop=True)
                    last.then_inc(*PT.done())
                elif kind == "cum":
                    pe.wait_ge(*sig.cum.at(1))
                    acc = PT.open(pe, J("ct"))
                    for t in range(2):
                        last = pe.matmul(acc[:, 8 * t:8 * t + 8], CUM[0:8, t * P:(t + 1) * P], ident[0:8, 0:8],
                                         start=True, stop=True)
                    last.then_inc(*PT.done())
                    for n in range(4):
                        acc = PT.open(pe, J("cb", n))
                        for h in (2 * n, 2 * n + 1):
                            last = pe.matmul(acc[:, (h % 2) * T:(h % 2 + 1) * T],
                                             par[0:8, M_SEL + h * P:M_SEL + (h + 1) * P], CUM[0:8, :],
                                             start=True, stop=True)
                        last.then_inc(*PT.done())
                elif kind == "score":
                    j, t = units[i]
                    n = P * (t + 1)
                    if i == 0:
                        pe.wait_ge(*PJ.evacuated(J("q", 3)))
                        pe.wait_ge(*PJ.evacuated(J("k", 3)))
                    for u in range(2):
                        acc = PS.open(pe, J("score", i, u))
                        pe.matmul(acc[:, 0:n], Q[64 * u:64 * u + 64, j, t * P:(t + 1) * P], K[64 * u:64 * u + 64, j, 0:n],
                                  start=True, stop=True).then_inc(*PS.done())
                elif kind == "turn":
                    for u in range(2):
                        pe.wait_ge(*sig.probs.at(2 * i + u + 1))
                        acc = PT.open(pe, J("turn", i, u))
                        for b in range(units[i][1] + 1):
                            last = pe.transpose(acc[:, b * P:(b + 1) * P], PR[:, i % 2, u, b * P:(b + 1) * P], ident)
                        last.then_inc(*PT.done())
                elif kind == "pv":
                    j, t = units[i]
                    if i == 0:
                        pe.wait_ge(*PJ.evacuated(J("v", 0)))
                        pe.wait_ge(*PJ.evacuated(J("v", 1)))
                    acc = PJ.open(pe, J("pv", i))
                    for u in range(2):
                        pe.wait_ge(*PT.evacuated(J("turn", i, u)))
                        c = (2 * j + u) * 64
                        for b in range(t + 1):
                            last = pe.matmul(acc[64 * u:64 * u + 64, 0:P], V[:, b, c:c + 64],
                                             PTB[:, i % 2, u, b * P:(b + 1) * P], start=(b == 0), stop=(b == t))
                    last.then_inc(*PJ.done())

        @block.scalar
        def _(act):
            link = linker(act, sig.act_own)
            act.wait_ge(*sig.small_in.at(16))
            x = par[:, M_LAM:M_LAM + 4]
            link(act.activation(lam[:, 0:4], x, ACT.Abs))
            link(act.activation(lam[:, 0:4], lam[:, 0:4], ACT.Exp, scale=-1.0))
            act.activation(lam[:, 0:4], lam[:, 0:4], ACT.Ln, bias=one).then_inc(*sig.lam.one())
            for kind, i in steps:
                if kind == "norm":
                    link(act.activation(XS[:, i, :], xlat[:, i, :], ACT.Square, accum_out=st[:, i:i + 1]))
                    link(act.activation(st[:, 2 + i:3 + i], st[:, i:i + 1], ACT.Ln, bias=eps, scale=1 / D))
                    act.activation(st[:, 4 + i:5 + i], st[:, 2 + i:3 + i], ACT.Exp, scale=-0.5)\
                        .then_inc(*sig.norm_rstd.one())
                elif kind == "f":
                    act.wait_ge(*PT.ready(J("f")))
                    link(act.activation(FT[:], PT.tile(J("f"))[0:8, 0:T], ACT.Abs, bias=par[0:8, M_BF:M_BF + 1]))
                    link(act.activation(FT[:], FT[:], ACT.Exp, scale=-1.0))
                    act.activation(FT[:], FT[:], ACT.Ln, bias=one[0:8]).then_inc(*sig.fsoft.one())
                elif kind in ("rec", "q", "k", "v"):
                    dst = {"rec": RP[:, i, 3:3 + T], "q": Q[:, i, :], "k": K[:, i, :], "v": V[:, i % 2, :]}[kind]
                    act.wait_ge(*PJ.ready(J(kind, i)))
                    act.activation(dst, PJ.tile(J(kind, i))[:, 0:512 if kind == "v" else T], ACT.Copy)\
                        .then_inc(*PJ.evac(J(kind, i)))
                elif kind == "ri":
                    act.wait_ge(*PT.ready(J("ri", i)))
                    acc = PT.tile(J("ri", i))
                    act.activation(RG[:, i, :], acc[:, 0:T], ACT.Sigmoid, bias=par[:, M_BA + i:M_BA + i + 1])
                    act.activation(IG[:, i, :], acc[:, T:2 * T], ACT.Sigmoid, bias=par[:, M_BX + i:M_BX + i + 1])\
                        .then_inc(*PT.evac(J("ri", i)))
                elif kind == "lru":
                    act.wait_ge(*PT.evacuated(J("ri", 3)))
                    act.wait_ge(*sig.lam.at(2))
                    for n in range(4):
                        act.activation(MUL[:, n, :], RG[:, n, :], ACT.Tanh, scale=lam[:, 8 + n:9 + n])
                        last = act.activation(RG[:, n, :], RG[:, n, :], ACT.Exp, scale=lam[:, 4 + n:5 + n])
                    last.then_inc(*sig.gates_ri.one())
                    act.wait_ge(*sig.lru_mult.at(1))
                    act.activation(MUL[:], MUL[:], ACT.Sqrt).then_inc(*sig.gates_ri.one())
                elif kind == "gat":
                    act.wait_ge(*PJ.ready(J("gat", i)))
                    act.activation(CAT[:, 4 + i, :], PJ.tile(J("gat", i))[:, 0:T], ACT.Gelu_apprx_tanh)\
                        .then_inc(*PJ.evac(J("gat", i)))
                elif kind == "score":
                    n = P * (units[i][1] + 1)
                    for u in range(2):
                        act.wait_ge(*sig.neg_max.at(2 * i + u + 1))
                        act.activation(PR[:, i % 2, u, 0:n], LG[:, u, 0:n], ACT.Exp, bias=small[:, i % 2, 2 + u:3 + u],
                                       accum_out=small[:, i % 2, 4 + u:5 + u]).then_inc(*sig.route_exp.one())
                elif kind == "turn":
                    n = P * (units[i][1] + 1)
                    for u in range(2):
                        act.wait_ge(*PT.ready(J("turn", i, u)))
                        if i >= 2:
                            act.wait_ge(*PJ.ready(J("pv", i - 2)))
                        act.activation(PTB[:, i % 2, u, 0:n], PT.tile(J("turn", i, u))[:, 0:n], ACT.Copy)\
                            .then_inc(*PT.evac(J("turn", i, u)))

        @block.vector
        def _(dve):
            link = linker(dve, sig.dve_own)
            dve.wait_ge(*sig.small_in.at(16))
            dve.memset(RP[:, :, 0:3], 0.0)
            dve.wait_ge(*sig.lam.at(1))
            link(dve.tensor_scalar(lam[:, 12:16], par[:, M_LAM:M_LAM + 4], -1.0, 0.0, ALU.mult, ALU.max))
            link(dve.tensor_tensor(lam[:, 12:16], lam[:, 12:16], lam[:, 0:4], ALU.add))
            dve.tensor_scalar(lam[:, 4:8], lam[:, 12:16], -8.0, None, ALU.mult)
            dve.tensor_scalar(lam[:, 8:12], lam[:, 12:16], 8.0, None, ALU.mult).then_inc(*sig.lam.one())
            for kind, i in steps:
                if kind == "norm":
                    dve.wait_ge(*sig.norm_rstd.at(i + 1))
                    dve.tensor_scalar(XS[:, i, :], xlat[:, i, :], st[:, 4 + i:5 + i], None, ALU.mult)\
                        .then_inc(*sig.scaled.one())
                elif kind == "turnx":
                    dve.wait_ge(*PT.ready(J("turnx", i)))
                    g = par[:, M_NORM1 + 2 * i:M_NORM1 + 2 * i + 2].unsqueeze(2).to_broadcast([P, 2, T])
                    acc = PT.tile(J("turnx", i))[:, :].rearrange("p (k t) -> p k t", k=2)
                    dve.tensor_tensor(hT[:, 2 * i:2 * i + 2, :], acc, g, ALU.mult).then_inc(*PT.evac(J("turnx", i)))
                elif kind == "f":
                    dve.wait_ge(*sig.fsoft.at(1))
                    dve.tensor_scalar(CUM[:], PT.tile(J("f"))[0:8, 0:T], par[0:8, M_BF:M_BF + 1], 0.0,
                                      ALU.add, ALU.min).then_inc(*PT.evac(J("f")))
                    dve.wait_ge(*PT.evacuated(J("f")))
                    link(dve.tensor_tensor(CUM[:], CUM[:], FT[:], ALU.subtract))
                    dve.tensor_tensor_scan(CUM[:], one[0:8].to_broadcast([8, T]), CUM[:], 0.0, ALU.mult, ALU.add)\
                        .then_inc(*sig.cum.one())
                elif kind == "rec":
                    dve.wait_ge(*PJ.evacuated(J("rec", i)))
                    w = lambda n: par[:, M_CONVW + 4 * i + n:M_CONVW + 4 * i + n + 1]
                    link(dve.tensor_scalar(Y[:, i, :], RP[:, i, 0:T], w(0), par[:, M_CONVB + i:M_CONVB + i + 1],
                                           ALU.mult, ALU.add))
                    for n in range(1, 4):
                        ins = dve.scalar_tensor_tensor(Y[:, i, :], RP[:, i, n:n + T], w(n), Y[:, i, :], ALU.mult, ALU.add)
                        if n < 3:
                            link(ins)
                    ins.then_inc(*sig.conv.one())
                elif kind == "cum":
                    dve.wait_ge(*PT.ready(J("ct")))
                    dve.tensor_copy(CT[:], PT.tile(J("ct"))[:, 0:16].rearrange("p (t h) -> p t h", t=2))\
                        .then_inc(*PT.evac(J("ct")))
                    for n in range(4):
                        dve.wait_ge(*PT.ready(J("cb", n)))
                        dve.tensor_copy(CB[:, 2 * n:2 * n + 2, :],
                                        PT.tile(J("cb", n))[:, :].rearrange("p (h t) -> p h t", h=2))\
                            .then_inc(*PT.evac(J("cb", n)))
                elif kind == "lru":
                    dve.wait_ge(*sig.gates_ri.at(1))
                    link(dve.tensor_tensor(CAT[:, 0:4, :], RG[:], RG[:], ALU.mult))
                    link(dve.scalar_tensor_tensor(MUL[:], CAT[:, 0:4, :], 1.0, MUL[:], ALU.add, ALU.mult))
                    dve.tensor_tensor(IG[:], IG[:], Y[:], ALU.mult).then_inc(*sig.lru_mult.one())
                    dve.wait_ge(*sig.lru_mult.at(1))
                    dve.wait_ge(*sig.gates_ri.at(2))
                    link(dve.tensor_tensor(IG[:], IG[:], MUL[:], ALU.mult))
                    for n in range(4):
                        last = dve.tensor_tensor_scan(Y[:, n, :], RG[:, n, :], IG[:, n, :], 0.0, ALU.mult, ALU.add)
                    link(last)
                elif kind == "gat":
                    if i == 3:
                        dve.wait_ge(*PJ.evacuated(J("gat", 3)))
                        dve.tensor_tensor(CAT[:, 4:8, :], CAT[:, 4:8, :], Y[:], ALU.mult).then_inc(*sig.lru_seq.one())
                elif kind == "score":
                    j, t = units[i]
                    n = P * (t + 1)
                    for u in range(2):
                        h = 2 * j + u
                        lg = LG[:, u, 0:n]
                        if i:
                            dve.wait_ge(*sig.route_exp.at(2 * (i - 1) + u + 1))
                        link(dve.tensor_scalar(lg, CB[:, h, 0:n], CT[:, t, h:h + 1], -1.0, ALU.subtract, ALU.mult))
                        diag = LG[:, u, n - P:n]
                        link(dve.tensor_tensor(diag, diag, par[:, M_CAUSAL:M_CAUSAL + P], ALU.add))
                        dve.wait_ge(*PS.ready(J("score", i, u)))
                        dve.scalar_tensor_tensor(lg, PS.tile(J("score", i, u))[:, 0:n], 0.125, lg, ALU.mult, ALU.add)\
                            .then_inc(*PS.evac(J("score", i, u)))
                        dve.wait_ge(*PS.evacuated(J("score", i, u)))
                        link(dve.reduce_max(small[:, i % 2, u:u + 1], lg, AX.X))
                        dve.tensor_scalar(small[:, i % 2, 2 + u:3 + u], small[:, i % 2, u:u + 1], -1.0, None,
                                          ALU.mult).then_inc(*sig.neg_max.one())
                elif kind == "turn":
                    n = P * (units[i][1] + 1)
                    for u in range(2):
                        dve.wait_ge(*sig.route_exp.at(2 * i + u + 1))
                        link(dve.reciprocal(small[:, i % 2, 6 + u:7 + u], small[:, i % 2, 4 + u:5 + u]))
                        dve.tensor_scalar(PR[:, i % 2, u, 0:n], PR[:, i % 2, u, 0:n], small[:, i % 2, 6 + u:7 + u],
                                          None, ALU.mult).then_inc(*sig.probs.one())
                elif kind == "pv":
                    j, t = units[i]
                    dve.wait_ge(*PJ.ready(J("pv", i)))
                    dve.tensor_copy(CAT[:, j, t * P:(t + 1) * P], PJ.tile(J("pv", i))[:, 0:P])\
                        .then_inc(*PJ.evac(J("pv", i)))
                elif kind == "out":
                    for h in range(2):
                        dve.wait_ge(*PJ.ready(J("out", i, h)))
                        x = xlat[:, i, h * 512:(h + 1) * 512]
                        dve.tensor_tensor(x, x, PJ.tile(J("out", i, h))[:, :], ALU.add).then_inc(*PJ.evac(J("out", i, h)))

        @block.sync
        def _(sp):
            sp.dma_start(par[:], io["mixer_params"]).then_inc(*sig.small_in.dma())
            W.issue(sp, len(STREAM))
            EW.issue(sp, 2)



class ExpertWeights:

    def __init__(self, ctx, nc, dram, ring):
        self.dram = dram
        own = ctx.enter_context(nc.sbuf_tensor("expert_slots", [P, 2, ESLOT], F32))
        flat = ring[:].rearrange("p s c -> p (s c)")
        self.place = [own[:, 0], own[:, 1], flat[:, 0:ESLOT], flat[:, ESLOT:2 * ESLOT]]
        self.landed = [ctx.enter_context(nc.semaphore(f"expert_slot{i}_landed")) for i in range(NESLOT)]
        self.used = ctx.enter_context(nc.semaphore("expert_slots_used"))
        self.issued = 0

    def issue(self, sp, upto, source=None):
        for i in range(self.issued, upto):
            if i >= NESLOT:
                sp.wait_ge(self.used, i - NESLOT + 1)
            src = self.dram[i] if source is None else source(i)
            sp.dma_start(self.place[i % NESLOT], src).then_inc(self.landed[i % NESLOT], 16)
        self.issued = upto

    def slot(self, pe, i):
        pe.wait_ge(self.landed[i % NESLOT], 16 * (i // NESLOT + 1))
        w = self.place[i % NESLOT]
        return (w[:, 0:KT * 2 * FF].rearrange("p (k c) -> p k c", c=2 * FF),
                w[:, KT * 2 * FF:ESLOT].rearrange("p (k c) -> p k c", c=D))


def experts(nc, io, out, EW, jobs, sig, xlat, store):
    T = M_TOK
    PJ, PS, PT = jobs
    J = lambda name, *i: f"e.{name}" + "".join(f".{x}" for x in i)
    NP = G + 1

    with ExitStack() as ctx:
        def sb(name, shape, dt=F32):
            return ctx.enter_context(nc.sbuf_tensor(f"e_{name}", shape, dt))

        par = sb("params", [P, M_W])
        ident = par[:, M_ID:M_ID + P]
        eps = par[:, M_EPS:M_EPS + 1]
        fin = sb("final_norm", [P, D])
        XS = sb("scaled", [P, 2, D])
        hT = sb("hT", [P, KT, T])
        L = sb("logits", [P, 2, 36])
        GP, G1, G2, OH = (sb(n, [P, 2, G]) for n in ("group_p", "group_eq", "group_t", "group_one_hot"))
        MX = sb("maxima", [P, 2, 16])
        PROD = sb("inner_products", [P, 2, G, E])
        IL, IP, I1, I2, O1, O2 = (sb(n, [P, 2, E]) for n in ("inner_logits", "inner_p", "eq", "t", "first", "second"))
        COMB = sb("combine", [P, 2, NP, E])
        RK = sb("rank", [P, 2, NP])
        OV = sb("over", [P, G])
        FLAG = sb("flag", [P, 4])
        FLAGI = sb("flag_int", [P, 2], I32)
        SELT = sb("select_t", [P, NP, 2, P])
        SEL = sb("select", [P, NP, 2, P])
        CS = sb("slot_combine", [P, NP, E])
        XG = sb("gathered", [P, 2, KT, P])
        HS, HG, HT = sb("silu", [P, 2, FF]), sb("hidden", [P, 2, FF]), sb("hidden_t", [P, 2, 2, P])
        YB = sb("y_slots", [P, D])
        st = sb("stats", [P, 8])

        def work(first, count):
            s = []
            for n in range(first, first + count + 1):
                if n < first + count:
                    s += ([("gather", n // E)] if n % E == 0 else []) + [("gu", n)]
                if n > first:
                    s += [("down", n - 1)] + ([("scatter", (n - 1) // E)] if n % E == 0 else [])
            return s

        main_work = [("norm", 0), ("norm", 1)] + [("turnx", i) for i in range(4)]
        main_work += [("route", 0), ("route", 1), ("rank", 0)] + work(0, G * E)
        over_work = work(G * E, E)

        block = ctx.enter_context(nc.Block())

        def tensor_steps(pe, steps):
            for kind, i in steps:
                if kind == "turnx":
                    if i == 0:
                        pe.wait_ge(*sig.scaled.at(2))
                    acc = PT.open(pe, J("turnx", i))
                    for n in range(4):
                        k, t = 2 * i + n // 2, n % 2
                        last = pe.transpose(acc[:, n * P:(n + 1) * P], XS[:, t, k * P:(k + 1) * P], ident)
                    last.then_inc(*PT.done())
                elif kind == "route":
                    if i == 0:
                        pe.wait_ge(*PT.evacuated(J("turnx", 2)))
                        pe.wait_ge(*PT.evacuated(J("turnx", 3)))
                    acc = PT.open(pe, J("route", i))
                    for k in range(KT):
                        last = pe.matmul(acc[:, 0:36], hT[:, k, i * P:(i + 1) * P], par[:, M_WR + 36 * k:M_WR + 36 * (k + 1)],
                                         start=(k == 0), stop=(k == KT - 1))
                    last.then_inc(*PT.done())
                elif kind == "rank":
                    pe.wait_ge(*sig.one_hot.at(1))
                    acc = PT.open(pe, J("rank"))
                    tri, ones = par[:, M_TRI:M_TRI + P], par[:, M_ONES:M_ONES + P]
                    pe.matmul(acc[:, 0:4], tri, OH[:, 0, :], start=True, stop=True)
                    pe.matmul(acc[:, 4:8], tri, OH[:, 1, :], start=True, stop=False)
                    pe.matmul(acc[:, 4:8], ones, OH[:, 0, :], start=False, stop=True)
                    pe.matmul(acc[:, 8:12], ones, OH[:, 0, :], start=True, stop=False)
                    pe.matmul(acc[:, 8:12], ones, OH[:, 1, :], start=False, stop=True).then_inc(*PT.done())
                    pe.wait_ge(*sig.selected.at(1))
                    acc = PT.open(pe, J("slotw"))
                    for n in range(NP):
                        for t in range(2):
                            last = pe.matmul(acc[:, n * E:(n + 1) * E], SELT[:, n, t, :], COMB[:, t, n, :],
                                             start=(t == 0), stop=(t == 1))
                    last.then_inc(*PT.done())
                    for b in range(3):
                        acc = PT.open(pe, J("sel", b))
                        for n in range(4 * b, min(4 * b + 4, 2 * NP)):
                            last = pe.transpose(acc[:, (n % 4) * P:(n % 4 + 1) * P], SELT[:, n // 2, n % 2, :], ident)
                        last.then_inc(*PT.done())
                elif kind == "gather":
                    for b in range(2):
                        acc = PT.open(pe, J("gather", i, b))
                        for n in range(4):
                            k = 4 * b + n
                            for t in range(2):
                                last = pe.matmul(acc[:, n * P:(n + 1) * P], XS[:, t, k * P:(k + 1) * P], SELT[:, i, t, :],
                                                 start=(t == 0), stop=(t == 1))
                        last.then_inc(*PT.done())
                elif kind == "gu":
                    p = i // E
                    if i % E == 0:
                        pe.wait_ge(*PT.evacuated(J("gather", p, 0)))
                        pe.wait_ge(*PT.evacuated(J("gather", p, 1)))
                    w, _ = EW.slot(pe, i)
                    acc = PJ.open(pe, J("gu", i))
                    for k in range(KT):
                        last = pe.matmul(acc[:, :], XG[:, p % 2, k, :], w[:, k, :], start=(k == 0), stop=(k == KT - 1))
                    last.then_inc(*PJ.done())
                elif kind == "down":
                    p, e = i // E, i % E
                    pe.wait_ge(*PJ.evacuated(J("gu", i)))
                    acc = PT.open(pe, J("turnh", i))
                    for f in range(2):
                        last = pe.transpose(acc[:, f * P:(f + 1) * P], HG[:, i % 2, f * P:(f + 1) * P], ident)
                    last.then_inc(*PT.done())
                    if e == 0:
                        for h in range(2):
                            PS.open(pe, J("y", p, h))
                    pe.wait_ge(*PT.evacuated(J("turnh", i)))
                    _, w = EW.slot(pe, i)
                    for h in range(2):
                        y = PS.tile(J("y", p, h))
                        for f in range(2):
                            last = pe.matmul(y[:, :], HT[:, i % 2, f, :], w[:, f, h * 512:(h + 1) * 512],
                                             start=(e == 0 and f == 0), stop=(e == E - 1 and f == 1))
                    last.then_inc(EW.used, 1)
                elif kind == "scatter":
                    pe.wait_ge(*sig.slots_w.at(i + 1))
                    for t in range(2):
                        for h in range(2):
                            acc = PT.open(pe, J("scatter", i, t, h))
                            pe.matmul(acc[:, :], SEL[:, i, t, :], YB[:, h * 512:(h + 1) * 512],
                                      start=True, stop=True).then_inc(*PT.done())

        def scalar_steps(act, steps):
            link = linker(act, sig.act_own)
            for kind, i in steps:
                if kind == "norm":
                    link(act.activation(XS[:, i, :], xlat[:, i, :], ACT.Square, accum_out=st[:, i:i + 1]))
                    link(act.activation(st[:, 2 + i:3 + i], st[:, i:i + 1], ACT.Ln, bias=eps, scale=1 / D))
                    act.activation(st[:, 4 + i:5 + i], st[:, 2 + i:3 + i], ACT.Exp, scale=-0.5)\
                        .then_inc(*sig.norm_rstd.one())
                elif kind == "route":
                    act.wait_ge(*sig.route_max.at(i + 1))
                    act.activation(GP[:, i, :], L[:, i, 0:G], ACT.Exp, bias=MX[:, i, 0:1], accum_out=MX[:, i, 1:2])\
                        .then_inc(*sig.route_exp.one())
                elif kind == "rank":
                    act.wait_ge(*sig.inner_max.at(1))
                    for t in range(2):
                        last = act.activation(IP[:, t, :], IL[:, t, :], ACT.Exp, bias=MX[:, t, 2:3], accum_out=MX[:, t, 3:4])
                    last.then_inc(*sig.inner_exp.one())
                elif kind == "gu":
                    act.wait_ge(*PJ.ready(J("gu", i)))
                    if i >= 2:
                        act.wait_ge(*PJ.evacuated(J("gu", i - 2)))
                    act.activation(HS[:, i % 2, :], PJ.tile(J("gu", i))[:, 0:FF], ACT.Silu).then_inc(*sig.silu_g.one())
                elif kind == "down":
                    act.wait_ge(*PT.ready(J("turnh", i)))
                    if i >= 2:
                        act.wait_ge(EW.used, i - 1)
                    act.activation(HT[:, i % 2, :, :], PT.tile(J("turnh", i))[:, 0:2 * P].rearrange("p (f s) -> p f s", f=2),
                                   ACT.Copy).then_inc(*PT.evac(J("turnh", i)))

        def first_max(dve, link, p, eq, t, out, top, top_col, n):
            m = top[:, :, top_col:top_col + 1]
            link(dve.tensor_reduce(m, p, AX.X, ALU.max))
            link(dve.tensor_tensor(eq, p, m.to_broadcast([P, 2, n]), ALU.is_equal))
            idx = par[:, M_GI:M_GI + n].unsqueeze(1).to_broadcast([P, 2, n])
            link(dve.scalar_tensor_tensor(t, eq, -100.0, idx, ALU.mult, ALU.add))
            link(dve.tensor_reduce(top[:, :, 15:16], t, AX.X, ALU.min))
            return dve.tensor_tensor(out, t, top[:, :, 15:16].to_broadcast([P, 2, n]), ALU.is_equal)

        def vector_steps(dve, steps):
            link = linker(dve, sig.dve_own)
            for kind, i in steps:
                if kind == "norm":
                    dve.wait_ge(*sig.norm_rstd.at(i + 1))
                    dve.tensor_scalar(XS[:, i, :], xlat[:, i, :], st[:, 4 + i:5 + i], None, ALU.mult)\
                        .then_inc(*sig.scaled.one())
                elif kind == "turnx":
                    dve.wait_ge(*PT.ready(J("turnx", i)))
                    g = par[:, M_NORM2 + 2 * i:M_NORM2 + 2 * i + 2].unsqueeze(2).to_broadcast([P, 2, T])
                    acc = PT.tile(J("turnx", i))[:, :].rearrange("p (k t) -> p k t", k=2)
                    dve.tensor_tensor(hT[:, 2 * i:2 * i + 2, :], acc, g, ALU.mult).then_inc(*PT.evac(J("turnx", i)))
                elif kind == "route":
                    dve.wait_ge(*PT.ready(J("route", i)))
                    dve.tensor_tensor(L[:, i, :], PT.tile(J("route", i))[:, 0:36], par[:, M_BR:M_BR + 36], ALU.add)\
                        .then_inc(*PT.evac(J("route", i)))
                    dve.wait_ge(*PT.evacuated(J("route", i)))
                    link(dve.reduce_max(MX[:, i, 0:1], L[:, i, 0:G], AX.X))
                    dve.tensor_scalar(MX[:, i, 0:1], MX[:, i, 0:1], -1.0, None, ALU.mult).then_inc(*sig.route_max.one())
                elif kind == "rank":
                    dve.wait_ge(*sig.route_exp.at(2))
                    link(dve.reciprocal(MX[:, :, 4:5], MX[:, :, 1:2]))
                    link(dve.tensor_tensor(GP[:], GP[:], MX[:, :, 4:5].to_broadcast([P, 2, G]), ALU.mult))
                    first_max(dve, link, GP[:], G1[:], G2[:], OH[:], MX, 5, G).then_inc(*sig.one_hot.one())
                    dve.wait_ge(*sig.one_hot.at(1))
                    for t in range(2):
                        last = dve.tensor_tensor(PROD[:, t], L[:, t, G:36].rearrange("p (g e) -> p g e", g=G),
                                                 OH[:, t, :].unsqueeze(2).to_broadcast([P, G, E]), ALU.mult)
                    link(last)
                    for t in range(2):
                        last = dve.tensor_reduce(IL[:, t, :], PROD[:, t].rearrange("p g e -> p e g"), AX.X, ALU.add)
                    link(last)
                    link(dve.tensor_reduce(MX[:, :, 6:7], IL[:], AX.X, ALU.max))
                    dve.tensor_scalar(MX[:, :, 2:3], MX[:, :, 6:7], -1.0, None, ALU.mult).then_inc(*sig.inner_max.one())
                    dve.wait_ge(*sig.inner_exp.at(1))
                    link(dve.reciprocal(MX[:, :, 7:8], MX[:, :, 3:4]))
                    link(dve.tensor_tensor(IP[:], IP[:], MX[:, :, 7:8].to_broadcast([P, 2, E]), ALU.mult))
                    link(first_max(dve, link, IP[:], I1[:], I2[:], O1[:], MX, 8, E))
                    link(dve.scalar_tensor_tensor(I1[:], O1[:], -2.0, IP[:], ALU.mult, ALU.add))
                    link(first_max(dve, link, I1[:], IP[:], I2[:], O2[:], MX, 9, E))
                    link(dve.tensor_tensor(MX[:, :, 10:11], MX[:, :, 8:9], MX[:, :, 9:10], ALU.add))
                    link(dve.reciprocal(MX[:, :, 11:12], MX[:, :, 10:11]))
                    link(dve.tensor_tensor(MX[:, :, 8:10], MX[:, :, 8:10], MX[:, :, 11:12].to_broadcast([P, 2, 2]), ALU.mult))
                    link(dve.tensor_tensor(O1[:], O1[:], MX[:, :, 8:9].to_broadcast([P, 2, E]), ALU.mult))
                    link(dve.tensor_tensor(O2[:], O2[:], MX[:, :, 9:10].to_broadcast([P, 2, E]), ALU.mult))
                    link(dve.tensor_tensor(O1[:], O1[:], O2[:], ALU.add))
                    link(dve.tensor_tensor(O1[:], O1[:], MX[:, :, 5:6].to_broadcast([P, 2, E]), ALU.mult))
                    for t in range(2):
                        last = dve.tensor_tensor(COMB[:, t, 0:G, :], O1[:, t, :].unsqueeze(1).to_broadcast([P, G, E]),
                                                 OH[:, t, :].unsqueeze(2).to_broadcast([P, G, E]), ALU.mult)
                    link(last)
                    dve.wait_ge(*PT.ready(J("rank")))
                    rank = PT.tile(J("rank"))[:, 0:8].rearrange("p (t g) -> p t g", t=2)
                    link(dve.scalar_tensor_tensor(RK[:, :, 0:G], rank, 1.0, OH[:], ALU.add, ALU.mult))
                    dve.tensor_scalar(OV[:], PT.tile(J("rank"))[:, 8:12], float(P), None, ALU.is_gt)\
                        .then_inc(*PT.evac(J("rank")))
                    dve.wait_ge(*PT.evacuated(J("rank")))
                    over = OV[:].unsqueeze(1).to_broadcast([P, 2, G])
                    link(dve.tensor_tensor(G2[:], RK[:, :, 0:G], over, ALU.mult))
                    link(dve.tensor_reduce(RK[:, :, G:G + 1], G2[:], AX.X, ALU.add))
                    link(dve.tensor_scalar(RK[:, :, 0:G], RK[:, :, 0:G], 1.0, None, ALU.subtract))
                    link(dve.tensor_scalar(RK[:, :, G:G + 1], RK[:, :, G:G + 1], float(P + 1), None, ALU.subtract))
                    for t in range(2):
                        link(dve.tensor_tensor(PROD[:, t], COMB[:, t, 0:G, :], OV[:].unsqueeze(2).to_broadcast([P, G, E]), ALU.mult))
                        last = dve.tensor_reduce(COMB[:, t, G, :], PROD[:, t].rearrange("p g e -> p e g"), AX.X, ALU.add)
                    link(last)
                    dve.tensor_reduce(FLAG[:, 0:1], OV[:], AX.X, ALU.max)
                    link(dve.tensor_tensor(MX[:, 0, 0:G], OV[:], par[:, M_GI:M_GI + G], ALU.mult))
                    link(dve.tensor_reduce(FLAG[:, 1:2], MX[:, 0, 0:G], AX.X, ALU.add))
                    dve.tensor_copy(FLAGI[:], FLAG[:, 0:2]).then_inc(*sig.over_flag.one())
                    for n in range(NP):
                        for t in range(2):
                            last = dve.tensor_scalar(SELT[:, n, t, :], par[:, M_IOTA:M_IOTA + P], RK[:, t, n:n + 1], None,
                                                     ALU.is_equal)
                    last.then_inc(*sig.selected.one())
                    dve.wait_ge(*PT.ready(J("slotw")))
                    dve.tensor_copy(CS[:], PT.tile(J("slotw"))[:, 0:NP * E].rearrange("p (n e) -> p n e", e=E))\
                        .then_inc(*PT.evac(J("slotw")))
                    flat = SEL[:].rearrange("p n t c -> p (n t c)")
                    for b in range(3):
                        dve.wait_ge(*PT.ready(J("sel", b)))
                        n = min(512, NP * 2 * P - 512 * b)
                        dve.tensor_copy(flat[:, 512 * b:512 * b + n], PT.tile(J("sel", b))[:, 0:n])\
                            .then_inc(*PT.evac(J("sel", b)))
                elif kind == "gather":
                    for b in range(2):
                        dve.wait_ge(*PT.ready(J("gather", i, b)))
                        g = par[:, M_NORM2 + 4 * b:M_NORM2 + 4 * b + 4].unsqueeze(2).to_broadcast([P, 4, P])
                        acc = PT.tile(J("gather", i, b))[:, :].rearrange("p (k s) -> p k s", k=4)
                        dve.tensor_tensor(XG[:, i % 2, 4 * b:4 * b + 4, :], acc, g, ALU.mult)\
                            .then_inc(*PT.evac(J("gather", i, b)))
                elif kind == "gu":
                    dve.wait_ge(*sig.silu_g.at(i + 1))
                    if i >= 2:
                        dve.wait_ge(*PT.ready(J("turnh", i - 2)))
                    dve.scalar_tensor_tensor(HG[:, i % 2, :], PJ.tile(J("gu", i))[:, FF:2 * FF],
                                             CS[:, i // E, i % E:i % E + 1], HS[:, i % 2, :], ALU.mult, ALU.mult)\
                        .then_inc(*PJ.evac(J("gu", i)))
                elif kind == "scatter":
                    dve.wait_ge(EW.used, E * (i + 1))
                    if i:
                        dve.wait_ge(*PT.ready(J("scatter", i - 1, 1, 1)))
                    for h in range(2):
                        last = dve.tensor_copy(YB[:, h * 512:(h + 1) * 512], PS.tile(J("y", i, h))[:, :])
                        last.then_inc(*PS.evac(J("y", i, h)))
                    dve.wait_ge(*PS.evacuated(J("y", i, 0)))
                    dve.wait_ge(*PS.evacuated(J("y", i, 1)))
                    dve.engine_nop().then_inc(*sig.slots_w.one())
                    for t in range(2):
                        for h in range(2):
                            dve.wait_ge(*PT.ready(J("scatter", i, t, h)))
                            x = xlat[:, t, h * 512:(h + 1) * 512]
                            dve.tensor_tensor(x, x, PT.tile(J("scatter", i, t, h))[:, :], ALU.add)\
                                .then_inc(*PT.evac(J("scatter", i, t, h)))

        @block.tensor
        def _(pe):
            pe.wait_ge(*sig.small_in.at(32))
            tensor_steps(pe, main_work)
            pe.wait_ge(*sig.over_flag.at(1))
            with pe.register("pe_over") as r:
                pe.reg_load(r, FLAGI[0:1, 0:1])
                with pe.If_ne(r, 0):
                    tensor_steps(pe, over_work)

        @block.scalar
        def _(act):
            link = linker(act, sig.act_own)
            act.wait_ge(*sig.small_in.at(32))
            scalar_steps(act, main_work)
            act.wait_ge(*sig.over_flag.at(1))
            with act.register("act_over") as r:
                act.reg_load(r, FLAGI[0:1, 0:1])
                with act.If_ne(r, 0):
                    scalar_steps(act, over_work)
            act.wait_ge(*sig.x_done.at(1))
            for t in range(2):
                link(act.activation(XS[:, t, :], xlat[:, t, :], ACT.Square, accum_out=st[:, t:t + 1]))
                link(act.activation(st[:, 2 + t:3 + t], st[:, t:t + 1], ACT.Ln, bias=eps, scale=1 / D))
                act.activation(st[:, 6 + t:7 + t], st[:, 2 + t:3 + t], ACT.Exp, scale=-0.5).then_inc(*sig.norm_rstd.one())

        @block.vector
        def _(dve):
            link = linker(dve, sig.dve_own)
            dve.wait_ge(*sig.small_in.at(32))
            vector_steps(dve, main_work)
            with dve.register("dve_over") as r:
                dve.wait_ge(*sig.over_flag.at(1))
                dve.reg_load(r, FLAGI[0:1, 0:1])
                with dve.If_ne(r, 0):
                    vector_steps(dve, over_work)
            dve.engine_nop().then_inc(*sig.x_done.one())
            for t in range(2):
                dve.wait_ge(*sig.norm_rstd.at(2 + t + 1))
                dve.scalar_tensor_tensor(xlat[:, t, :], xlat[:, t, :], st[:, 6 + t:7 + t], fin[:], ALU.mult, ALU.mult)\
                    .then_inc(*sig.norm_out.one())

        @block.sync
        def _(sp):
            sp.dma_start(par[:], io["mixer_params"]).then_inc(*sig.small_in.dma())
            sp.dma_start(fin[:], io["final_norm"].partition_broadcast(P)).then_inc(*sig.small_in.dma())
            EW.issue(sp, G * E)
            sp.wait_ge(*sig.over_flag.at(1))
            with sp.register("sp_over") as r, sp.register("sp_group") as g:
                sp.reg_load(r, FLAGI[0:1, 0:1])
                sp.reg_load(g, FLAGI[0:1, 1:2])
                with sp.If_ne(r, 0):
                    group = sp.snap(g)
                    w = io["experts"].rearrange("(g e) p c -> g e p c", g=G)
                    EW.issue(sp, (G + 1) * E, lambda n: w[bass.ds(group, 1), n % E].rearrange("a p c -> (a p) c"))
            for t in range(2):
                sp.wait_ge(*sig.norm_out.at(t + 1))
                sp.dma_start(out[t * P:(t + 1) * P, :], xlat[:, t, :]).then_inc(*store.dma())
            sp.wait_ge(*store.now())



def build(nc, io, out):
    with ExitStack() as ctx:
        sig = Signals(ctx, nc)
        jobs = tuple(Banks(ctx, nc, n, k) for n, k in (("proj", 4), ("score", 2), ("turn", 2)))
        W = Weights(ctx, nc, io["stream"])
        xlat = ctx.enter_context(nc.sbuf_tensor("x_latent", [P, 2, D], F32))
        store = Signal(ctx, nc, "stored")
        with ExitStack() as trunk:
            def sb(name, shape):
                return trunk.enter_context(nc.sbuf_tensor(name, shape, F32))

            consts = sb("consts", [P, C_W])
            silu_c = sb("silu_c", [P, KT, 2])
            hT = sb("hT", [P, KT, TOK])
            gla_v = sb("gla_v", [P, 4, 512])
            for l in range(DEPTH):
                trunk_layer(nc, l, io, W, jobs, sig, consts, silu_c, xlat, gla_v, hT)
                sig.seal()
        EW = ExpertWeights(ctx, nc, io["experts"], W.ring)
        mixer(nc, io, W, EW, jobs, sig, xlat)
        sig.seal()
        experts(nc, io, out, EW, jobs, sig, xlat, store)



def trunk_constants():
    c = np.zeros((P, C_W), np.float32)
    r = np.arange(P)
    c[:, C_ID:C_ID + P] = np.eye(P)
    c[:, C_ONES:C_ONES + P] = 1 / 128
    c[:, C_BONES:C_BONES + P] = (r[:, None] // 64 == r[None, :] // 64) / 64
    rot = np.zeros((P, P), np.float32)
    for m in range(P):
        if m % 32 < 16:
            rot[m + 16, m] = -1
        else:
            rot[m - 16, m] = 1
    c[:, C_ROT:C_ROT + P] = rot
    tok = np.arange(256)
    freqs = (np.float32(10000.0) ** (-np.arange(0, 32, 2, dtype=np.float32) / np.float32(32))).astype(np.float32)
    pos = np.where((r[:, None] % 64) < 32, (tok // 64)[None, :], (tok % 64)[None, :]).astype(np.float32)
    ang = (pos * freqs[r % 16][:, None]).astype(np.float32)
    c[:, C_COS:C_COS + 256] = np.cos(ang.astype(np.float64))
    c[:, C_SIN:C_SIN + 256] = np.sin(ang.astype(np.float64))
    for i, h in enumerate(LEVELS):
        same = r[:, None] // (2 * h) == r[None, :] // (2 * h)
        c[:, C_MASK + i * P:C_MASK + (i + 1) * P] = same & (r[:, None] // h != r[None, :] // h)
    c[:, C_EPS] = EPS
    c[:, C_ONE] = 1
    return c


def tiles(w):
    k, n = w.shape
    return w.reshape(k // P, P, n).transpose(1, 0, 2).reshape(P, -1)


def mixer_params(i):
    c = np.zeros((P, M_W), np.float32)
    r = np.arange(P)
    c[:, M_ID:M_ID + P] = np.eye(P)
    c[:, M_TRI:M_TRI + P] = r[:, None] < r[None, :]
    c[:, M_ONES:M_ONES + P] = 1
    c[:, M_IOTA:M_IOTA + P] = r
    c[:, M_CAUSAL:M_CAUSAL + P] = np.where(r[None, :] <= r[:, None], 0, -1e30)
    for h in range(8):
        c[h, M_SEL + h * P:M_SEL + (h + 1) * P] = 1
    c[:, M_EPS], c[:, M_ONE] = EPS, 1
    c[:, M_GI:M_GI + 8] = np.arange(8)
    c[:, M_NORM1:M_NORM1 + 8] = i["mix_norm_2"][0].reshape(8, P).T
    c[:, M_NORM2:M_NORM2 + 8] = i["ffn_norm_2"][0].reshape(8, P).T
    c[:, M_CONVW:M_CONVW + 16] = i["conv_w_2"][0].reshape(4, 4, P).transpose(2, 1, 0).reshape(P, 16)
    c[:, M_CONVB:M_CONVB + 4] = i["conv_b_2"][0].reshape(4, P).T
    c[:, M_BA:M_BA + 4] = i["b_a_2"][0].reshape(4, P).T
    c[:, M_BX:M_BX + 4] = i["b_x_2"][0].reshape(4, P).T
    c[:, M_LAM:M_LAM + 4] = i["lru_lambda_2"][0].reshape(4, P).T
    c[0:8, M_BF] = i["b_forget_2"][0]
    c[:, M_BR:M_BR + 4] = i["b_group_2"][0]
    c[:, M_BR + 4:M_BR + 36] = i["b_inner_2"][0].reshape(-1)
    c[:, M_WF:M_WF + 64] = tiles(i["w_in_2"][0][:, 1536:1544])
    c[:, M_WR:M_WR + 288] = tiles(np.concatenate([i["w_group_2"][0], i["w_inner_2"][0].transpose(1, 0, 2).reshape(D, 32)], 1))
    for n in range(8):
        a, b = (n % 2) * 64, (n // 2) * P
        c[a:a + 64, M_WA + b + a:M_WA + b + a + 64] = i["w_a_2"][0, n]
        c[a:a + 64, M_WX + b + a:M_WX + b + a + 64] = i["w_x_2"][0, n]
    return c


def layouts(i):
    stream = np.zeros((len(STREAM), P, SLOT), np.float32)

    def put(name, w):
        w = tiles(w)
        assert w.shape[1] == SLOT_WIDTH[SLOT_OF[name]], (name, w.shape)
        stream[SLOT_OF[name], :, 0:w.shape[1]] = w

    sizes = [512, 128, 128, 512, 256, 256, 512, 16, 16, 512, 512, 512, 512, 1024, 1024, 1024]
    at = [0, *np.cumsum(sizes)]
    heads = np.concatenate([np.r_[j * 64:j * 64 + 64, (j + 4) * 64:(j + 4) * 64 + 64] for j in range(4)])
    params, rows = np.zeros((DEPTH, P, A_W), np.float32), np.zeros((DEPTH, P, R_W), np.float32)
    for l in range(DEPTH):
        w = i["w_in"][l]
        aq, ak, av, ag, gq, gk, gv, gaf, gab, gg, su, sv, s_g, ma, mg, ms = (w[:, a:b] for a, b in zip(at, at[1:]))
        for n in range(6):
            put(f"{l}.ada{n}", i["w_ada"][l][:, n * 512:(n + 1) * 512])
        for n, x in (("sg", s_g), ("su", su), ("ag", ag[:, heads]), ("gg", gg), ("aq", aq[:, heads]), ("gv", gv), ("sv", sv)):
            put(f"{l}.{n}", x)
        put(f"{l}.ak_gq_gate", np.concatenate([ak, gq, gaf, gab], 1))
        put(f"{l}.gk_av", np.concatenate([gk, av], 1))
        for b, m, wb in (("s", ms, i["w_br_sgu"][l]), ("a", ma, i["w_br_attn"][l][heads]), ("g", mg, i["w_br_gla"][l])):
            put(f"{l}.m{b}0", m[:, 0:512])
            put(f"{l}.m{b}1", m[:, 512:])
            put(f"{l}.wbr{b}", wb)
        for n in range(2):
            put(f"{l}.wo{n}", i["w_out"][l][:, n * 512:(n + 1) * 512])
        p = params[l]
        p[:, A_BADA:A_BADA + 24] = i["b_ada"][l].reshape(24, P).T
        p[:, A_QN] = np.concatenate([i["attn_q_norm"][l]] * 2)
        p[:, A_KN] = np.concatenate([i["attn_k_norm"][l]] * 2)
        p[:, A_ABF:A_ABF + 2] = i["gla_ab_f"][l].reshape(2, P).T
        p[:, A_ABB:A_ABB + 2] = i["gla_ab_b"][l].reshape(2, P).T
        p[:, A_ON] = i["gla_o_norm"][l]
        p[0:16, A_A2:A_A2 + 256] = i["gla_a2_f"][l]
        p[16:32, A_A2 + 256:A_A2 + 512] = i["gla_a2_b"][l]
        p[:, A_WS:A_WS + 512] = i["sgu_w"][l].transpose(2, 0, 1).reshape(P, 512)
        rows[l, :, R_G:R_G + 512] = i["sgu_ln_g"][l]
        rows[l, :, R_B:R_B + 512] = i["sgu_ln_b"][l]
        rows[l, :, R_SB:R_SB + 512] = i["sgu_b"][l].reshape(-1)
    w = i["w_in_2"][0]
    for n, a in (("q", 0), ("k", 512), ("v", 1024), ("gat", 1544), ("rec", 2056)):
        put(f"x.{n}", w[:, a:a + 512])
    for n in range(2):
        put(f"x.wo{n}", i["w_out_2"][0][:, n * 512:(n + 1) * 512])
    ex = np.empty((G * E, P, ESLOT), np.float32)
    gu = ex[:, :, 0:KT * 2 * FF].reshape(G * E, P, KT, 2, FF)
    for n, x in enumerate(("w_gate_2", "w_up_2")):
        gu[:, :, :, n, :] = i[x][0].reshape(G * E, KT, P, FF).transpose(0, 2, 1, 3)
    ex[:, :, 0:KT * 2 * FF] = gu.reshape(G * E, P, -1)
    ex[:, :, KT * 2 * FF:] = i["w_down_2"][0].reshape(G * E, 2, P, D).transpose(0, 2, 1, 3).reshape(G * E, P, 2 * D)
    xT = np.concatenate([i["ctx"][0], i["x"][0]], 0).T.reshape(KT, P, TOK).transpose(1, 0, 2)
    cond = np.stack([i["c_ctx"], i["c"][0]], -1).reshape(KT, P, 2).transpose(1, 0, 2)
    return {
        "stream": stream, "consts": trunk_constants(), "params": params, "rows": rows,
        "cond": cond, "xT": xT,
        "x_rows": i["x"][0].reshape(2, P, D).transpose(1, 0, 2),
        "ctx_rows": i["ctx"][0].reshape(2, P, D).transpose(1, 0, 2),
        "mixer_params": mixer_params(i), "experts": ex, "final_norm": i["final_norm_2"],
        "post": np.stack([i["post_ln_g"], i["post_ln_b"]], 1),
    }


def kernel(**inputs):
    import concourse.bacc as bacc
    from concourse.bass_utils import run_bass_kernel_spmd

    nc = bacc.Bacc("TRN2", target_bir_lowering=False, num_devices=1)
    arrays, io = {}, {}
    for name, a in layouts({k: np.asarray(v) for k, v in inputs.items()}).items():
        arrays["in_" + name] = np.ascontiguousarray(a)
        io[name] = nc.dram_tensor("in_" + name, a.shape, mybir.dt.from_np(a.dtype), kind="ExternalInput").ap()
    out = nc.dram_tensor("out", (256, D), F32, kind="ExternalOutput").ap()
    build(nc, io, out)
    r = run_bass_kernel_spmd(nc, [arrays], core_ids=[0])
    return r.results[0]["out"].reshape(1, 256, D)
```

```python
from contextlib import ExitStack

import concourse.bass as bass
import numpy as np
from concourse import mybir

F32 = mybir.dt.float32
F32R = mybir.dt.float32r
I32 = mybir.dt.int32
ALU = mybir.AluOpType
ACT = mybir.ActivationFunctionType
AX = mybir.AxisListType

P = 128
D = 1024
KT = D // P
TOK = 512
DEPTH = 2
ALPHA = (2 * DEPTH) ** 0.25
EPS = 1e-6
LEVELS = [64, 32, 16, 8, 4, 2, 1]
NCH = TOK // P
SLOT = 4096
NSLOT = 2
PIECE = 1024
NPIECE = 3

C_ID, C_ONES, C_BONES, C_ROT, C_COS, C_SIN = 0, 128, 256, 384, 512, 768
C_MASK = 1024
C_EPS = C_MASK + 128 * len(LEVELS)
C_ONE = C_EPS + 1
C_W = C_EPS + 4
A_QN, A_KN, A_ABF, A_ABB, A_ON = 24, 25, 26, 28, 30
A_A2 = 32
A_WS = A_A2 + 512
A_BADA = A_WS + 512
A_W = A_BADA + 24 * DEPTH
R_G, R_B, R_SB = 0, 512, 1024
R_W = 1536


M_ID, M_TRI, M_ONES, M_IOTA, M_CAUSAL, M_SEL = 0, 128, 256, 384, 512, 640
M_EPS = M_SEL + 1024
M_ONE = M_EPS + 1
M_GI = M_EPS + 2
M_NORM1, M_NORM2 = M_GI + 8, M_GI + 16
M_CONVW, M_CONVB = M_GI + 24, M_GI + 40
M_BA, M_BX, M_LAM, M_BF = M_GI + 44, M_GI + 48, M_GI + 52, M_GI + 56
M_BR = M_BF + 1
M_WF = M_BR + 36
M_WR = M_WF + 64
M_WA = M_WR + 288
M_WX = M_WA + 512
M_W = M_WX + 512
M_TOK = 256
G, E, FF = 4, 8, 256
ESLOT = KT * 2 * FF + 2 * D
PART = ESLOT // 3
OWN_PARTS = 6


class Signal:

    def __init__(self, ctx, nc, name):
        self.sem = ctx.enter_context(nc.semaphore(name))
        self.count = self.base = 0

    def one(self):
        self.count += 1
        return self.sem, 1

    def dma(self):
        self.count += 16
        return self.sem, 16

    def at(self, k):
        return self.sem, self.base + k

    def now(self):
        return self.sem, self.count

    def seal(self):
        self.base = self.count


class Banks:

    def __init__(self, ctx, nc, name, n):
        self.tiles = [ctx.enter_context(nc.psum_tensor(f"{name}{i}", [P, 512], F32)) for i in range(n)]
        self.ready_sem = ctx.enter_context(nc.semaphore(f"{name}_ready"))
        self.evac_sem = [ctx.enter_context(nc.semaphore(f"{name}{i}_evacuated")) for i in range(n)]
        self.job = {}

    def open(self, pe, name):
        n, size = len(self.job), len(self.tiles)
        assert name not in self.job, name
        self.job[name] = n
        if n >= size:
            pe.wait_ge(self.evac_sem[n % size], n // size)
        return self.tiles[n % size]

    def done(self):
        return self.ready_sem, 1

    def tile(self, name):
        return self.tiles[self.job[name] % len(self.tiles)]

    def ready(self, name):
        return self.ready_sem, self.job[name] + 1

    def evac(self, name):
        return self.evac_sem[self.job[name] % len(self.tiles)], 1

    def evacuated(self, name):
        n, size = self.job[name], len(self.tiles)
        return self.evac_sem[n % size], n // size + 1


class Weights:

    def __init__(self, ctx, nc, dram):
        self.dram = dram
        self.ring = ctx.enter_context(nc.sbuf_tensor("weight_ring", [P, NSLOT, SLOT], F32))
        self.landed = [ctx.enter_context(nc.semaphore(f"half_slot{i}_landed")) for i in range(2 * NSLOT)]
        self.last_reader = {}
        self.issued = 0

    def slot(self, name):
        return self.ring[:, SLOT_OF[name] % NSLOT, :]

    def has_landed(self, name, half):
        n = 2 * SLOT_OF[name] + half
        return self.landed[n % (2 * NSLOT)], 16 * (n // (2 * NSLOT) + 1)

    def last_read(self, name, wait, halves=(0, 1)):
        for half in halves:
            self.last_reader[2 * SLOT_OF[name] + half] = wait

    def issue(self, sp, upto):
        for n in range(self.issued, 2 * min(upto, len(STREAM))):
            if n >= 2 * NSLOT:
                sp.wait_ge(*self.last_reader[n - 2 * NSLOT])
            c = slice(n % 2 * SLOT // 2, (n % 2 + 1) * SLOT // 2)
            sp.dma_start(self.ring[:, n // 2 % NSLOT, c], self.dram[n // 2, :, c]).then_inc(self.landed[n % (2 * NSLOT)], 16)
        self.issued = max(self.issued, 2 * min(upto, len(STREAM)))


class Pieces:

    def __init__(self, ctx, nc, W):
        self.W = W
        self.hi_ring = ctx.enter_context(nc.sbuf_tensor("pieces_hi", [P, NPIECE, PIECE], F32R))
        self.lo_ring = ctx.enter_context(nc.sbuf_tensor("pieces_lo", [P, NPIECE, PIECE], F32R))
        self.hi_written = ctx.enter_context(nc.semaphore("pieces_hi_written"))
        self.lo_written = {e: ctx.enter_context(nc.semaphore(f"pieces_lo_written_{e}")) for e in ("dve", "pool")}
        self.count = {"dve": 0, "pool": 0}
        self.done = Signal(ctx, nc, "pieces_used")
        self.index, self.info, self.used = {}, [], {}

    def plan(self, slot, c, kind, engine, last):
        self.index[slot, c] = len(self.info)
        self.count[engine] += 1
        self.info.append((slot, c, kind, engine, self.count[engine]))
        if c == 1 or last:
            self.W.last_read(slot, (self.lo_written[engine], self.count[engine]), (c // 2,))

    def raw(self, slot, c, kind):
        return self.part(self.W.slot(slot)[:, c * PIECE:(c + 1) * PIECE], kind)

    def part(self, x, kind):
        return x.rearrange("p (k c) -> p k c", k={"rows": 2, "cols": 8, "branch": 4}[kind])

    def hi(self, act, slot, c):
        n = self.index[slot, c]
        kind = self.info[n][2]
        act.wait_ge(*self.W.has_landed(slot, c // 2))
        if n >= NPIECE:
            act.wait_ge(*self.used[n - NPIECE])
        act.activation(self.part(self.hi_ring[:, n % NPIECE, :], kind), self.raw(slot, c, kind), ACT.Copy)\
            .then_inc(self.hi_written, 1)

    def lo(self, eng, name, slot, c):
        n = self.index[slot, c]
        _, _, kind, engine, _ = self.info[n]
        if engine == name:
            eng.wait_ge(self.hi_written, n + 1)
            eng.tensor_tensor(self.part(self.lo_ring[:, n % NPIECE, :], kind), self.raw(slot, c, kind),
                              self.part(self.hi_ring[:, n % NPIECE, :], kind).bitcast(F32), ALU.subtract)\
                .then_inc(self.lo_written[engine], 1)

    def take(self, pe, slot, c):
        n = self.index[slot, c]
        _, _, kind, engine, count = self.info[n]
        pe.wait_ge(self.lo_written[engine], count)
        return tuple(self.part(r[:, n % NPIECE, :], kind) for r in (self.hi_ring, self.lo_ring))

    def last_use(self, slot, c, wait):
        self.used[self.index[slot, c]] = wait


def split_product(pe, out, stationary, moving, start, stop):
    (sh, sl), (mh, ml) = stationary, moving
    pe.matmul(out, sh, mh, start=start, stop=False)
    pe.matmul(out, sh, ml, start=False, stop=False)
    return pe.matmul(out, sl, mh, start=False, stop=stop)


def linker(eng, own):
    def link(ins):
        ins.then_inc(*own.one())
        eng.wait_ge(*own.now())
    return link


class Signals:

    def __init__(self, ctx, nc):
        self.all = []

        def signal(name):
            self.all.append(Signal(ctx, nc, name))
            return self.all[-1]

        self.cond_in = signal("cond_in")
        self.small_in = signal("small_in")
        self.x_in = signal("x_in")
        self.post_in = signal("post_in")
        self.silu_c = signal("silu_c")
        self.h_ready = signal("h_ready")
        self.normed = signal("normed")
        self.roped = signal("roped")
        self.soft = signal("soft")
        self.neg_max = signal("neg_max")
        self.probs = signal("probs")
        self.keys = signal("keys")
        self.key_diff = signal("key_diff")
        self.key_exp = signal("key_exp")
        self.lev_diff = signal("lev_diff")
        self.lev_exp = signal("lev_exp")
        self.lev_q = signal("lev_q")
        self.lev_k = signal("lev_k")
        self.query_exp = signal("query_exp")
        self.queries = signal("queries")
        self.vn = signal("vn")
        self.osq = signal("osq")
        self.act_own = signal("act_own")
        self.dve_own = signal("dve_own")
        self.norm_root = signal("norm_root")
        self.scaled = signal("scaled")
        self.fsoft = signal("fsoft")
        self.cum = signal("cum")
        self.conv = signal("conv")
        self.gates_ri = signal("gates_ri")
        self.lam = signal("lam")
        self.lru_mult = signal("lru_mult")
        self.lru_seq = signal("lru_seq")
        self.route_max = signal("route_max")
        self.route_exp = signal("route_exp")
        self.inner_max = signal("inner_max")
        self.inner_exp = signal("inner_exp")
        self.one_hot = signal("one_hot")
        self.selected = signal("selected")
        self.silu_g = signal("silu_g")
        self.slots_w = signal("slots_w")
        self.x_done = signal("x_done")
        self.norm_out = signal("norm_out")
        self.over_flag = signal("over_flag")
        self.gathered_hi = signal("gathered_hi")
        self.gathered = signal("gathered")
        self.hidden_hi = signal("hidden_hi")
        self.h_ready_pool = signal("h_ready_pool")
        self.rows_in = signal("rows_in")
        self.orstd = signal("orstd")
        self.head_rstd = signal("head_rstd")
        self.par_in = signal("par_in")
        self.fin_in = signal("fin_in")
        self.sv_stat = signal("sv_stat")
        self.sv_root = signal("sv_root")
        self.x_stat = signal("x_stat")
        self.x_root = signal("x_root")
        self.z_abs = signal("z_abs")
        self.z_exp = signal("z_exp")
        self.x_hi = signal("x_hi")
        self.h_f32 = signal("h_f32")
        self.y_gla = signal("y_gla")
        self.y_hi = signal("y_hi")
        self.y_lo = signal("y_lo")
        self.m_hi = signal("m_hi")
        self.m_lo = signal("m_lo")

    def seal(self):
        for s in self.all:
            s.seal()



def units_of(l):
    return [(s, j, t) for s in ((0, 1) if l == 0 else (1,)) for j in range(4) for t in range(2)]


def piece_of(l, kind, i):
    if kind in ("sg", "su", "ag", "gg", "aq"):
        return f"{l}.{kind}", i, "cols"
    if kind in ("ak", "gq", "gate"):
        return f"{l}.ak_gq_gate", {"ak": 0, "gq": 1, "gate": 3}[kind] + i, "cols"
    if kind in ("gk", "av"):
        return f"{l}.gk_av", {"gk": 0, "av": 2}[kind] + i, "cols"
    if kind in ("gv", "sv"):
        return f"{l}.{kind}", i, "rows"
    if kind == "merge_gate":
        return f"{l}.m{i[0]}{i[1] // 4}", i[1] % 4, "cols"
    if kind == "merge" and i[1] % 2 == 0:
        return f"{l}.wbr{i[0]}", i[1] // 2, "branch"
    if kind == "final":
        return f"{l}.wo{i // 4}", i % 4, "rows"
    return None


PIECES_OF_SLOT = {"gk_av": 3}


def with_splits(steps, pieces, piece_of_step, ahead=2):
    use = [(n, piece_of_step(*s)) for n, s in enumerate(steps) if piece_of_step(*s)]
    place, plain = {}, [n for n, s in enumerate(steps) if s[0] == "ada"]
    for m, (n, (slot, c, kind)) in enumerate(use):
        at = max([use[max(m - ahead, 0)][0]] + [a + 1 for a in plain if a < n])
        engine = "pool" if steps[n][0] in ("gv", "sv", "final") else "dve"
        if m < NPIECE:
            at = steps.index(("hsplit", 2)) if plain and plain[0] == 0 else 0
            engine = "pool"
        pieces.plan(slot, c, kind, engine, c == PIECES_OF_SLOT.get(slot[2:], 4) - 1)
        place.setdefault(at, []).append(("split", (slot, c)))
    out = []
    for n, s in enumerate(steps):
        out += place.get(n, []) + [s]
    return out


def trunk_schedule(l):
    n_units = len(units_of(l))
    first = sum(([("ada", (0, n)), ("adat", (0, n))] for n in range(4)), []) if l == 0 else []
    first += [("h", k) for k in range(4)] + [("hsplit", 0), ("h", 4), ("h", 5), ("hsplit", 1), ("h", 6), ("h", 7)]
    first += [("hsplit", 2), ("hsplit", 3)]
    first += [(n, i) for n in ("sg", "su", "ag") for i in range(4)]
    first += [("ak", 0), ("gq", 0), ("gq", 1), ("gate", 0)]
    first += [("aq", 0), ("z", 0), ("aq", 1), ("z", 1), ("aq", 2), ("z", 2), ("aq", 3), ("z", 3)]
    first += [("stat", 0), ("gk", 0), ("stat", 1), ("stat", 2), ("gk", 1), ("stat", 3), ("stat", 4), ("soft", 0), ("av", 0)]
    first += [("rstd", i) for i in range(5)] + [("rot", i) for i in range(5)] + [("vt", 0), ("decay", 0)]
    att = []
    for i in range(n_units + 2):
        att += [s for s in (("sums", i - 1), ("score", i), ("turn", i - 1), ("pv", i - 2)) if 0 <= s[1] < n_units]
    gv, sv = ([(n, g) for g in range(4)] for n in ("gv", "sv"))
    rest = [("key", 0), gv, ("keyt", 0), ("key", 1)]
    rest += [sv + [("svn", 0)], ("keyt", 1), ("kv", 0), ("kv", 1), ("kv", 2), ("diag", 0)]
    fill = [("mix", g) for g in range(4)]
    if l == 0:
        ada = [("ada", x) for x in [(0, 4), (0, 5)] + [(1, n) for n in range(6)]]
        fill = sum(([a, fill.pop(0)] if fill else [a] for a in ada), [])
    halves = 2 * len(LEVELS)
    for n in range(halves + 2):
        rest += [s for s in (("scale", n - 1), ("pairs", n - 2), ("diff", n))
                 if 0 <= s[1] < halves]
        if n % 2 and fill:
            rest.append(fill.pop(0))
    rest += [("query", 0)] + fill
    for n in [n for n, s in enumerate(rest) if s[0] == "ada"][::-1]:
        rest.insert(n + (1 if rest[n + 1:n + 2] == [] or rest[n + 1][0] in ("ada", "adat") else 2), ("adat", rest[n][1]))
    steps, done = list(first), 0
    for n, a in enumerate(att):
        steps.append(a)
        upto = (n + 1) * len(rest) // len(att)
        steps += sum((r if type(r) is list else [r] for r in rest[done:upto]), [])
        done = upto
    steps += [("out", 0), ("out", 1), ("ostat", 0), ("out", 2), ("ostat", 1), ("out", 3), ("ostat", 2), ("gg", 0), ("ostat", 3)]
    steps += [("gg", i) for i in (1, 2, 3)]
    last = []
    for b in "sag":
        for c in range(8):
            steps += [("merge_gate", (b, c))] + last
            last = [("merge", (b, c))]
            if c == 0:
                steps += [("ysplit", (b, k)) for k in range(4)]
    steps += last + [("msplit", 0), ("msplit", 1), ("growb", 0), ("msplit", 2), ("msplit", 3)]
    steps += [("final", g) for g in range(4)] + [("finish", 0)] + [("final", g) for g in range(4, 8)] + [("finish", 1)]
    return steps


def stream_order():
    names = {}
    for l in range(DEPTH):
        for kind, i in trunk_schedule(l):
            piece = (f"{i[0]}.ada{i[1]}",) if kind == "ada" else piece_of(l, kind, i)
            if piece:
                names[piece[0]] = None
    return list(names) + [f"x.{n}" for n in ("rec", "q", "k", "v", "gat", "wo0", "wo1")]


STREAM = stream_order()
SLOT_OF = {n: i for i, n in enumerate(STREAM)}


def trunk_layer(nc, l, io, W, PC, jobs, sig, consts, silu_c, modulation, xlat, xctx, HH, HL):
    T0 = 0 if l == 0 else 256
    last_pair = 2 * len(LEVELS) - 1
    NT = TOK - T0
    C0 = T0 // P
    NC = NCH - C0
    steps = with_splits(trunk_schedule(l), PC, lambda kind, i: piece_of(l, kind, i))
    small_in = 16 * (2 if l == 0 else 1)
    first_use = ("adat", (0, 0)) if l == 0 else ("z", 0)
    units = units_of(l)
    PJ, PS, PT = jobs
    ident = consts[:, C_ID:C_ID + P]
    eps = consts[:, C_EPS:C_EPS + 1]
    one = consts[:, C_ONE:C_ONE + 1]
    J = lambda name, *i: f"{l}.{name}" + "".join(f".{x}" for x in i)

    with ExitStack() as ctx:
        def sb(name, shape, dt=F32):
            return ctx.enter_context(nc.sbuf_tensor(f"l{l}_{name}", shape, dt))

        par = sb("params", [P, A_W])
        YA, YG, YS = sb("y_attn", [P, 4, 512]), sb("y_gla", [P, 4, 512]), sb("y_sgu", [P, 4, 512])
        small = sb("small", [P, 2, 8])
        ada = modulation[:, l]
        ada_row = YG[0:2, 3, :]
        diag = sb("diag", [P, 2, P])
        stats = sb("stats", [P, 4, 16])
        rstd4 = sb("rstd", [P, 4, 2])
        with ExitStack() as mixing:
            def sa(name, shape, dt=F32):
                return mixing.enter_context(nc.sbuf_tensor(f"l{l}_{name}", shape, dt))

            rows = sa("rows", [P, R_W])
            Q, GQ, GK = sa("q", [P, 4, 512]), sa("gla_q", [P, 2, 512]), sa("gla_k", [P, 2, 512])
            DD = sa("decayed", [P, 4, 512])
            DQ, DK = DD[:, 0:2], DD[:, 2:4]
            SCR = sa("probs", [P, 4, 512])
            PR = SCR[:].rearrange("p (b u) l -> p b u l", b=2)
            PTB = sa("probs_t", [P, 2, 2, 512])
            K = sa("k", [P, 512])
            V = sa("v", [P, 4, P])
            BF, BB = sa("b_fwd", [P, 2, 512]), sa("b_bwd", [P, 2, 512])
            GV = xctx[:].rearrange("p t (a c) -> p (t a) c", a=2)
            ATT = sa("gla_att", [P, 4, 512])
            ATH = ATT[:].rearrange("p (u x) (c y) -> p u (x c) y", u=2, c=2)
            KET = ATT[:, :, 0:384]
            agT = ATT[0:32, 3, :]
            S = YG[:].rearrange("p a c -> p (a c)")[:, 0:1536].rearrange("p (a n c) -> p a n c", a=4, n=3)
            ED = sa("gla_chunk_decay", [P, 4, 4])
        with ExitStack() as merging:
            def sm(name, shape, dt=F32):
                return merging.enter_context(nc.sbuf_tensor(f"l{l}_{name}", shape, dt))

            mT = sm("merged", [P, 8, 512])
            YH, YL = sm("y_hi", [P, 4, 512], F32R), sm("y_lo", [P, 4, 512], F32R)
            SGM = sm("merge_gate", [P, 4, 512])
            TMP = sm("merge_tmp", [P, 2, 512])
            gateb = sm("out_gate", [P, 2, 2, 512])
            post = [sm("post_g", [P, D]), sm("post_b", [P, D])]
        HF = [DD[:], SCR[:]]
        VN = (xlat[:].rearrange("p t (a c) -> p (t a) c", a=2) if l == 0 else None)

        def modulated(layer, n):
            return f"modulation.{layer}.{n}"

        def modulated_t(layer, n):
            return f"modulation_t.{layer}.{n}"

        def vn(t):
            if l == 0:
                return VN[:, t, :]
            return Q[:, 2 * (t - 2):2 * (t - 2) + 2, 0:256]

        def vn_group(t, g):
            if l == 0:
                return VN[:, t, g * P:(g + 1) * P]
            return Q[:, 2 * (t - 2) + g // 2, (g % 2) * P:(g % 2) * P + P]

        def xres(t):
            return xctx[:, t, :] if t < 2 else xlat[:, t - 2, :]

        def sq(i):
            return (SCR[:, i] if i < 4 else PTB[:, 0, 0])

        def out_bank(t, h):
            if h == 0:
                return PJ
            return PS if t < 2 else PT

        def DQK(i):
            return (DQ[:, 0], DQ[:, 1], DK[:, 0], DK[:, 1])[i]

        block = ctx.enter_context(nc.Block())

        @block.tensor
        def _(pe):
            def feature_major(name, step, t0=T0):
                slot, c, _ = piece_of(l, *step)
                acc = PJ.open(pe, name)
                wh, wl = PC.take(pe, slot, c)
                for k in range(KT):
                    if step == ("sg", 0) and k % 2 == 0:
                        pe.wait_ge(*(sig.h_ready_pool.at(1) if k == 4 else sig.h_ready.at((1, 2, 2, 3)[k // 2])))
                    last = split_product(pe, acc[:, 0:TOK - t0], (wh[:, k], wl[:, k]), (HH[:, k, t0:], HL[:, k, t0:]),
                                         k == 0, k == KT - 1)
                last.then_inc(*PJ.done())
                PC.last_use(slot, c, PJ.ready(name))

            def token_major(step, g, tiles, x, names):
                slot, c, _ = piece_of(l, *step)
                if g == 0:
                    for t in tiles:
                        names(t)[0].open(pe, names(t)[1])
                wh, wl = PC.take(pe, slot, c)
                for t in tiles:
                    banks, name = names(t)
                    for n in range(2):
                        k = 2 * g + n
                        xt = tuple(a[:, k, t * P:(t + 1) * P] for a in x)
                        last = split_product(pe, banks.tile(name)[:, :], xt, (wh[:, n], wl[:, n]), k == 0, k == KT - 1)
                    if g == 3:
                        last.then_inc(*banks.done())
                if g == 3:
                    PC.last_use(slot, c, banks.ready(name))
                else:
                    last.then_inc(*PC.done.one())
                    PC.last_use(slot, c, PC.done.now())

            if l == 0:
                pe.wait_ge(*sig.silu_c.at(1))
            for kind, i in steps:
                if (kind, i) == first_use:
                    pe.wait_ge(*sig.small_in.at(small_in))
                if kind == "ada":
                    acc = PT.open(pe, modulated(*i))
                    slot = f"{i[0]}.ada{i[1]}"
                    w = W.slot(slot).rearrange("p (k c) -> p k c", c=512)
                    for k in range(KT):
                        if k % 4 == 0:
                            pe.wait_ge(*W.has_landed(slot, k // 4))
                        last = pe.matmul(acc[0:2, :], silu_c[:, k, :], w[:, k, :], start=(k == 0), stop=(k == KT - 1))
                    last.then_inc(*PT.done())
                    W.last_read(slot, PT.ready(modulated(*i)))
                elif kind == "adat":
                    pe.wait_ge(*PT.evacuated(modulated(*i)))
                    acc = PT.open(pe, modulated_t(*i))
                    for m in range(4):
                        last = pe.matmul(acc[:, 2 * m:2 * m + 2], ada_row[:, m * P:(m + 1) * P], ident[0:2, 0:2],
                                         start=True, stop=True)
                    last.then_inc(*PT.done())
                elif kind == "h":
                    if l:
                        acc = PT.open(pe, J("h", i))
                        for t in range(4):
                            last = pe.transpose(acc[:, t * P:(t + 1) * P], xres(t)[:, i * P:(i + 1) * P], ident)
                        last.then_inc(*PT.done())
                elif kind in ("sg", "su", "ag", "gg", "aq", "gq", "merge_gate"):
                    feature_major(J(kind, i), (kind, i))
                elif kind in ("ak", "gate", "gk", "av"):
                    feature_major(J(kind, i), (kind, i), 0)
                elif kind == "vt":
                    pe.wait_ge(*PJ.evacuated(J("av", 0)))
                    acc = PT.open(pe, J("vt"))
                    for t in range(4):
                        last = pe.transpose(acc[:, t * P:(t + 1) * P], PTB[:, 1, 1, t * P:(t + 1) * P], ident)
                    last.then_inc(*PT.done())
                elif kind == "gv":
                    token_major((kind, i), i, range(4), (HH, HL), lambda t: (PJ, J("gv", t)))
                elif kind == "sv":
                    token_major((kind, i), i, range(C0, 4), (HH, HL), lambda t: (PJ, J("sv", t)))
                elif kind == "z":
                    if i == 0:
                        pe.wait_ge(*PJ.evacuated(J("gate", 0)))
                    acc = PT.open(pe, J("z", i))
                    pe.matmul(acc[:, :], par[0:32, A_A2 + i * P:A_A2 + (i + 1) * P], agT[:, :],
                              start=True, stop=True).then_inc(*PT.done())
                elif kind == "stat":
                    n = TOK if i == 0 else NT
                    pe.wait_ge(*PJ.evacuated(J("ak", 0) if i == 0 else J("aq", i - 1)))
                    acc = PT.open(pe, J("stat", i))
                    pe.matmul(acc[:, 0:n], consts[:, C_BONES:C_BONES + P], sq(i)[:, 0:n],
                              start=True, stop=True).then_inc(*PT.done())
                elif kind == "rot":
                    pe.wait_ge(*sig.normed.at(i + 1))
                    acc = PT.open(pe, J("rot", i))
                    src = K[:, 256:512] if i == 0 else Q[:, i - 1, 256:512]
                    pe.matmul(acc[:, 0:256], consts[:, C_ROT:C_ROT + P], src,
                              start=True, stop=True).then_inc(*PT.done())
                elif kind == "score":
                    s, j, t = units[i]
                    n = 256 * (s + 1)
                    if i == 0:
                        pe.wait_ge(*sig.roped.at(5))
                    for u in range(2):
                        acc = PS.open(pe, J("score", i, u))
                        tok = s * 256 + t * P
                        pe.matmul(acc[:, 0:n], Q[64 * u:64 * u + 64, j, tok:tok + P], K[64 * u:64 * u + 64, 0:n],
                                  start=True, stop=True).then_inc(*PS.done())
                elif kind == "turn":
                    s = units[i][0]
                    for u in range(2):
                        pe.wait_ge(*sig.probs.at(2 * i + u + 1))
                        acc = PT.open(pe, J("turn", i, u))
                        for b in range(2 * (s + 1)):
                            last = pe.matmul(acc[:, b * P:(b + 1) * P], PR[:, i % 2, u, b * P:(b + 1) * P], diag[:, u, :],
                                             start=True, stop=True)
                        last.then_inc(*PT.done())
                elif kind == "pv":
                    s = units[i][0]
                    if i == 0:
                        pe.wait_ge(*PT.evacuated(J("vt")))
                    acc = PJ.open(pe, J("pv", i))
                    nb = 2 * (s + 1)
                    for u in range(2):
                        pe.wait_ge(*PT.evacuated(J("turn", i, u)))
                        for b in range(nb):
                            last = pe.matmul(acc[64 * u:64 * u + 64, 0:P], V[:, b, 64 * u:64 * u + 64],
                                             PTB[:, i % 2, u, b * P:(b + 1) * P], start=(b == 0), stop=(b == nb - 1))
                    last.then_inc(*PJ.done())
                elif kind == "keyt":
                    pe.wait_ge(*sig.keys.at(i + 1))
                    for p in range(2):
                        acc = PT.open(pe, J("keyt", i, p))
                        for n, c in enumerate((0, 1, 2) if i == 0 else (1, 0, 3)):
                            last = pe.transpose(acc[:, n * P:(n + 1) * P], DK[:, p, c * P:(c + 1) * P], ident)
                        last.then_inc(*PT.done())
                elif kind == "kv":
                    if i == 0:
                        pe.wait_ge(*PJ.evacuated(J("gv", 3)))
                        for d in range(2):
                            for p in range(2):
                                pe.wait_ge(*PT.evacuated(J("keyt", d, p)))
                    acc = PT.open(pe, J("kv", i))
                    for d in range(2):
                        c = (0, 1, 2)[i] if d == 0 else (1, 0, 3)[i]
                        for p in range(2):
                            for u in range(2):
                                last = pe.matmul(acc[64 * u:64 * u + 64, (2 * d + p) * P:(2 * d + p + 1) * P],
                                                 KET[:, 2 * d + p, i * P + 64 * u:i * P + 64 * u + 64],
                                                 GV[:, c, (2 * p + u) * P:(2 * p + u + 1) * P], start=True, stop=True)
                    last.then_inc(*PT.done())
                elif kind in ("diag", "pairs"):
                    if kind == "diag":
                        pe.wait_ge(*PJ.evacuated(J("gq", 1)))
                        pe.wait_ge(*PJ.evacuated(J("gk", 1)))
                        q, k = GQ, GK
                    else:
                        pe.wait_ge(*sig.lev_q.at(i + 1))
                        pe.wait_ge(*sig.lev_k.at(i + 1))
                        q, k = DQ, DK
                    for p in ((0, 1) if kind == "diag" else (i % 2,)):
                        for u in range(2):
                            acc = PT.open(pe, J(kind, i, p, u))
                            for c in range(C0, NCH):
                                last = pe.matmul(acc[:, (c - C0) * P:(c - C0 + 1) * P],
                                                 k[64 * u:64 * u + 64, p, c * P:(c + 1) * P],
                                                 q[64 * u:64 * u + 64, p, c * P:(c + 1) * P], start=True, stop=True)
                            last.then_inc(*PT.done())
                elif kind == "mix":
                    for c in range(C0, NCH):
                        pe.wait_ge(*sig.vn.at(c - C0 + 1))
                    acc = PJ.open(pe, J("mix", i))
                    for c in range(C0, NCH):
                        last = pe.matmul(acc[:, (c - C0) * P:(c - C0 + 1) * P], vn_group(c, i),
                                         par[:, A_WS + i * P:A_WS + (i + 1) * P], start=True, stop=True)
                    last.then_inc(*PJ.done())
                elif kind == "out":
                    if i == 0:
                        pe.wait_ge(*sig.queries.at(2))
                        pe.wait_ge(*PT.evacuated(J("kv", 2)))
                        for u in range(2):
                            pe.wait_ge(*PT.evacuated(J("pairs", last_pair, 1, u)))
                    p, u = i // 2, i % 2
                    acc = PJ.open(pe, J("out", i))
                    for c in range(C0, NCH):
                        o = acc[:, (c - C0) * P:(c - C0 + 1) * P]
                        from_state = [(d, n) for d, n in ((0, c), (1, c ^ 1)) if n > 0]
                        pe.matmul(o, GV[:, c, i * P:(i + 1) * P], ATH[:, u, c, p * P:(p + 1) * P], start=True, stop=False)
                        for x, (d, n) in enumerate(from_state):
                            b = (BF, BB)[d]
                            last = pe.matmul(o, S[64 * u:64 * u + 64, 2 * d + p, n - 1, :],
                                             b[64 * u:64 * u + 64, p, c * P:(c + 1) * P],
                                             start=False, stop=(x == len(from_state) - 1))
                    last.then_inc(*PJ.done())
                elif kind == "ostat":
                    pe.wait_ge(*sig.osq.at(i + 1))
                    acc = PT.open(pe, J("ostat", i))
                    pe.matmul(acc[:, 0:NT], consts[:, C_ONES:C_ONES + P], DQK(i)[:, 0:NT],
                              start=True, stop=True).then_inc(*PT.done())
                elif kind == "merge":
                    b, c = i
                    slot, pc, _ = piece_of(l, "merge", (b, c - c % 2))
                    acc = PS.open(pe, J("br", b, c))
                    wh, wl = PC.take(pe, slot, pc)
                    m = slice((c % 2) * P, (c % 2 + 1) * P)
                    for k in range(4):
                        if c == 0:
                            pe.wait_ge(*sig.y_lo.at(4 * "sag".index(b) + k + 1))
                        last = split_product(pe, acc[:, 0:NT], (wh[:, k, m], wl[:, k, m]), (YH[:, k, T0:], YL[:, k, T0:]),
                                             k == 0, k == 3)
                    last.then_inc(*PS.done())
                    if c % 2:
                        PC.last_use(slot, pc, PS.ready(J("br", b, c)))
                elif kind == "growb":
                    pe.wait_ge(*PT.evacuated(modulated_t(l, 4)))
                    pe.wait_ge(*PT.evacuated(modulated_t(l, 5)))
                    for s in range(C0 // 2, 2):
                        for h in range(2):
                            acc = PT.open(pe, J("growb", s, h))
                            for m in range(4):
                                col = ada[:, 16 + 4 * h + m, s:s + 1]
                                last = pe.matmul(acc[:, m * P:(m + 1) * P], col.to_broadcast([P, P]), ident,
                                                 start=True, stop=True)
                            last.then_inc(*PT.done())
                elif kind == "final":
                    h, g = i // 4, i % 4
                    if h == 0:
                        pe.wait_ge(*sig.m_lo.at(g + 1))
                    token_major((kind, i), g, range(C0, 4), (HH, HL), lambda t: (out_bank(t, h), J("final", t, h)))

        @block.scalar
        def _(act):
            link = linker(act, sig.act_own)
            if l == 0:
                act.wait_ge(*sig.cond_in.at(16))
                act.activation(silu_c[:], silu_c[:], ACT.Silu).then_inc(*sig.silu_c.one())
            for kind, i in steps:
                if (kind, i) == first_use:
                    act.wait_ge(*sig.small_in.at(small_in))
                if kind == "split":
                    PC.hi(act, *i)
                elif kind == "ada":
                    act.wait_ge(*PT.ready(modulated(*i)))
                    if i[0] or i[1]:
                        act.wait_ge(*PT.ready(modulated_t(*((i[0], i[1] - 1) if i[1] else (i[0] - 1, 5)))))
                    act.activation(ada_row, PT.tile(modulated(*i))[0:2, :], ACT.Copy).then_inc(*PT.evac(modulated(*i)))
                elif kind == "hsplit":
                    act.wait_ge(*sig.h_f32.at(i + 1))
                    act.activation(HH[:, 2 * i:2 * i + 2, :], HF[i // 2][:, 2 * (i % 2):2 * (i % 2) + 2, :], ACT.Copy)\
                        .then_inc(*sig.x_hi.one())
                elif kind == "ysplit":
                    b, k = i
                    n = "sag".index(b)
                    if k == 0:
                        act.wait_ge(*PJ.evacuated({"s": J("mix", 3), "a": J("pv", len(units) - 1), "g": J("gg", 3)}[b]))
                        if n:
                            act.wait_ge(*PS.ready(J("br", "sag"[n - 1], 7)))
                        else:
                            act.wait_ge(*sig.y_gla.at(4))
                    act.activation(YH[:, k, T0:], {"s": YS, "a": YA, "g": YG}[b][:, k, T0:], ACT.Copy)\
                        .then_inc(*sig.y_hi.one())
                elif kind == "msplit":
                    k = slice(2 * i, 2 * i + 2)
                    act.wait_ge(*PS.evacuated(J("br", "g", 2 * i + 1)))
                    act.wait_ge(*PJ.ready(J("merge_gate", ("g", 7))))
                    act.activation(HH[:, k, T0:], mT[:, k, T0:], ACT.Copy).then_inc(*sig.m_hi.one())
                elif kind in ("sg", "ag", "gg"):
                    act.wait_ge(*PJ.ready(J(kind, i)))
                    y = {"sg": YS, "ag": YA, "gg": YG}[kind]
                    act.activation(y[:, i, T0:], PJ.tile(J(kind, i))[:, 0:NT], ACT.Silu).then_inc(*PJ.evac(J(kind, i)))
                elif kind in ("ak", "aq"):
                    name, n, t0 = (J("ak", 0), 0, 0) if kind == "ak" else (J("aq", i), i + 1, T0)
                    dst = K[:, :] if kind == "ak" else Q[:, i, T0:]
                    act.wait_ge(*PJ.ready(name))
                    acc = PJ.tile(name)[:, 0:TOK - t0]
                    act.activation(dst, acc, ACT.Copy)
                    act.activation(sq(n)[:, 0:TOK - t0], acc, ACT.Square).then_inc(*PJ.evac(name))
                elif kind == "gq":
                    act.wait_ge(*PJ.ready(J("gq", i)))
                    act.activation(GQ[:, i, T0:], PJ.tile(J("gq", i))[:, 0:NT], ACT.Copy, scale=0.125)\
                        .then_inc(*PJ.evac(J("gq", i)))
                elif kind == "gk":
                    act.wait_ge(*PJ.ready(J("gk", i)))
                    act.activation(GK[:, i, :], PJ.tile(J("gk", i))[:, :], ACT.Copy).then_inc(*PJ.evac(J("gk", i)))
                elif kind == "gate":
                    act.wait_ge(*PJ.ready(J("gate", 0)))
                    act.activation(agT[:, :], PJ.tile(J("gate", 0))[0:32, :], ACT.Copy).then_inc(*PJ.evac(J("gate", 0)))
                elif kind == "av":
                    act.wait_ge(*PJ.ready(J("av", 0)))
                    act.activation(PTB[:, 1, 1], PJ.tile(J("av", 0))[:, :], ACT.Copy).then_inc(*PJ.evac(J("av", 0)))
                elif kind == "vt":
                    act.wait_ge(*PT.ready(J("vt")))
                    act.activation(V[:], PT.tile(J("vt"))[:].rearrange("p (t c) -> p t c", t=4), ACT.Copy)\
                        .then_inc(*PT.evac(J("vt")))
                elif kind == "gv" and i == 3:
                    for t in range(4):
                        act.wait_ge(*PJ.ready(J("gv", t)))
                        act.activation(GV[:, t, :], PJ.tile(J("gv", t))[:, :], ACT.Copy).then_inc(*PJ.evac(J("gv", t)))
                elif kind == "z":
                    t = DD[:, i, :]
                    act.wait_ge(*PT.ready(J("z", i)))
                    act.activation(t, PT.tile(J("z", i))[:, :], ACT.Abs, bias=par[:, A_ABF + i:A_ABF + i + 1])\
                        .then_inc(*sig.z_abs.one())
                    act.wait_ge(*sig.z_abs.at(i + 1))
                    act.activation(t, t, ACT.Exp, scale=-1.0).then_inc(*sig.z_exp.one())
                elif kind == "stat":
                    n = TOK if i == 0 else NT
                    act.wait_ge(*PT.ready(J("stat", i)))
                    act.activation(sq(i)[:, 0:n], PT.tile(J("stat", i))[:, 0:n], ACT.Ln, bias=eps)\
                        .then_inc(*PT.evac(J("stat", i)))
                elif kind == "rstd":
                    act.wait_ge(*PT.evacuated(J("stat", i)))
                    n = TOK if i == 0 else NT
                    act.activation(sq(i)[:, 0:n], sq(i)[:, 0:n], ACT.Exp, scale=-0.5).then_inc(*sig.head_rstd.one())
                elif kind == "svn":
                    act.wait_ge(*sig.sv_stat.at(NC))
                    act.activation(rstd4[:, C0:, 0:1], stats[:, C0:, 13:14], ACT.Sqrt, bias=eps).then_inc(*sig.sv_root.one())
                elif kind == "ostat":
                    act.wait_ge(*PT.ready(J("ostat", i)))
                    d = DQK(i)[:, 0:NT]
                    act.activation(d, PT.tile(J("ostat", i))[:, 0:NT], ACT.Ln, bias=eps).then_inc(*PT.evac(J("ostat", i)))
                    act.wait_ge(*PT.evacuated(J("ostat", i)))
                    act.activation(d, d, ACT.Exp, scale=-0.5).then_inc(*sig.orstd.one())
                elif kind == "finish" and i == 1:
                    for t in range(C0, 4):
                        act.wait_ge(*sig.x_stat.at(t - C0 + 1))
                        act.activation(rstd4[:, t, 1:2], stats[:, t, 13:14], ACT.Sqrt, bias=eps).then_inc(*sig.x_root.one())
                elif kind == "soft":
                    act.wait_ge(*sig.z_exp.at(4))
                    act.activation(DD[:], DD[:], ACT.Ln, bias=one).then_inc(*sig.soft.one())
                elif kind == "score":
                    s, j, t = units[i]
                    n = 256 * (s + 1)
                    for u in range(2):
                        act.wait_ge(*sig.neg_max.at(2 * i + u + 1))
                        if i == 0 and u == 0:
                            act.wait_ge(*sig.roped.at(5))
                        act.activation(PR[:, i % 2, u, 0:n], PS.tile(J("score", i, u))[:, 0:n], ACT.Exp,
                                       bias=small[:, i % 2, 2 + u:3 + u], scale=0.125,
                                       accum_out=small[:, i % 2, 4 + u:5 + u]).then_inc(*PS.evac(J("score", i, u)))
                elif kind == "turn":
                    n = 256 * (units[i][0] + 1)
                    for u in range(2):
                        act.wait_ge(*PT.ready(J("turn", i, u)))
                        if i >= 2:
                            act.wait_ge(*PJ.ready(J("pv", i - 2)))
                        act.activation(PTB[:, i % 2, u, 0:n], PT.tile(J("turn", i, u))[:, 0:n], ACT.Copy)\
                            .then_inc(*PT.evac(J("turn", i, u)))
                elif kind == "key":
                    act.wait_ge(*sig.key_diff.at(i + 1))
                    e = act.activation(DK, DK, ACT.Exp, scale=1 / 16)
                    b, edge = ((BF, 127), (BB, 0))[i]
                    bv = b[:].rearrange("p a (c t) -> p a c t", t=P)
                    act.activation(ED[:, 2 * i:2 * i + 2, :], bv[:, :, :, edge], ACT.Exp, scale=1 / 16)\
                        .then_inc(*sig.key_exp.one())
                elif kind == "keyt":
                    for p in range(2):
                        act.wait_ge(*PT.ready(J("keyt", i, p)))
                        act.activation(KET[:, 2 * i + p, :], PT.tile(J("keyt", i, p))[:, 0:384], ACT.Copy)\
                            .then_inc(*PT.evac(J("keyt", i, p)))
                elif kind == "diff":
                    act.wait_ge(*sig.lev_diff.at(i + 1))
                    qk = DD[:, i % 2::2, T0:]
                    act.activation(qk, qk, ACT.Exp, scale=1 / 16).then_inc(*sig.lev_exp.one())
                elif kind == "query":
                    if i == 0:
                        act.wait_ge(*sig.lev_diff.at(2 * len(LEVELS)))
                    act.activation(BF[:, :, T0:], BF[:, :, T0:], ACT.Exp, scale=1 / 16).then_inc(*sig.query_exp.one())
                    act.activation(BB[:, :, T0:], BB[:, :, T0:], ACT.Exp, scale=1 / 16).then_inc(*sig.query_exp.one())
                elif kind == "out":
                    act.wait_ge(*PJ.ready(J("out", i)))
                    act.activation(DQK(i)[:, 0:NT], PJ.tile(J("out", i))[:, 0:NT], ACT.Square).then_inc(*sig.osq.one())
                elif kind == "merge_gate":
                    b, c = i
                    n = "sag".index(b) * 8 + c
                    act.wait_ge(*PJ.ready(J("merge_gate", i)))
                    if n >= 4:
                        act.wait_ge(*PS.evacuated(J("br", "sag"[(n - 4) // 8], (n - 4) % 8)))
                    act.activation(SGM[:, n % 4, 0:NT], PJ.tile(J("merge_gate", i))[:, 0:NT], ACT.Sigmoid)\
                        .then_inc(*PJ.evac(J("merge_gate", i)))
                elif kind == "growb":
                    for s in range(C0 // 2, 2):
                        for h in range(2):
                            act.wait_ge(*PT.ready(J("growb", s, h)))
                            act.activation(gateb[:, s, h, :], PT.tile(J("growb", s, h))[:, :], ACT.Copy)\
                                .then_inc(*PT.evac(J("growb", s, h)))

        @block.vector
        def _(dve):
            link = linker(dve, sig.dve_own)

            def att_of(p, u):
                return ATH[:, u, C0:, p * P:(p + 1) * P]

            def half_views(x, p, h):
                return x[:, p, T0:].rearrange("p (n two h) -> p n two h", two=2, h=h)

            for kind, i in steps:
                if (kind, i) == first_use:
                    dve.wait_ge(*sig.small_in.at(small_in))
                if kind == "split":
                    PC.lo(dve, "dve", *i)
                elif kind == "adat":
                    lay, n = i
                    m = slice(4 * n, 4 * n + 4)
                    dve.wait_ge(*PT.ready(modulated_t(*i)))
                    acc = PT.tile(modulated_t(*i))[:, 0:8].rearrange("p (m s) -> p m s", s=2)
                    bias = par[:, A_BADA + 24 * lay + 4 * n:A_BADA + 24 * lay + 4 * n + 4].unsqueeze(2).to_broadcast([P, 4, 2])
                    dve.scalar_tensor_tensor(modulation[:, lay, m, :], acc, 1.0 if n in (2, 3) else 0.0, bias,
                                             ALU.add, ALU.add).then_inc(*PT.evac(modulated_t(*i)))
                elif kind == "h":
                    if i == 0:
                        for n in range(4):
                            dve.wait_ge(*PT.evacuated(modulated_t(l, n)))
                        if l == 0:
                            dve.wait_ge(*sig.x_in.at(32))
                    if l:
                        dve.wait_ge(*PT.ready(J("h", i)))
                    h = HF[i // 4][:, i % 4, :]
                    for s in range(2):
                        src = (PT.tile(J("h", i))[:, :] if l else h)[:, s * 256:(s + 1) * 256]
                        last = dve.tensor_scalar(h[:, s * 256:(s + 1) * 256], src, ada[:, 8 + i, s:s + 1],
                                                 ada[:, i, s:s + 1], ALU.mult, ALU.add)
                    if l:
                        last.then_inc(*PT.evac(J("h", i)))
                        if i % 2:
                            dve.wait_ge(*PT.evacuated(J("h", i)))
                            dve.engine_nop().then_inc(*sig.h_f32.one())
                    elif i % 2:
                        last.then_inc(*sig.h_f32.one())
                elif kind == "hsplit":
                    k = slice(2 * i, 2 * i + 2)
                    if i != 2:
                        dve.wait_ge(*sig.x_hi.at(i + 1))
                        dve.tensor_tensor(HL[:, k, :], HF[i // 2][:, 2 * (i % 2):2 * (i % 2) + 2, :],
                                          HH[:, k, :].bitcast(F32), ALU.subtract).then_inc(*sig.h_ready.one())
                elif kind == "ysplit":
                    b, k = i
                    dve.wait_ge(*sig.y_hi.at(4 * "sag".index(b) + k + 1))
                    dve.tensor_tensor(YL[:, k, T0:], {"s": YS, "a": YA, "g": YG}[b][:, k, T0:],
                                      YH[:, k, T0:].bitcast(F32), ALU.subtract).then_inc(*sig.y_lo.one())
                elif kind == "msplit":
                    k = slice(2 * i, 2 * i + 2)
                    dve.wait_ge(*sig.m_hi.at(i + 1))
                    dve.tensor_tensor(HL[:, k, T0:], mT[:, k, T0:], HH[:, k, T0:].bitcast(F32), ALU.subtract)\
                        .then_inc(*sig.m_lo.one())
                elif kind == "su":
                    dve.wait_ge(*PJ.ready(J("su", i)))
                    dve.wait_ge(*PJ.evacuated(J("sg", i)))
                    dve.tensor_tensor(YS[:, i, T0:], PJ.tile(J("su", i))[:, 0:NT], YS[:, i, T0:], ALU.mult)\
                        .then_inc(*PJ.evac(J("su", i)))
                elif kind == "z":
                    b = (BF, BB)[i // 2][:, i % 2, :]
                    dve.wait_ge(*sig.z_abs.at(i + 1))
                    dve.tensor_scalar(b, PT.tile(J("z", i))[:, :], par[:, A_ABF + i:A_ABF + i + 1], 0.0,
                                      ALU.add, ALU.min).then_inc(*PT.evac(J("z", i)))
                elif kind == "decay":
                    dve.wait_ge(*sig.soft.at(1))
                    for n in range(4):
                        dve.wait_ge(*PT.evacuated(J("z", n)))
                    dve.tensor_tensor(BF[:], BF[:], DQ, ALU.subtract)
                    link(dve.tensor_tensor(BB[:], BB[:], DK, ALU.subtract))
                    for d in range(2):
                        for p in range(2):
                            for c in range(NCH):
                                b = (BF, BB)[d][:, p, c * P:(c + 1) * P]
                                if d:
                                    b = b[:, ::-1]
                                last = dve.tensor_tensor_scan(b, one.to_broadcast([P, P]), b, 0.0, ALU.mult, ALU.add)
                    link(last)
                elif kind == "rstd":
                    n = slice(0, TOK) if i == 0 else slice(T0, TOK)
                    x = K[:, n] if i == 0 else Q[:, i - 1, n]
                    w = A_KN if i == 0 else A_QN
                    rstd = sq(i)[:, 0:(TOK if i == 0 else NT)]
                    dve.wait_ge(*sig.head_rstd.at(i + 1))
                    dve.scalar_tensor_tensor(x, x, par[:, w:w + 1], rstd, ALU.mult, ALU.mult).then_inc(*sig.normed.one())
                elif kind == "rot":
                    x = K[:, 256:512] if i == 0 else Q[:, i - 1, 256:512]
                    t = sq(i)[:, 0:256]
                    dve.wait_ge(*PT.ready(J("rot", i)))
                    dve.tensor_tensor(t, PT.tile(J("rot", i))[:, 0:256], consts[:, C_SIN:C_SIN + 256], ALU.mult)\
                        .then_inc(*PT.evac(J("rot", i)))
                    link(dve.tensor_tensor(x, x, consts[:, C_COS:C_COS + 256], ALU.mult))
                    dve.tensor_tensor(x, x, t, ALU.add).then_inc(*sig.roped.one())
                elif kind == "score":
                    n = 256 * (units[i][0] + 1)
                    for u in range(2):
                        dve.wait_ge(*PS.ready(J("score", i, u)))
                        link(dve.reduce_max(small[:, i % 2, u:u + 1], PS.tile(J("score", i, u))[:, 0:n], AX.X))
                        dve.tensor_scalar(small[:, i % 2, 2 + u:3 + u], small[:, i % 2, u:u + 1], -0.125, None,
                                          ALU.mult).then_inc(*sig.neg_max.one())
                elif kind == "sums":
                    for u in range(2):
                        dve.wait_ge(*PS.evacuated(J("score", i, u)))
                        if i:
                            dve.wait_ge(*PT.ready(J("turn", i - 1, u)))
                        link(dve.reciprocal(small[:, i % 2, 6 + u:7 + u], small[:, i % 2, 4 + u:5 + u]))
                        dve.tensor_scalar(diag[:, u, :], ident, small[:, i % 2, 6 + u:7 + u],
                                          None, ALU.mult).then_inc(*sig.probs.one())
                elif kind == "pv":
                    s, j, t = units[i]
                    tok = s * 256 + t * P
                    dve.wait_ge(*PJ.ready(J("pv", i)))
                    if i == 0:
                        dve.wait_ge(*PJ.evacuated(J("ag", 3)))
                    dve.tensor_tensor(YA[:, j, tok:tok + P], PJ.tile(J("pv", i))[:, 0:P], YA[:, j, tok:tok + P],
                                      ALU.mult).then_inc(*PJ.evac(J("pv", i)))
                elif kind == "key":
                    b, edge = ((BF, 127), (BB, 0))[i]
                    bv = b[:].rearrange("p a (c t) -> p a c t", t=P)
                    dk = DK.rearrange("p a (c t) -> p a c t", t=P)
                    if i:
                        dve.wait_ge(*PT.ready(J("keyt", 0, 1)))
                    for p in range(2):
                        last = dve.tensor_tensor(dk[:, p], bv[:, p, :, edge:edge + 1].to_broadcast([P, NCH, P]),
                                                 bv[:, p], ALU.subtract)
                    last.then_inc(*sig.key_diff.one())
                    dve.wait_ge(*sig.key_exp.at(i + 1))
                    dve.wait_ge(*PJ.evacuated(J("gk", 1)))
                    dve.tensor_tensor(DK, DK, GK[:], ALU.mult).then_inc(*sig.keys.one())
                elif kind == "kv":
                    dve.wait_ge(*PT.ready(J("kv", i)))
                    for d in range(2):
                        c = (0, 1, 2)[i] if d == 0 else (1, 0, 3)[i]
                        for p in range(2):
                            n = 2 * d + p
                            kv = PT.tile(J("kv", i))[:, n * P:(n + 1) * P]
                            if i == 0:
                                last = dve.tensor_copy(S[:, n, 0, :], kv)
                            else:
                                last = dve.scalar_tensor_tensor(S[:, n, i, :], S[:, n, i - 1, :], ED[:, n, c:c + 1], kv,
                                                                ALU.mult, ALU.add)
                    last.then_inc(*PT.evac(J("kv", i)))
                    dve.wait_ge(*PT.evacuated(J("kv", i)))
                elif kind == "diag":
                    eye = ident.unsqueeze(1).to_broadcast([P, NC, P])
                    for p, u in ((0, 0), (0, 1), (1, 0), (1, 1)):
                        job = J("diag", 0, p, u)
                        dve.wait_ge(*PT.ready(job))
                        acc = PT.tile(job)[:, 0:NT].rearrange("p (c t) -> p c t", t=P)
                        dve.scalar_tensor_tensor(att_of(p, u), acc, 2.0, eye, ALU.mult, ALU.mult).then_inc(*PT.evac(job))
                elif kind == "diff":
                    h, p = LEVELS[i // 2], i % 2
                    if i == 0:
                        dve.wait_ge(*PT.ready(J("keyt", 1, 1)))
                        dve.wait_ge(*PJ.evacuated(J("gq", 1)))
                    elif i > 1:
                        dve.wait_ge(*PT.ready(J("pairs", i - 2, p, 1)))
                    f, b, q, k = (half_views(x, p, h) for x in (BF, BB, DQ, DK))
                    n = [P, NT // (2 * h), h]
                    fe = f[:, :, 0, h - 1:h].to_broadcast(n)
                    be = b[:, :, 1, 0:1].to_broadcast(n)
                    dve.tensor_tensor(q[:, :, 1, :], f[:, :, 1, :], fe, ALU.subtract)
                    dve.tensor_tensor(q[:, :, 0, :], b[:, :, 0, :], be, ALU.subtract)
                    dve.tensor_tensor(k[:, :, 0, :], fe, f[:, :, 0, :], ALU.subtract)
                    dve.tensor_tensor(k[:, :, 1, :], be, b[:, :, 1, :], ALU.subtract).then_inc(*sig.lev_diff.one())
                elif kind == "scale":
                    dve.wait_ge(*sig.lev_exp.at(i + 1))
                    dve.tensor_tensor(DQ[:, i % 2, T0:], DQ[:, i % 2, T0:], GQ[:, i % 2, T0:], ALU.mult)\
                        .then_inc(*sig.lev_q.one())
                elif kind == "pairs":
                    lev, p = i // 2, i % 2
                    m = consts[:, C_MASK + lev * P:C_MASK + (lev + 1) * P].bitcast(I32).unsqueeze(1).to_broadcast([P, NC, P])
                    for u in range(2):
                        job = J("pairs", i, p, u)
                        dve.wait_ge(*PT.ready(job))
                        acc = PT.tile(job)[:, 0:NT].rearrange("p (c t) -> p c t", t=P)
                        if lev == 0:
                            dve.wait_ge(*PT.evacuated(J("diag", 0, p, u)))
                        dve.copy_predicated(att_of(p, u), m, acc).then_inc(*PT.evac(job))
                elif kind == "query":
                    for d, b in enumerate((BF, BB)):
                        dve.wait_ge(*sig.query_exp.at(d + 1))
                        dve.tensor_tensor(b[:, :, T0:], b[:, :, T0:], GQ[:, :, T0:], ALU.mult).then_inc(*sig.queries.one())
                elif kind == "svn":
                    dve.wait_ge(*sig.rows_in.at(16))
                    for t in range(C0, 4):
                        dve.wait_ge(*PJ.ready(J("sv", t)))
                        link(dve.bn_stats(stats[:, t, 0:6], PJ.tile(J("sv", t))[:, :]))
                        dve.bn_aggr(stats[:, t, 12:14], stats[:, t, 0:6]).then_inc(*sig.sv_stat.one())
                    dve.wait_ge(*sig.sv_root.at(1))
                    link(dve.reciprocal(rstd4[:, C0:, 0:1], rstd4[:, C0:, 0:1]))
                    for t in range(C0, 4):
                        acc, g, b = PJ.tile(J("sv", t))[:, :], rows[:, R_G:R_G + 512], rows[:, R_B:R_B + 512]
                        if l:
                            acc, g, b = (x.rearrange("p (a c) -> p a c", a=2) for x in (acc, g, b))
                        dve.scalar_tensor_tensor(vn(t), acc, stats[:, t, 12:13], g, ALU.subtract, ALU.mult)\
                            .then_inc(*PJ.evac(J("sv", t)))
                        dve.wait_ge(*PJ.evacuated(J("sv", t)))
                        dve.scalar_tensor_tensor(vn(t), vn(t), rstd4[:, t, 0:1], b, ALU.mult, ALU.add).then_inc(*sig.vn.one())
                elif kind == "mix":
                    dve.wait_ge(*PJ.ready(J("mix", i)))
                    acc = PJ.tile(J("mix", i))[:, 0:NT].rearrange("p (c t) -> p c t", t=P)
                    bias = rows[:, R_SB + i * P:R_SB + (i + 1) * P].unsqueeze(1).to_broadcast([P, NC, P])
                    link(dve.tensor_tensor(acc, acc, bias, ALU.add))
                    dve.tensor_tensor(YS[:, i, T0:], YS[:, i, T0:], PJ.tile(J("mix", i))[:, 0:NT], ALU.mult)\
                        .then_inc(*PJ.evac(J("mix", i)))
                elif kind == "ostat":
                    d = DQK(i)[:, 0:NT]
                    dve.wait_ge(*sig.orstd.at(i + 1))
                    dve.scalar_tensor_tensor(d, PJ.tile(J("out", i))[:, 0:NT], par[:, A_ON:A_ON + 1], d,
                                             ALU.mult, ALU.mult).then_inc(*PJ.evac(J("out", i)))
                elif kind == "gg":
                    dve.wait_ge(*PJ.evacuated(J("gg", i)))
                    dve.wait_ge(*PJ.evacuated(J("out", i)))
                    dve.tensor_tensor(YG[:, i, T0:], YG[:, i, T0:], DQK(i)[:, 0:NT], ALU.mult).then_inc(*sig.y_gla.one())
                elif kind == "merge":
                    b, c = i
                    n = "sag".index(b) * 8 + c
                    g = SGM[:, n % 4, 0:NT]
                    dve.wait_ge(*PJ.evacuated(J("merge_gate", i)))
                    dve.wait_ge(*PS.ready(J("br", b, c)))
                    acc = PS.tile(J("br", b, c))[:, 0:NT]
                    if b == "s":
                        dve.tensor_tensor(mT[:, c, T0:], acc, g, ALU.mult).then_inc(*PS.evac(J("br", b, c)))
                    else:
                        link(dve.tensor_tensor(TMP[:, c % 2, 0:NT], acc, g, ALU.mult))
                        last = dve.tensor_tensor(mT[:, c, T0:], mT[:, c, T0:], TMP[:, c % 2, 0:NT], ALU.add)
                        last.then_inc(*PS.evac(J("br", b, c)))
                elif kind == "finish":
                    h = i
                    if h == 0:
                        dve.wait_ge(*sig.post_in.at(16 * (4 if l == 0 else 2)))
                        for s in range(C0 // 2, 2):
                            dve.wait_ge(*PT.evacuated(J("growb", s, 1)))
                    for t in range(C0, 4):
                        banks, job = out_bank(t, h), J("final", t, h)
                        x = xres(t)
                        xh = x[:, h * 512:(h + 1) * 512]
                        dve.wait_ge(*banks.ready(job))
                        dve.tensor_tensor(TMP[:, t % 2, :], banks.tile(job)[:, :], gateb[:, t // 2, h, :], ALU.mult)\
                            .then_inc(*banks.evac(job))
                        dve.wait_ge(*banks.evacuated(job))
                        link(dve.scalar_tensor_tensor(xh, xh, ALPHA, TMP[:, t % 2, :], ALU.mult, ALU.add))
                        stat = dve.bn_stats(stats[:, t, 6 * h:6 * h + 6], xh)
                        if h:
                            link(stat)
                            dve.bn_aggr(stats[:, t, 12:14], stats[:, t, 0:12].rearrange("p (a b) -> p a b", a=2))\
                                .then_inc(*sig.x_stat.one())
                    for t in range(C0, 4) if h else ():
                        x = xres(t)
                        dve.wait_ge(*sig.x_root.at(t - C0 + 1))
                        link(dve.reciprocal(rstd4[:, t, 1:2], rstd4[:, t, 1:2]))
                        link(dve.scalar_tensor_tensor(x, x, stats[:, t, 12:13], post[0][:], ALU.subtract, ALU.mult))
                        scaled = dve.scalar_tensor_tensor(x, x, rstd4[:, t, 1:2], post[1][:], ALU.mult, ALU.add)
                    if h:
                        link(scaled)

        @block.gpsimd
        def _(pool):
            for kind, i in steps:
                if kind == "split":
                    PC.lo(pool, "pool", *i)
                elif kind == "hsplit" and i == 2:
                    pool.wait_ge(*sig.x_hi.at(3))
                    pool.tensor_tensor(HL[:, 4:6, :], HF[1][:, 0:2, :], HH[:, 4:6, :].bitcast(F32), ALU.subtract)\
                        .then_inc(*sig.h_ready_pool.one())
                elif kind == "scale":
                    if i == 0:
                        pool.wait_ge(*PJ.evacuated(J("gk", 1)))
                    pool.wait_ge(*sig.lev_exp.at(i + 1))
                    pool.tensor_tensor(DK[:, i % 2, T0:], DK[:, i % 2, T0:], GK[:, i % 2, T0:], ALU.mult)\
                        .then_inc(*sig.lev_k.one())

        @block.sync
        def _(sp):
            if l == 0:
                sp.dma_start(silu_c[:], io["cond"]).then_inc(*sig.cond_in.dma())
                W.issue(sp, 1)
                sp.dma_start(consts[:], io["consts"]).then_inc(*sig.small_in.dma())
            sp.dma_start(par[:], io["params"][l]).then_inc(*sig.small_in.dma())
            if l == 0:
                W.issue(sp, NSLOT)
                for n in range(2):
                    sp.dma_start(HF[n], io["xT"][:, 4 * n:4 * n + 4, :]).then_inc(*sig.x_in.dma())
            sp.dma_start(rows[:], io["rows"][l]).then_inc(*sig.rows_in.dma())
            W.issue(sp, SLOT_OF[f"{l}.wo0"] - 1)
            sp.wait_ge(*PJ.evacuated(J("out", 3)))
            if l == 0:
                sp.wait_ge(*PJ.ready(J("mix", 3)))
                sp.dma_start(xctx[:], io["ctx_rows"]).then_inc(*sig.post_in.dma())
                sp.dma_start(xlat[:], io["x_rows"]).then_inc(*sig.post_in.dma())
            for n in range(2):
                sp.dma_start(post[n][:], io["post"][l, n].partition_broadcast(P)).then_inc(*sig.post_in.dma())
            W.issue(sp, SLOT_OF[f"{l}.wo1"] + 1 + NSLOT)



def mixer_schedule():
    steps = [("norm", t) for t in range(2)] + [("turnx", i) for i in range(4)]
    steps += [("f", 0)] + [("rec", i) for i in range(4)] + [("q", i) for i in range(4)] + [("cum", 0)]
    steps += [("lambda", 0)] + [("k", i) for i in range(4)] + [("ri", i) for i in range(4)] + [("lru", 0)] + [("v", t) for t in range(2)]
    for i in range(8 + 2):
        steps += [s for s in (("sums", i - 1), ("score", i), ("turn", i - 1), ("pv", i - 2)) if 0 <= s[1] < 8]
        if i % 2 == 0 and i < 8:
            steps += [("gat", i // 2)]
    return steps + [("out", t) for t in range(2)]


def mixer(nc, io, W, EW, jobs, sig, par, xlat):
    T = M_TOK
    PJ, PS, PT = jobs
    J = lambda name, *i: f"x.{name}" + "".join(f".{x}" for x in i)
    steps = mixer_schedule()
    units = [(j, t) for j in range(4) for t in range(2)]

    with ExitStack() as ctx:
        def sb(name, shape, dt=F32):
            return ctx.enter_context(nc.sbuf_tensor(f"x_{name}", shape, dt))

        ident = par[:, M_ID:M_ID + P]
        eps, one = par[:, M_EPS:M_EPS + 1], par[:, M_ONE:M_ONE + 1]
        XS = sb("scaled", [P, 2, D])
        hT = sb("hT", [P, KT, T])
        Q, K = sb("q", [P, 4, T]), sb("k", [P, 4, T])
        V = sb("v", [P, 2, 512])
        RP = sb("rec_padded", [P, 4, T + 3])
        Y = sb("conv", [P, 4, T])
        RG, IG = sb("r_gate", [P, 4, T]), sb("i_gate", [P, 4, T])
        MUL = XS[:].rearrange("p t (i c) -> p (t i) c", c=T)[:, 0:4]
        CAT = sb("mixed", [P, 8, T])
        CUM = sb("cum_decay", [8, T])
        FT = sb("f_tmp", [8, T])
        CT = sb("cum_decay_t", [P, 2, 8])
        CB = sb("cum_decay_rows", [P, 8, T])
        LG = sb("logits", [P, 2, T])
        PR, PTB = sb("probs", [P, 2, 2, T]), sb("probs_t", [P, 2, 2, T])
        small = sb("small", [P, 2, 8])
        st = sb("stats", [P, 8])
        lam = sb("lambda", [P, 16])
        block = ctx.enter_context(nc.Block())

        @block.tensor
        def _(pe):
            held = {}

            def slot(name):
                if name not in held:
                    for half in range(2):
                        pe.wait_ge(*W.has_landed(f"x.{name}", half))
                    held[name] = W.slot(f"x.{name}").rearrange("p (k c) -> p k c", c=512)
                return held[name]

            def used(name, job):
                W.last_read(f"x.{name}", PJ.ready(job))

            pe.wait_ge(*sig.small_in.at(32))
            for kind, i in steps:
                if kind == "turnx":
                    if i == 0:
                        pe.wait_ge(*sig.scaled.at(2))
                    acc = PT.open(pe, J("turnx", i))
                    for n in range(4):
                        k, t = 2 * i + n // 2, n % 2
                        last = pe.transpose(acc[:, n * P:(n + 1) * P], XS[:, t, k * P:(k + 1) * P], ident)
                    last.then_inc(*PT.done())
                elif kind == "f":
                    pe.wait_ge(*sig.par_in.at(32))
                    pe.wait_ge(*PT.evacuated(J("turnx", 2)))
                    pe.wait_ge(*PT.evacuated(J("turnx", 3)))
                    acc = PT.open(pe, J("f"))
                    for k in range(KT):
                        last = pe.matmul(acc[0:8, 0:T], par[:, M_WF + 8 * k:M_WF + 8 * k + 8], hT[:, k, :],
                                         start=(k == 0), stop=(k == KT - 1))
                    last.then_inc(*PT.done())
                elif kind in ("rec", "q", "k", "gat"):
                    w = slot(kind)
                    acc = PJ.open(pe, J(kind, i))
                    for k in range(KT):
                        last = pe.matmul(acc[:, 0:T], w[:, k, i * P:(i + 1) * P], hT[:, k, :],
                                         start=(k == 0), stop=(k == KT - 1))
                    last.then_inc(*PJ.done())
                    used(kind, J(kind, i))
                elif kind in ("v", "out"):
                    src = hT if kind == "v" else CAT
                    if kind == "out" and i == 0:
                        pe.wait_ge(*sig.lru_seq.at(1))
                        pe.wait_ge(*PJ.evacuated(J("pv", 6)))
                        pe.wait_ge(*PJ.evacuated(J("pv", 7)))
                    for h in range(1 if kind == "v" else 2):
                        name = "v" if kind == "v" else f"wo{h}"
                        job = J("v", i) if kind == "v" else J("out", i, h)
                        w = slot(name)
                        acc = PJ.open(pe, job)
                        for k in range(KT):
                            last = pe.matmul(acc[:, :], src[:, k, i * P:(i + 1) * P], w[:, k, :],
                                             start=(k == 0), stop=(k == KT - 1))
                        last.then_inc(*PJ.done())
                        used(name, job)
                elif kind == "ri":
                    pe.wait_ge(*sig.conv.at(i + 1))
                    acc = PT.open(pe, J("ri", i))
                    for n, w in enumerate((M_WA, M_WX)):
                        last = pe.matmul(acc[:, n * T:(n + 1) * T], par[:, w + i * P:w + (i + 1) * P], Y[:, i, :],
                                         start=True, stop=True)
                    last.then_inc(*PT.done())
                elif kind == "cum":
                    pe.wait_ge(*sig.cum.at(1))
                    acc = PT.open(pe, J("ct"))
                    for t in range(2):
                        last = pe.matmul(acc[:, 8 * t:8 * t + 8], CUM[0:8, t * P:(t + 1) * P], ident[0:8, 0:8],
                                         start=True, stop=True)
                    last.then_inc(*PT.done())
                    for n in range(4):
                        acc = PT.open(pe, J("cb", n))
                        for h in (2 * n, 2 * n + 1):
                            last = pe.matmul(acc[:, (h % 2) * T:(h % 2 + 1) * T],
                                             par[0:8, M_SEL + h * P:M_SEL + (h + 1) * P], CUM[0:8, :],
                                             start=True, stop=True)
                        last.then_inc(*PT.done())
                elif kind == "score":
                    j, t = units[i]
                    n = P * (t + 1)
                    if i == 0:
                        pe.wait_ge(*PJ.evacuated(J("q", 3)))
                        pe.wait_ge(*PJ.evacuated(J("k", 3)))
                    for u in range(2):
                        acc = PS.open(pe, J("score", i, u))
                        pe.matmul(acc[:, 0:n], Q[64 * u:64 * u + 64, j, t * P:(t + 1) * P], K[64 * u:64 * u + 64, j, 0:n],
                                  start=True, stop=True).then_inc(*PS.done())
                elif kind == "turn":
                    for u in range(2):
                        pe.wait_ge(*sig.probs.at(2 * i + u + 1))
                        acc = PT.open(pe, J("turn", i, u))
                        for b in range(units[i][1] + 1):
                            last = pe.transpose(acc[:, b * P:(b + 1) * P], PR[:, i % 2, u, b * P:(b + 1) * P], ident)
                        last.then_inc(*PT.done())
                elif kind == "pv":
                    j, t = units[i]
                    if i == 0:
                        pe.wait_ge(*PJ.evacuated(J("v", 0)))
                        pe.wait_ge(*PJ.evacuated(J("v", 1)))
                    acc = PJ.open(pe, J("pv", i))
                    for u in range(2):
                        pe.wait_ge(*PT.evacuated(J("turn", i, u)))
                        c = (2 * j + u) * 64
                        for b in range(t + 1):
                            last = pe.matmul(acc[64 * u:64 * u + 64, 0:P], V[:, b, c:c + 64],
                                             PTB[:, i % 2, u, b * P:(b + 1) * P], start=(b == 0), stop=(b == t))
                    last.then_inc(*PJ.done())

        @block.scalar
        def _(act):
            link = linker(act, sig.act_own)
            for kind, i in steps:
                if kind == "norm":
                    link(act.activation(XS[:, i, :], xlat[:, i, :], ACT.Square, scale=D ** -0.5, accum_out=st[:, i:i + 1]))
                    if i == 0:
                        act.wait_ge(*sig.small_in.at(32))
                    act.activation(st[:, 4 + i:5 + i], st[:, i:i + 1], ACT.Sqrt, bias=eps).then_inc(*sig.norm_root.one())
                elif kind == "lambda":
                    x = par[:, M_LAM:M_LAM + 4]
                    link(act.activation(lam[:, 0:4], x, ACT.Abs))
                    link(act.activation(lam[:, 0:4], lam[:, 0:4], ACT.Exp, scale=-1.0))
                    act.activation(lam[:, 0:4], lam[:, 0:4], ACT.Ln, bias=one).then_inc(*sig.lam.one())
                elif kind == "f":
                    act.wait_ge(*PT.ready(J("f")))
                    link(act.activation(FT[:], PT.tile(J("f"))[0:8, 0:T], ACT.Abs, bias=par[0:8, M_BF:M_BF + 1]))
                    link(act.activation(FT[:], FT[:], ACT.Exp, scale=-1.0))
                    act.activation(FT[:], FT[:], ACT.Ln, bias=one[0:8]).then_inc(*sig.fsoft.one())
                elif kind in ("rec", "q", "k", "v"):
                    dst = {"rec": RP[:, i, 3:3 + T], "q": Q[:, i, :], "k": K[:, i, :], "v": V[:, i % 2, :]}[kind]
                    act.wait_ge(*PJ.ready(J(kind, i)))
                    act.activation(dst, PJ.tile(J(kind, i))[:, 0:512 if kind == "v" else T], ACT.Copy)\
                        .then_inc(*PJ.evac(J(kind, i)))
                elif kind == "ri":
                    act.wait_ge(*PT.ready(J("ri", i)))
                    acc = PT.tile(J("ri", i))
                    act.activation(RG[:, i, :], acc[:, 0:T], ACT.Sigmoid, bias=par[:, M_BA + i:M_BA + i + 1])
                    act.activation(IG[:, i, :], acc[:, T:2 * T], ACT.Sigmoid, bias=par[:, M_BX + i:M_BX + i + 1])\
                        .then_inc(*PT.evac(J("ri", i)))
                elif kind == "lru":
                    act.wait_ge(*PT.evacuated(J("ri", 3)))
                    act.wait_ge(*sig.lam.at(2))
                    for n in range(4):
                        act.activation(MUL[:, n, :], RG[:, n, :], ACT.Tanh, scale=lam[:, 8 + n:9 + n])
                    for n in range(4):
                        last = act.activation(RG[:, n, :], RG[:, n, :], ACT.Exp, scale=lam[:, 4 + n:5 + n])
                    last.then_inc(*sig.gates_ri.one())
                    act.wait_ge(*sig.lru_mult.at(1))
                    act.activation(MUL[:], MUL[:], ACT.Sqrt).then_inc(*sig.gates_ri.one())
                elif kind == "gat":
                    act.wait_ge(*PJ.ready(J("gat", i)))
                    act.activation(CAT[:, 4 + i, :], PJ.tile(J("gat", i))[:, 0:T], ACT.Gelu_apprx_tanh)\
                        .then_inc(*PJ.evac(J("gat", i)))
                elif kind == "score":
                    n = P * (units[i][1] + 1)
                    for u in range(2):
                        act.wait_ge(*sig.neg_max.at(2 * i + u + 1))
                        act.activation(PR[:, i % 2, u, 0:n], LG[:, u, 0:n], ACT.Exp, bias=small[:, i % 2, 2 + u:3 + u],
                                       accum_out=small[:, i % 2, 4 + u:5 + u]).then_inc(*sig.route_exp.one())
                elif kind == "turn":
                    n = P * (units[i][1] + 1)
                    for u in range(2):
                        act.wait_ge(*PT.ready(J("turn", i, u)))
                        if i >= 2:
                            act.wait_ge(*PJ.ready(J("pv", i - 2)))
                        act.activation(PTB[:, i % 2, u, 0:n], PT.tile(J("turn", i, u))[:, 0:n], ACT.Copy)\
                            .then_inc(*PT.evac(J("turn", i, u)))

        @block.vector
        def _(dve):
            link = linker(dve, sig.dve_own)
            dve.wait_ge(*sig.small_in.at(32))
            dve.memset(RP[:, :, 0:3], 0.0)
            for kind, i in steps:
                if kind == "norm":
                    dve.wait_ge(*sig.norm_root.at(i + 1))
                    link(dve.reciprocal(st[:, 4 + i:5 + i], st[:, 4 + i:5 + i]))
                    dve.tensor_scalar(XS[:, i, :], xlat[:, i, :], st[:, 4 + i:5 + i], None, ALU.mult)\
                        .then_inc(*sig.scaled.one())
                elif kind == "turnx":
                    dve.wait_ge(*PT.ready(J("turnx", i)))
                    g = par[:, M_NORM1 + 2 * i:M_NORM1 + 2 * i + 2].unsqueeze(2).to_broadcast([P, 2, T])
                    acc = PT.tile(J("turnx", i))[:, :].rearrange("p (k t) -> p k t", k=2)
                    dve.tensor_tensor(hT[:, 2 * i:2 * i + 2, :], acc, g, ALU.mult).then_inc(*PT.evac(J("turnx", i)))
                elif kind == "lambda":
                    dve.wait_ge(*sig.lam.at(1))
                    link(dve.tensor_scalar(lam[:, 12:16], par[:, M_LAM:M_LAM + 4], -1.0, 0.0, ALU.mult, ALU.max))
                    link(dve.tensor_tensor(lam[:, 12:16], lam[:, 12:16], lam[:, 0:4], ALU.add))
                    dve.tensor_scalar(lam[:, 4:8], lam[:, 12:16], -8.0, None, ALU.mult)
                    dve.tensor_scalar(lam[:, 8:12], lam[:, 12:16], 8.0, None, ALU.mult).then_inc(*sig.lam.one())
                elif kind == "f":
                    dve.wait_ge(*sig.fsoft.at(1))
                    dve.tensor_scalar(CUM[:], PT.tile(J("f"))[0:8, 0:T], par[0:8, M_BF:M_BF + 1], 0.0,
                                      ALU.add, ALU.min).then_inc(*PT.evac(J("f")))
                    dve.wait_ge(*PT.evacuated(J("f")))
                    link(dve.tensor_tensor(CUM[:], CUM[:], FT[:], ALU.subtract))
                    dve.tensor_tensor_scan(CUM[:], one[0:8].to_broadcast([8, T]), CUM[:], 0.0, ALU.mult, ALU.add)\
                        .then_inc(*sig.cum.one())
                elif kind == "rec":
                    dve.wait_ge(*PJ.evacuated(J("rec", i)))
                    w = lambda n: par[:, M_CONVW + 4 * i + n:M_CONVW + 4 * i + n + 1]
                    link(dve.tensor_scalar(Y[:, i, :], RP[:, i, 0:T], w(0), par[:, M_CONVB + i:M_CONVB + i + 1],
                                           ALU.mult, ALU.add))
                    for n in range(1, 4):
                        ins = dve.scalar_tensor_tensor(Y[:, i, :], RP[:, i, n:n + T], w(n), Y[:, i, :], ALU.mult, ALU.add)
                        if n < 3:
                            link(ins)
                    ins.then_inc(*sig.conv.one())
                elif kind == "cum":
                    dve.wait_ge(*PT.ready(J("ct")))
                    dve.tensor_copy(CT[:], PT.tile(J("ct"))[:, 0:16].rearrange("p (t h) -> p t h", t=2))\
                        .then_inc(*PT.evac(J("ct")))
                    for n in range(4):
                        dve.wait_ge(*PT.ready(J("cb", n)))
                        dve.tensor_copy(CB[:, 2 * n:2 * n + 2, :],
                                        PT.tile(J("cb", n))[:, :].rearrange("p (h t) -> p h t", h=2))\
                            .then_inc(*PT.evac(J("cb", n)))
                elif kind == "lru":
                    dve.wait_ge(*sig.gates_ri.at(1))
                    link(dve.tensor_tensor(CAT[:, 0:4, :], RG[:], RG[:], ALU.mult))
                    link(dve.scalar_tensor_tensor(MUL[:], CAT[:, 0:4, :], 1.0, MUL[:], ALU.add, ALU.mult))
                    dve.tensor_tensor(IG[:], IG[:], Y[:], ALU.mult).then_inc(*sig.lru_mult.one())
                    dve.wait_ge(*sig.lru_mult.at(1))
                    dve.wait_ge(*sig.gates_ri.at(2))
                    link(dve.tensor_tensor(IG[:], IG[:], MUL[:], ALU.mult))
                    for n in range(4):
                        last = dve.tensor_tensor_scan(Y[:, n, :], RG[:, n, :], IG[:, n, :], 0.0, ALU.mult, ALU.add)
                    link(last)
                elif kind == "gat":
                    if i == 3:
                        dve.wait_ge(*PJ.evacuated(J("gat", 3)))
                        dve.tensor_tensor(CAT[:, 4:8, :], CAT[:, 4:8, :], Y[:], ALU.mult).then_inc(*sig.lru_seq.one())
                elif kind == "score":
                    j, t = units[i]
                    n = P * (t + 1)
                    if i == 0:
                        dve.wait_ge(*sig.par_in.at(32))
                    for u in range(2):
                        h = 2 * j + u
                        lg = LG[:, u, 0:n]
                        if i:
                            dve.wait_ge(*sig.route_exp.at(2 * (i - 1) + u + 1))
                        link(dve.tensor_scalar(lg, CB[:, h, 0:n], CT[:, t, h:h + 1], -1.0, ALU.subtract, ALU.mult))
                        diag = LG[:, u, n - P:n]
                        link(dve.tensor_tensor(diag, diag, par[:, M_CAUSAL:M_CAUSAL + P], ALU.add))
                        dve.wait_ge(*PS.ready(J("score", i, u)))
                        dve.scalar_tensor_tensor(lg, PS.tile(J("score", i, u))[:, 0:n], 0.125, lg, ALU.mult, ALU.add)\
                            .then_inc(*PS.evac(J("score", i, u)))
                        dve.wait_ge(*PS.evacuated(J("score", i, u)))
                        link(dve.reduce_max(small[:, i % 2, u:u + 1], lg, AX.X))
                        dve.tensor_scalar(small[:, i % 2, 2 + u:3 + u], small[:, i % 2, u:u + 1], -1.0, None,
                                          ALU.mult).then_inc(*sig.neg_max.one())
                elif kind == "sums":
                    n = P * (units[i][1] + 1)
                    for u in range(2):
                        dve.wait_ge(*sig.route_exp.at(2 * i + u + 1))
                        link(dve.reciprocal(small[:, i % 2, 6 + u:7 + u], small[:, i % 2, 4 + u:5 + u]))
                        dve.tensor_scalar(PR[:, i % 2, u, 0:n], PR[:, i % 2, u, 0:n], small[:, i % 2, 6 + u:7 + u],
                                          None, ALU.mult).then_inc(*sig.probs.one())
                elif kind == "pv":
                    j, t = units[i]
                    dve.wait_ge(*PJ.ready(J("pv", i)))
                    dve.tensor_copy(CAT[:, j, t * P:(t + 1) * P], PJ.tile(J("pv", i))[:, 0:P])\
                        .then_inc(*PJ.evac(J("pv", i)))
                elif kind == "out":
                    for h in range(2):
                        dve.wait_ge(*PJ.ready(J("out", i, h)))
                        x = xlat[:, i, h * 512:(h + 1) * 512]
                        dve.tensor_tensor(x, x, PJ.tile(J("out", i, h))[:, :], ALU.add).then_inc(*PJ.evac(J("out", i, h)))

        @block.sync
        def _(sp):
            for a, b in ((0, P), (M_EPS, M_WF)):
                sp.dma_start(par[:, a:b], io["mixer_params"][:, a:b]).then_inc(*sig.small_in.dma())
            for a, b in ((P, M_EPS), (M_WF, M_W)):
                sp.dma_start(par[:, a:b], io["mixer_params"][:, a:b]).then_inc(*sig.par_in.dma())
            W.issue(sp, len(STREAM))
            EW.issue(sp, OWN_PARTS)



def work(first, count):
    end = first + count
    s = [("gather", first // E), ("split", (first, 0)), ("split", (first, 1))]
    for n in range(first, end + 1):
        if n > first:
            s += [("turnh", n - 1)]
        if n + 1 < end:
            s += [("split", (n + 1, 0))]
        if n < end:
            s += [("gu", n)]
        if n % E == 1 and n - E > first:
            s += [("scatter", n // E - 1)]
        if n + 1 < end:
            s += [("split", (n + 1, 1))]
        if n > first:
            s += [("down", n - 1)]
            if n % E == 0:
                s += [("rows", n // E - 1)]
        if n < end:
            s += [("split", (n, 2))]
        if n % E == E - 2 and n + 2 < end:
            s += [("gather", n // E + 1)]
    return s + [("scatter", end // E - 1)]


MAIN_STEPS = work(0, G * E)
OVER_STEPS = work(G * E, E)


class ExpertWeights:

    def __init__(self, ctx, nc, dram, ring):
        self.dram = dram
        own = ctx.enter_context(nc.sbuf_tensor("expert_parts", [P, OWN_PARTS, PART], F32))
        flat = ring[:].rearrange("p s c -> p (s c)")
        self.place = [own[:, n] for n in range(OWN_PARTS)]
        self.place += [flat[:, n * PART:(n + 1) * PART] for n in range(NSLOT * SLOT // PART)]
        self.landed = [ctx.enter_context(nc.semaphore(f"expert_part{i}_landed")) for i in range(len(self.place))]
        self.used = ctx.enter_context(nc.semaphore("experts_used"))
        self.half_used = ctx.enter_context(nc.semaphore("expert_half_used"))
        self.hi_written = ctx.enter_context(nc.semaphore("expert_hi_written"))
        self.lo_written = ctx.enter_context(nc.semaphore("expert_lo_written"))
        self.order = [i for kind, i in MAIN_STEPS + OVER_STEPS if kind == "split"]
        self.index = {x: n for n, x in enumerate(self.order)}
        self.issued = 0

    def split_places(self, ctx, nc):
        self.hi_ring, self.lo_ring = (ctx.enter_context(nc.sbuf_tensor(n, [P, 3, PART], F32R))
                                      for n in ("expert_hi", "expert_lo"))

    def issue(self, sp, upto, source=None):
        for n in range(self.issued, upto):
            place = n % len(self.place)
            if n >= len(self.place):
                sp.wait_ge(self.lo_written, n - len(self.place) + 1)
            i, part = self.order[n]
            src = self.dram[i] if source is None else source(i)
            sp.dma_start(self.place[place], src[:, part * PART:(part + 1) * PART]).then_inc(self.landed[place], 16)
        self.issued = upto

    def raw(self, i, part):
        return self.place[self.index[i, part] % len(self.place)]

    def hi(self, act, i, part, gu_done):
        n = self.index[i, part]
        act.wait_ge(self.landed[n % len(self.place)], 16 * (n // len(self.place) + 1))
        if i:
            act.wait_ge(*((self.half_used, i), gu_done, (self.used, i))[part])
        act.activation(self.hi_ring[:, part, :], self.raw(i, part), ACT.Copy).then_inc(self.hi_written, 1)

    def lo(self, dve, i, part):
        dve.wait_ge(self.hi_written, self.index[i, part] + 1)
        dve.tensor_tensor(self.lo_ring[:, part, :], self.raw(i, part), self.hi_ring[:, part, :].bitcast(F32),
                          ALU.subtract).then_inc(self.lo_written, 1)

    def take(self, pe, i, part):
        pe.wait_ge(self.lo_written, self.index[i, part] + 1)
        return tuple(r[:, part, :].rearrange("p (k c) -> p k c", c=D if part == 2 else 2 * FF)
                     for r in (self.hi_ring, self.lo_ring))


def experts(nc, io, out, EW, jobs, sig, par, xlat, store):
    T = M_TOK
    PJ, PS, PT = jobs
    J = lambda name, *i: f"e.{name}" + "".join(f".{x}" for x in i)
    NP = G + 1

    with ExitStack() as ctx:
        def sb(name, shape, dt=F32):
            return ctx.enter_context(nc.sbuf_tensor(f"e_{name}", shape, dt))

        ident = par[:, M_ID:M_ID + P]
        eps = par[:, M_EPS:M_EPS + 1]
        fin = sb("final_norm", [P, D])
        XS = sb("scaled", [P, 2, D])
        hT = sb("hT", [P, KT, T])
        L = sb("logits", [P, 2, 36])
        GP, G1, G2, OH = (sb(n, [P, 2, G]) for n in ("group_p", "group_eq", "group_t", "group_one_hot"))
        MX = sb("maxima", [P, 2, 16])
        PROD = sb("inner_products", [P, 2, G, E])
        IL, IP, I1, I2, O1, O2 = (sb(n, [P, 2, E]) for n in ("inner_logits", "inner_p", "eq", "t", "first", "second"))
        COMB = sb("combine", [P, 2, NP, E])
        RK = sb("rank", [P, 2, NP])
        OV = sb("over", [P, G])
        FLAG = sb("flag", [P, 4])
        FLAGI = sb("flag_int", [P, 2], I32)
        SELT = sb("select_t", [P, NP, 2, P])
        SEL = sb("select", [P, NP, 2, P])
        CS = sb("slot_combine", [P, NP, E])
        hT_flat = hT[:].rearrange("p k t -> p (k t)")
        XF = hT_flat[:, 0:D].rearrange("p (b k s) -> p b k s", b=2, s=P)
        YB = hT_flat[:, D:2 * D]
        XGH, XGL = (sb(n, [P, 2, KT, P], F32R) for n in ("gathered_hi", "gathered_lo"))
        HS, HG = sb("silu", [P, 2, FF]), sb("hidden", [P, 2, FF])
        HTH, HTL = (sb(n, [P, 2, 2, P], F32R) for n in ("hidden_t_hi", "hidden_t_lo"))
        st = sb("stats", [P, 8])

        main_work = [("norm", 0), ("norm", 1)] + [("turnx", i) for i in range(4)]
        main_work += [("route", 0), ("route", 1), ("rank", 0)]
        main_work = main_work[:2] + MAIN_STEPS[1:3] + main_work[2:] + [("gather", 0), ("sel", 0)] + MAIN_STEPS[3:]
        EW.split_places(ctx, nc)

        block = ctx.enter_context(nc.Block())

        def tensor_steps(pe, steps):
            for kind, i in steps:
                if kind == "turnx":
                    if i == 0:
                        pe.wait_ge(*sig.scaled.at(2))
                    acc = PT.open(pe, J("turnx", i))
                    for n in range(4):
                        k, t = 2 * i + n // 2, n % 2
                        last = pe.transpose(acc[:, n * P:(n + 1) * P], XS[:, t, k * P:(k + 1) * P], ident)
                    last.then_inc(*PT.done())
                elif kind == "route":
                    if i == 0:
                        pe.wait_ge(*PT.evacuated(J("turnx", 2)))
                        pe.wait_ge(*PT.evacuated(J("turnx", 3)))
                    acc = PT.open(pe, J("route", i))
                    for k in range(KT):
                        last = pe.matmul(acc[:, 0:36], hT[:, k, i * P:(i + 1) * P], par[:, M_WR + 36 * k:M_WR + 36 * (k + 1)],
                                         start=(k == 0), stop=(k == KT - 1))
                    last.then_inc(*PT.done())
                elif kind == "rank":
                    pe.wait_ge(*sig.one_hot.at(1))
                    acc = PT.open(pe, J("rank"))
                    tri, ones = par[:, M_TRI:M_TRI + P], par[:, M_ONES:M_ONES + P]
                    pe.matmul(acc[:, 0:4], tri, OH[:, 0, :], start=True, stop=True)
                    pe.matmul(acc[:, 4:8], tri, OH[:, 1, :], start=True, stop=False)
                    pe.matmul(acc[:, 4:8], ones, OH[:, 0, :], start=False, stop=True)
                    pe.matmul(acc[:, 8:12], ones, OH[:, 0, :], start=True, stop=False)
                    pe.matmul(acc[:, 8:12], ones, OH[:, 1, :], start=False, stop=True).then_inc(*PT.done())
                elif kind == "sel":
                    acc = PT.open(pe, J("slotw"))
                    for n in range(NP):
                        for t in range(2):
                            last = pe.matmul(acc[:, n * E:(n + 1) * E], SELT[:, n, t, :], COMB[:, t, n, :],
                                             start=(t == 0), stop=(t == 1))
                    last.then_inc(*PT.done())
                    for b in range(3):
                        acc = PT.open(pe, J("sel", b))
                        for n in range(4 * b, min(4 * b + 4, 2 * NP)):
                            last = pe.transpose(acc[:, (n % 4) * P:(n % 4 + 1) * P], SELT[:, n // 2, n % 2, :], ident)
                        last.then_inc(*PT.done())
                elif kind == "gather":
                    if i == 0:
                        pe.wait_ge(*sig.selected.at(1))
                    for b in range(2):
                        acc = PT.open(pe, J("gather", i, b))
                        for n in range(4):
                            k = 4 * b + n
                            for t in range(2):
                                last = pe.matmul(acc[:, n * P:(n + 1) * P], XS[:, t, k * P:(k + 1) * P], SELT[:, i, t, :],
                                                 start=(t == 0), stop=(t == 1))
                        last.then_inc(*PT.done())
                elif kind == "gu":
                    p = i // E
                    if i % E == 0:
                        pe.wait_ge(*sig.gathered.at(2 * p + 2))
                    acc = PJ.open(pe, J("gu", i))
                    for part in range(2):
                        wh, wl = EW.take(pe, i, part)
                        for n in range(4):
                            k = 4 * part + n
                            last = split_product(pe, acc[:, :], (XGH[:, p % 2, k, :], XGL[:, p % 2, k, :]),
                                                 (wh[:, n], wl[:, n]), k == 0, k == KT - 1)
                        if part == 0:
                            last.then_inc(EW.half_used, 1)
                    last.then_inc(*PJ.done())
                elif kind == "turnh":
                    pe.wait_ge(*PJ.evacuated(J("gu", i)))
                    acc = PT.open(pe, J("turnh", i))
                    for f in range(2):
                        last = pe.transpose(acc[:, f * P:(f + 1) * P], HG[:, i % 2, f * P:(f + 1) * P], ident)
                    last.then_inc(*PT.done())
                elif kind == "down":
                    p, e = i // E, i % E
                    if e == 0:
                        for h in range(2):
                            PS.open(pe, J("y", p, h))
                    pe.wait_ge(*PT.evacuated(J("turnh", i)))
                    wh, wl = EW.take(pe, i, 2)
                    for h in range(2):
                        y, c = PS.tile(J("y", p, h)), slice(h * 512, (h + 1) * 512)
                        for f in range(2):
                            last = split_product(pe, y[:, :], (HTH[:, i % 2, f, :], HTL[:, i % 2, f, :]),
                                                 (wh[:, f, c], wl[:, f, c]), e == 0 and f == 0, e == E - 1 and f == 1)
                    last.then_inc(EW.used, 1)
                elif kind == "scatter":
                    pe.wait_ge(*sig.slots_w.at(i + 1))
                    for t in range(2):
                        for h in range(2):
                            acc = PT.open(pe, J("scatter", i, t, h))
                            pe.matmul(acc[:, :], SEL[:, i, t, :], YB[:, h * 512:(h + 1) * 512],
                                      start=True, stop=True).then_inc(*PT.done())

        def scalar_steps(act, steps):
            link = linker(act, sig.act_own)
            for kind, i in steps:
                if kind == "norm":
                    link(act.activation(XS[:, i, :], xlat[:, i, :], ACT.Square, scale=D ** -0.5, accum_out=st[:, i:i + 1]))
                    act.activation(st[:, 4 + i:5 + i], st[:, i:i + 1], ACT.Sqrt, bias=eps).then_inc(*sig.norm_root.one())
                elif kind == "route":
                    act.wait_ge(*sig.route_max.at(i + 1))
                    act.activation(GP[:, i, :], L[:, i, 0:G], ACT.Exp, bias=MX[:, i, 0:1], accum_out=MX[:, i, 1:2])\
                        .then_inc(*sig.route_exp.one())
                elif kind == "rank":
                    act.wait_ge(*sig.inner_max.at(1))
                    for t in range(2):
                        last = act.activation(IP[:, t, :], IL[:, t, :], ACT.Exp, bias=MX[:, t, 2:3], accum_out=MX[:, t, 3:4])
                    last.then_inc(*sig.inner_exp.one())
                elif kind == "gu":
                    act.wait_ge(*PJ.ready(J("gu", i)))
                    if i >= 2:
                        act.wait_ge(*PJ.evacuated(J("gu", i - 2)))
                    act.activation(HS[:, i % 2, :], PJ.tile(J("gu", i))[:, 0:FF], ACT.Silu).then_inc(*sig.silu_g.one())
                elif kind == "split":
                    e, part = i
                    EW.hi(act, e, part, PJ.ready(J("gu", e - 1)) if e else None)
                elif kind == "gather":
                    for b in range(2):
                        act.wait_ge(*PT.evacuated(J("gather", i, b)))
                        act.activation(XGH[:, i % 2, 4 * b:4 * b + 4, :], XF[:, b], ACT.Copy).then_inc(*sig.gathered_hi.one())
                elif kind == "turnh":
                    act.wait_ge(*PT.ready(J("turnh", i)))
                    if i >= 2:
                        act.wait_ge(EW.used, i - 1)
                    act.activation(HTH[:, i % 2, :, :], PT.tile(J("turnh", i))[:, 0:2 * P].rearrange("p (f s) -> p f s", f=2),
                                   ACT.Copy).then_inc(*sig.hidden_hi.one())

        def first_max(dve, link, p, eq, t, out, top, top_col, n):
            m = top[:, :, top_col:top_col + 1]
            link(dve.tensor_reduce(m, p, AX.X, ALU.max))
            link(dve.tensor_tensor(eq, p, m.to_broadcast([P, 2, n]), ALU.is_equal))
            idx = par[:, M_GI:M_GI + n].unsqueeze(1).to_broadcast([P, 2, n])
            link(dve.scalar_tensor_tensor(t, eq, -100.0, idx, ALU.mult, ALU.add))
            link(dve.tensor_reduce(top[:, :, 15:16], t, AX.X, ALU.min))
            return dve.tensor_tensor(out, t, top[:, :, 15:16].to_broadcast([P, 2, n]), ALU.is_equal)

        def vector_steps(dve, steps):
            link = linker(dve, sig.dve_own)
            for kind, i in steps:
                if kind == "norm":
                    dve.wait_ge(*sig.norm_root.at(i + 1))
                    link(dve.reciprocal(st[:, 4 + i:5 + i], st[:, 4 + i:5 + i]))
                    dve.tensor_scalar(XS[:, i, :], xlat[:, i, :], st[:, 4 + i:5 + i], None, ALU.mult)\
                        .then_inc(*sig.scaled.one())
                elif kind == "turnx":
                    dve.wait_ge(*PT.ready(J("turnx", i)))
                    g = par[:, M_NORM2 + 2 * i:M_NORM2 + 2 * i + 2].unsqueeze(2).to_broadcast([P, 2, T])
                    acc = PT.tile(J("turnx", i))[:, :].rearrange("p (k t) -> p k t", k=2)
                    dve.tensor_tensor(hT[:, 2 * i:2 * i + 2, :], acc, g, ALU.mult).then_inc(*PT.evac(J("turnx", i)))
                elif kind == "route":
                    dve.wait_ge(*PT.ready(J("route", i)))
                    dve.tensor_tensor(L[:, i, :], PT.tile(J("route", i))[:, 0:36], par[:, M_BR:M_BR + 36], ALU.add)\
                        .then_inc(*PT.evac(J("route", i)))
                    dve.wait_ge(*PT.evacuated(J("route", i)))
                    link(dve.reduce_max(MX[:, i, 0:1], L[:, i, 0:G], AX.X))
                    dve.tensor_scalar(MX[:, i, 0:1], MX[:, i, 0:1], -1.0, None, ALU.mult).then_inc(*sig.route_max.one())
                elif kind == "rank":
                    dve.wait_ge(*sig.route_exp.at(2))
                    link(dve.reciprocal(MX[:, :, 4:5], MX[:, :, 1:2]))
                    link(dve.tensor_tensor(GP[:], GP[:], MX[:, :, 4:5].to_broadcast([P, 2, G]), ALU.mult))
                    first_max(dve, link, GP[:], G1[:], G2[:], OH[:], MX, 5, G).then_inc(*sig.one_hot.one())
                    dve.wait_ge(*sig.one_hot.at(1))
                    for t in range(2):
                        last = dve.tensor_tensor(PROD[:, t], L[:, t, G:36].rearrange("p (g e) -> p g e", g=G),
                                                 OH[:, t, :].unsqueeze(2).to_broadcast([P, G, E]), ALU.mult)
                    link(last)
                    for t in range(2):
                        last = dve.tensor_reduce(IL[:, t, :], PROD[:, t].rearrange("p g e -> p e g"), AX.X, ALU.add)
                    link(last)
                    link(dve.tensor_reduce(MX[:, :, 6:7], IL[:], AX.X, ALU.max))
                    dve.tensor_scalar(MX[:, :, 2:3], MX[:, :, 6:7], -1.0, None, ALU.mult).then_inc(*sig.inner_max.one())
                    dve.wait_ge(*sig.inner_exp.at(1))
                    link(dve.reciprocal(MX[:, :, 7:8], MX[:, :, 3:4]))
                    link(dve.tensor_tensor(IP[:], IP[:], MX[:, :, 7:8].to_broadcast([P, 2, E]), ALU.mult))
                    link(first_max(dve, link, IP[:], I1[:], I2[:], O1[:], MX, 8, E))
                    link(dve.scalar_tensor_tensor(I1[:], O1[:], -2.0, IP[:], ALU.mult, ALU.add))
                    link(first_max(dve, link, I1[:], IP[:], I2[:], O2[:], MX, 9, E))
                    link(dve.tensor_tensor(MX[:, :, 10:11], MX[:, :, 8:9], MX[:, :, 9:10], ALU.add))
                    link(dve.reciprocal(MX[:, :, 11:12], MX[:, :, 10:11]))
                    link(dve.tensor_tensor(MX[:, :, 8:10], MX[:, :, 8:10], MX[:, :, 11:12].to_broadcast([P, 2, 2]), ALU.mult))
                    link(dve.tensor_tensor(O1[:], O1[:], MX[:, :, 8:9].to_broadcast([P, 2, E]), ALU.mult))
                    link(dve.tensor_tensor(O2[:], O2[:], MX[:, :, 9:10].to_broadcast([P, 2, E]), ALU.mult))
                    link(dve.tensor_tensor(O1[:], O1[:], O2[:], ALU.add))
                    link(dve.tensor_tensor(O1[:], O1[:], MX[:, :, 5:6].to_broadcast([P, 2, E]), ALU.mult))
                    for t in range(2):
                        last = dve.tensor_tensor(COMB[:, t, 0:G, :], O1[:, t, :].unsqueeze(1).to_broadcast([P, G, E]),
                                                 OH[:, t, :].unsqueeze(2).to_broadcast([P, G, E]), ALU.mult)
                    link(last)
                    dve.wait_ge(*PT.ready(J("rank")))
                    rank = PT.tile(J("rank"))[:, 0:8].rearrange("p (t g) -> p t g", t=2)
                    link(dve.scalar_tensor_tensor(RK[:, :, 0:G], rank, 1.0, OH[:], ALU.add, ALU.mult))
                    dve.tensor_scalar(OV[:], PT.tile(J("rank"))[:, 8:12], float(P), None, ALU.is_gt)\
                        .then_inc(*PT.evac(J("rank")))
                    dve.wait_ge(*PT.evacuated(J("rank")))
                    over = OV[:].unsqueeze(1).to_broadcast([P, 2, G])
                    link(dve.tensor_tensor(G2[:], RK[:, :, 0:G], over, ALU.mult))
                    link(dve.tensor_reduce(RK[:, :, G:G + 1], G2[:], AX.X, ALU.add))
                    link(dve.tensor_scalar(RK[:, :, 0:G], RK[:, :, 0:G], 1.0, None, ALU.subtract))
                    link(dve.tensor_scalar(RK[:, :, G:G + 1], RK[:, :, G:G + 1], float(P + 1), None, ALU.subtract))
                    for t in range(2):
                        link(dve.tensor_tensor(PROD[:, t], COMB[:, t, 0:G, :], OV[:].unsqueeze(2).to_broadcast([P, G, E]), ALU.mult))
                        last = dve.tensor_reduce(COMB[:, t, G, :], PROD[:, t].rearrange("p g e -> p e g"), AX.X, ALU.add)
                    link(last)
                    dve.tensor_reduce(FLAG[:, 0:1], OV[:], AX.X, ALU.max)
                    link(dve.tensor_tensor(MX[:, 0, 0:G], OV[:], par[:, M_GI:M_GI + G], ALU.mult))
                    link(dve.tensor_reduce(FLAG[:, 1:2], MX[:, 0, 0:G], AX.X, ALU.add))
                    dve.tensor_copy(FLAGI[:], FLAG[:, 0:2]).then_inc(*sig.over_flag.one())
                    for n in range(NP):
                        for t in range(2):
                            last = dve.tensor_scalar(SELT[:, n, t, :], par[:, M_IOTA:M_IOTA + P], RK[:, t, n:n + 1], None,
                                                     ALU.is_equal)
                    last.then_inc(*sig.selected.one())
                elif kind == "sel":
                    dve.wait_ge(*PT.ready(J("slotw")))
                    dve.tensor_copy(CS[:], PT.tile(J("slotw"))[:, 0:NP * E].rearrange("p (n e) -> p n e", e=E))\
                        .then_inc(*PT.evac(J("slotw")))
                    flat = SEL[:].rearrange("p n t c -> p (n t c)")
                    for b in range(3):
                        dve.wait_ge(*PT.ready(J("sel", b)))
                        n = min(512, NP * 2 * P - 512 * b)
                        dve.tensor_copy(flat[:, 512 * b:512 * b + n], PT.tile(J("sel", b))[:, 0:n])\
                            .then_inc(*PT.evac(J("sel", b)))
                elif kind == "gather":
                    for b in range(2):
                        dve.wait_ge(*PT.ready(J("gather", i, b)))
                        g = par[:, M_NORM2 + 4 * b:M_NORM2 + 4 * b + 4].unsqueeze(2).to_broadcast([P, 4, P])
                        acc = PT.tile(J("gather", i, b))[:, :].rearrange("p (k s) -> p k s", k=4)
                        dve.tensor_tensor(XF[:, b], acc, g, ALU.mult).then_inc(*PT.evac(J("gather", i, b)))
                    for b in range(2):
                        dve.wait_ge(*sig.gathered_hi.at(2 * i + b + 1))
                        dve.tensor_tensor(XGL[:, i % 2, 4 * b:4 * b + 4, :], XF[:, b],
                                          XGH[:, i % 2, 4 * b:4 * b + 4, :].bitcast(F32), ALU.subtract)\
                            .then_inc(*sig.gathered.one())
                elif kind == "split":
                    EW.lo(dve, *i)
                elif kind == "turnh":
                    dve.wait_ge(*sig.hidden_hi.at(i + 1))
                    dve.tensor_tensor(HTL[:, i % 2, :, :], PT.tile(J("turnh", i))[:, 0:2 * P].rearrange("p (f s) -> p f s", f=2),
                                      HTH[:, i % 2, :, :].bitcast(F32), ALU.subtract).then_inc(*PT.evac(J("turnh", i)))
                elif kind == "gu":
                    dve.wait_ge(*sig.silu_g.at(i + 1))
                    if i >= 2:
                        dve.wait_ge(*PT.ready(J("turnh", i - 2)))
                    dve.scalar_tensor_tensor(HG[:, i % 2, :], PJ.tile(J("gu", i))[:, FF:2 * FF],
                                             CS[:, i // E, i % E:i % E + 1], HS[:, i % 2, :], ALU.mult, ALU.mult)\
                        .then_inc(*PJ.evac(J("gu", i)))
                elif kind == "rows":
                    dve.wait_ge(EW.used, E * (i + 1))
                    if i:
                        dve.wait_ge(*PT.ready(J("scatter", i - 1, 1, 1)))
                    for h in range(2):
                        last = dve.tensor_copy(YB[:, h * 512:(h + 1) * 512], PS.tile(J("y", i, h))[:, :])
                        last.then_inc(*PS.evac(J("y", i, h)))
                    dve.wait_ge(*PS.evacuated(J("y", i, 0)))
                    dve.wait_ge(*PS.evacuated(J("y", i, 1)))
                    dve.engine_nop().then_inc(*sig.slots_w.one())
                elif kind == "scatter":
                    for t in range(2):
                        for h in range(2):
                            dve.wait_ge(*PT.ready(J("scatter", i, t, h)))
                            x = xlat[:, t, h * 512:(h + 1) * 512]
                            dve.tensor_tensor(x, x, PT.tile(J("scatter", i, t, h))[:, :], ALU.add)\
                                .then_inc(*PT.evac(J("scatter", i, t, h)))

        @block.tensor
        def _(pe):
            tensor_steps(pe, main_work)
            pe.wait_ge(*sig.over_flag.at(1))
            with pe.register("pe_over") as r:
                pe.reg_load(r, FLAGI[0:1, 0:1])
                with pe.If_ne(r, 0):
                    tensor_steps(pe, OVER_STEPS)

        @block.scalar
        def _(act):
            link = linker(act, sig.act_own)
            scalar_steps(act, main_work)
            act.wait_ge(*sig.over_flag.at(1))
            with act.register("act_over") as r:
                act.reg_load(r, FLAGI[0:1, 0:1])
                with act.If_ne(r, 0):
                    scalar_steps(act, OVER_STEPS)
            act.wait_ge(*sig.x_done.at(1))
            for t in range(2):
                link(act.activation(XS[:, t, :], xlat[:, t, :], ACT.Square, scale=D ** -0.5, accum_out=st[:, 2 + t:3 + t]))
                act.activation(st[:, 6 + t:7 + t], st[:, 2 + t:3 + t], ACT.Sqrt, bias=eps).then_inc(*sig.norm_root.one())

        @block.vector
        def _(dve):
            link = linker(dve, sig.dve_own)
            vector_steps(dve, main_work)
            with dve.register("dve_over") as r:
                dve.wait_ge(*sig.over_flag.at(1))
                dve.reg_load(r, FLAGI[0:1, 0:1])
                with dve.If_ne(r, 0):
                    vector_steps(dve, OVER_STEPS)
            dve.engine_nop().then_inc(*sig.x_done.one())
            dve.wait_ge(*sig.fin_in.at(16))
            for t in range(2):
                dve.wait_ge(*sig.norm_root.at(2 + t + 1))
                link(dve.reciprocal(st[:, 6 + t:7 + t], st[:, 6 + t:7 + t]))
                dve.scalar_tensor_tensor(xlat[:, t, :], xlat[:, t, :], st[:, 6 + t:7 + t], fin[:], ALU.mult, ALU.mult)\
                    .then_inc(*sig.norm_out.one())

        @block.sync
        def _(sp):
            sp.dma_start(fin[:], io["final_norm"].partition_broadcast(P)).then_inc(*sig.fin_in.dma())
            EW.issue(sp, 3 * G * E)
            sp.wait_ge(*sig.over_flag.at(1))
            with sp.register("sp_over") as r, sp.register("sp_group") as g:
                sp.reg_load(r, FLAGI[0:1, 0:1])
                sp.reg_load(g, FLAGI[0:1, 1:2])
                with sp.If_ne(r, 0):
                    group = sp.snap(g)
                    w = io["experts"].rearrange("(g e) p c -> g e p c", g=G)
                    EW.issue(sp, 3 * (G + 1) * E, lambda n: w[bass.ds(group, 1), n % E].rearrange("a p c -> (a p) c"))
            for t in range(2):
                sp.wait_ge(*sig.norm_out.at(t + 1))
                sp.dma_start(out[t * P:(t + 1) * P, :], xlat[:, t, :]).then_inc(*store.dma())
            sp.wait_ge(*store.now())



def build(nc, io, out):
    with ExitStack() as ctx:
        sig = Signals(ctx, nc)
        jobs = tuple(Banks(ctx, nc, n, k) for n, k in (("proj", 4), ("score", 2), ("turn", 2)))
        W = Weights(ctx, nc, io["stream"])
        xlat = ctx.enter_context(nc.sbuf_tensor("x_latent", [P, 2, D], F32))
        store = Signal(ctx, nc, "stored")
        with ExitStack() as trunk:
            def sb(name, shape):
                return trunk.enter_context(nc.sbuf_tensor(name, shape, F32))

            PC = Pieces(trunk, nc, W)
            consts = sb("consts", [P, C_W])
            silu_c = sb("silu_c", [P, KT, 2])
            modulation = sb("modulation", [P, DEPTH, 24, 2])
            HH, HL = (trunk.enter_context(nc.sbuf_tensor(n, [P, KT, TOK], F32R)) for n in ("h_hi", "h_lo"))
            xctx = sb("x_context", [P, 2, D])
            for l in range(DEPTH):
                trunk_layer(nc, l, io, W, PC, jobs, sig, consts, silu_c, modulation, xlat, xctx, HH, HL)
                sig.seal()
                PC.done.seal()
        EW = ExpertWeights(ctx, nc, io["experts"], W.ring)
        par = ctx.enter_context(nc.sbuf_tensor("mixer_params", [P, M_W], F32))
        mixer(nc, io, W, EW, jobs, sig, par, xlat)
        sig.seal()
        experts(nc, io, out, EW, jobs, sig, par, xlat, store)



def trunk_constants():
    c = np.zeros((P, C_W), np.float32)
    r = np.arange(P)
    c[:, C_ID:C_ID + P] = np.eye(P)
    c[:, C_ONES:C_ONES + P] = 1 / 128
    c[:, C_BONES:C_BONES + P] = (r[:, None] // 64 == r[None, :] // 64) / 64
    rot = np.zeros((P, P), np.float32)
    for m in range(P):
        if m % 32 < 16:
            rot[m + 16, m] = -1
        else:
            rot[m - 16, m] = 1
    c[:, C_ROT:C_ROT + P] = rot
    tok = np.arange(256)
    freqs = (np.float32(10000.0) ** (-np.arange(0, 32, 2, dtype=np.float32) / np.float32(32))).astype(np.float32)
    pos = np.where((r[:, None] % 64) < 32, (tok // 64)[None, :], (tok % 64)[None, :]).astype(np.float32)
    ang = (pos * freqs[r % 16][:, None]).astype(np.float32)
    c[:, C_COS:C_COS + 256] = np.cos(ang.astype(np.float64))
    c[:, C_SIN:C_SIN + 256] = np.sin(ang.astype(np.float64))
    for i, h in enumerate(LEVELS):
        same = r[:, None] // (2 * h) == r[None, :] // (2 * h)
        c[:, C_MASK + i * P:C_MASK + (i + 1) * P] = same & (r[:, None] // h != r[None, :] // h)
    c[:, C_EPS] = EPS
    c[:, C_ONE] = 1
    return c


def tiles(w):
    k, n = w.shape
    return w.reshape(k // P, P, n).transpose(1, 0, 2).reshape(P, -1)


def mixer_params(i):
    c = np.zeros((P, M_W), np.float32)
    r = np.arange(P)
    c[:, M_ID:M_ID + P] = np.eye(P)
    c[:, M_TRI:M_TRI + P] = r[:, None] < r[None, :]
    c[:, M_ONES:M_ONES + P] = 1
    c[:, M_IOTA:M_IOTA + P] = r
    c[:, M_CAUSAL:M_CAUSAL + P] = np.where(r[None, :] <= r[:, None], 0, -1e30)
    for h in range(8):
        c[h, M_SEL + h * P:M_SEL + (h + 1) * P] = 1
    c[:, M_EPS], c[:, M_ONE] = EPS, 1
    c[:, M_GI:M_GI + 8] = np.arange(8)
    c[:, M_NORM1:M_NORM1 + 8] = i["mix_norm_2"][0].reshape(8, P).T
    c[:, M_NORM2:M_NORM2 + 8] = i["ffn_norm_2"][0].reshape(8, P).T
    c[:, M_CONVW:M_CONVW + 16] = i["conv_w_2"][0].reshape(4, 4, P).transpose(2, 1, 0).reshape(P, 16)
    c[:, M_CONVB:M_CONVB + 4] = i["conv_b_2"][0].reshape(4, P).T
    c[:, M_BA:M_BA + 4] = i["b_a_2"][0].reshape(4, P).T
    c[:, M_BX:M_BX + 4] = i["b_x_2"][0].reshape(4, P).T
    c[:, M_LAM:M_LAM + 4] = i["lru_lambda_2"][0].reshape(4, P).T
    c[0:8, M_BF] = i["b_forget_2"][0]
    c[:, M_BR:M_BR + 4] = i["b_group_2"][0]
    c[:, M_BR + 4:M_BR + 36] = i["b_inner_2"][0].reshape(-1)
    c[:, M_WF:M_WF + 64] = tiles(i["w_in_2"][0][:, 1536:1544])
    c[:, M_WR:M_WR + 288] = tiles(np.concatenate([i["w_group_2"][0], i["w_inner_2"][0].transpose(1, 0, 2).reshape(D, 32)], 1))
    for n in range(8):
        a, b = (n % 2) * 64, (n // 2) * P
        c[a:a + 64, M_WA + b + a:M_WA + b + a + 64] = i["w_a_2"][0, n]
        c[a:a + 64, M_WX + b + a:M_WX + b + a + 64] = i["w_x_2"][0, n]
    return c


def layouts(i):
    stream = np.zeros((len(STREAM), P, SLOT), np.float32)

    def put(name, w, kind="rows"):
        w = tiles(w)
        if kind != "rows":
            w = w.reshape(P, {"cols": 8, "branch": 4}[kind], 4, -1).transpose(0, 2, 1, 3)
        stream[SLOT_OF[name]] = w.reshape(P, SLOT)

    sizes = [512, 128, 128, 512, 256, 256, 512, 16, 16, 512, 512, 512, 512, 1024, 1024, 1024]
    at = [0, *np.cumsum(sizes)]
    heads = np.concatenate([np.r_[j * 64:j * 64 + 64, (j + 4) * 64:(j + 4) * 64 + 64] for j in range(4)])
    params, rows = np.zeros((DEPTH, P, A_W), np.float32), np.zeros((DEPTH, P, R_W), np.float32)
    for l in range(DEPTH):
        w = i["w_in"][l]
        aq, ak, av, ag, gq, gk, gv, gaf, gab, gg, su, sv, s_g, ma, mg, ms = (w[:, a:b] for a, b in zip(at, at[1:]))
        for n in range(6):
            put(f"{l}.ada{n}", i["w_ada"][l][:, n * 512:(n + 1) * 512])
        for n, x in (("sg", s_g), ("su", su), ("ag", ag[:, heads]), ("gg", gg), ("aq", aq[:, heads]), ("gv", gv), ("sv", sv)):
            put(f"{l}.{n}", x, "rows" if n in ("gv", "sv") else "cols")
        put(f"{l}.ak_gq_gate", np.concatenate([ak, gq, gaf, gab, np.zeros((D, 96), np.float32)], 1), "cols")
        put(f"{l}.gk_av", np.concatenate([gk, av, np.zeros((D, 128), np.float32)], 1), "cols")
        for b, m, wb in (("s", ms, i["w_br_sgu"][l]), ("a", ma, i["w_br_attn"][l][heads]), ("g", mg, i["w_br_gla"][l])):
            put(f"{l}.m{b}0", m[:, 0:512], "cols")
            put(f"{l}.m{b}1", m[:, 512:], "cols")
            put(f"{l}.wbr{b}", wb, "branch")
        for n in range(2):
            put(f"{l}.wo{n}", i["w_out"][l][:, n * 512:(n + 1) * 512])
        p = params[l]
        p[:, A_BADA:A_W] = i["b_ada"].reshape(24 * DEPTH, P).T
        p[:, A_QN] = np.concatenate([i["attn_q_norm"][l]] * 2)
        p[:, A_KN] = np.concatenate([i["attn_k_norm"][l]] * 2)
        p[:, A_ABF:A_ABF + 2] = i["gla_ab_f"][l].reshape(2, P).T
        p[:, A_ABB:A_ABB + 2] = i["gla_ab_b"][l].reshape(2, P).T
        p[:, A_ON] = i["gla_o_norm"][l]
        p[0:16, A_A2:A_A2 + 256] = i["gla_a2_f"][l]
        p[16:32, A_A2 + 256:A_A2 + 512] = i["gla_a2_b"][l]
        p[:, A_WS:A_WS + 512] = i["sgu_w"][l].transpose(2, 0, 1).reshape(P, 512)
        rows[l, :, R_G:R_G + 512] = i["sgu_ln_g"][l]
        rows[l, :, R_B:R_B + 512] = i["sgu_ln_b"][l]
        rows[l, :, R_SB:R_SB + 512] = i["sgu_b"][l].reshape(-1)
    w = i["w_in_2"][0]
    for n, a in (("q", 0), ("k", 512), ("v", 1024), ("gat", 1544), ("rec", 2056)):
        put(f"x.{n}", w[:, a:a + 512])
    for n in range(2):
        put(f"x.wo{n}", i["w_out_2"][0][:, n * 512:(n + 1) * 512])
    ex = np.empty((G * E, P, ESLOT), np.float32)
    gu = ex[:, :, 0:KT * 2 * FF].reshape(G * E, P, KT, 2, FF)
    for n, x in enumerate(("w_gate_2", "w_up_2")):
        gu[:, :, :, n, :] = i[x][0].reshape(G * E, KT, P, FF).transpose(0, 2, 1, 3)
    ex[:, :, 0:KT * 2 * FF] = gu.reshape(G * E, P, -1)
    ex[:, :, KT * 2 * FF:] = i["w_down_2"][0].reshape(G * E, 2, P, D).transpose(0, 2, 1, 3).reshape(G * E, P, 2 * D)
    xT = np.concatenate([i["ctx"][0], i["x"][0]], 0).T.reshape(KT, P, TOK).transpose(1, 0, 2)
    cond = np.stack([i["c_ctx"], i["c"][0]], -1).reshape(KT, P, 2).transpose(1, 0, 2)
    return {
        "stream": stream, "consts": trunk_constants(), "params": params, "rows": rows,
        "cond": cond, "xT": xT,
        "x_rows": i["x"][0].reshape(2, P, D).transpose(1, 0, 2),
        "ctx_rows": i["ctx"][0].reshape(2, P, D).transpose(1, 0, 2),
        "mixer_params": mixer_params(i), "experts": ex, "final_norm": i["final_norm_2"],
        "post": np.stack([i["post_ln_g"], i["post_ln_b"]], 1),
    }


def kernel(**inputs):
    import concourse.bacc as bacc
    from concourse.bass_utils import run_bass_kernel_spmd

    nc = bacc.Bacc("TRN2", target_bir_lowering=False, num_devices=1)
    arrays, io = {}, {}
    for name, a in layouts({k: np.asarray(v) for k, v in inputs.items()}).items():
        arrays["in_" + name] = np.ascontiguousarray(a)
        io[name] = nc.dram_tensor("in_" + name, a.shape, mybir.dt.from_np(a.dtype), kind="ExternalInput").ap()
    out = nc.dram_tensor("out", (256, D), F32, kind="ExternalOutput").ap()
    build(nc, io, out)
    r = run_bass_kernel_spmd(nc, [arrays], core_ids=[0])
    return r.results[0]["out"].reshape(1, 256, D)
```
